# Optimizing a Trainium2 kernel written in Bass

```python
import jax, jax.numpy as jnp
from jax import lax
import numpy as np

D_MODEL = 1024
BATCH = 1
SEQ = 1024
DEPTH = 2
DEC_BATCH = 1
DEC_SEQ = 64
PAST_LEN = 1024

CHUNK = 64
N_A = DEPTH // 2
N_B = DEPTH - N_A
N_DENSE = (DEPTH + 1) // 2
N_MOE = DEPTH // 2
HK = 8
HV = 16
DK = 128
DV = 128
QK_DIM = HK * DK
V_DIM = HV * DV
CONV_CH = 2 * QK_DIM + V_DIM
CONV_W = 4
A_PROJ = CONV_CH + V_DIM + 2 * HV
HQ = 16
HKV = 4
HD = 64
GQ = HQ // HKV
WINDOW = 128
ROT_DIM = HD // 4
ROPE_THETA = 500000.0
D_FF = 2816
N_EXPERTS = 8
TOP_K = 2
EPS = 1e-6

kernel_name = 'streaming_yoco_gdn_swa_moe_step'

def _rmsnorm(x, g):
    xf = x.astype(jnp.float32)
    y = xf * lax.rsqrt(jnp.mean(xf * xf, axis=-1, keepdims=True) + EPS) * g.astype(jnp.float32)
    return y.astype(x.dtype)

def _l2norm(x):
    return x * lax.rsqrt(jnp.sum(x * x, axis=-1, keepdims=True) + EPS)

def _rope_partial(x, pos):
    half = ROT_DIM // 2
    inv = jnp.power(ROPE_THETA, -jnp.arange(half, dtype=jnp.float32) * 2.0 / ROT_DIM)
    ang = pos.astype(jnp.float32)[:, None] * inv[None, :]
    cos = jnp.cos(ang)[None, :, None, :]
    sin = jnp.sin(ang)[None, :, None, :]
    x1 = x[..., :half].astype(jnp.float32)
    x2 = x[..., half:ROT_DIM].astype(jnp.float32)
    rot = jnp.concatenate([x1 * cos - x2 * sin, x2 * cos + x1 * sin], axis=-1).astype(x.dtype)
    return jnp.concatenate([rot, x[..., ROT_DIM:]], axis=-1)

def _gated_delta(q, k, v, g, beta, s0, chunk):
    B, T, H, _ = q.shape
    n = T // chunk

    def blk(t):
        t = t.reshape((B, n, chunk, H) + t.shape[3:])
        return jnp.moveaxis(t, (1, 3), (0, 2))

    qb, kb, vb, gb, bb = blk(q), blk(k), blk(v), blk(g), blk(beta)
    gb = jnp.cumsum(gb, axis=-1)
    idx = jnp.arange(chunk)
    incl = idx[:, None] >= idx[None, :]
    strict = idx[:, None] > idx[None, :]
    eye = jnp.eye(chunk, dtype=jnp.float32)

    def step(S, inp):
        qc, kc, vc, gc, bc = inp
        decay = jnp.exp(jnp.where(incl, gc[..., :, None] - gc[..., None, :], -jnp.inf))
        kbeta = kc * bc[..., None]
        a = jnp.where(strict, jnp.einsum('bhid,bhjd->bhij', kbeta, kc) * decay, 0.0) + eye
        rhs = jnp.concatenate([vc * bc[..., None], kbeta * jnp.exp(gc)[..., None]], axis=-1)
        sol = lax.linalg.triangular_solve(a, rhs, left_side=True, lower=True, unit_diagonal=True)
        u, w = sol[..., :DV], sol[..., DV:]
        v_new = u - jnp.einsum('bhck,bhkv->bhcv', w, S)
        attn = jnp.einsum('bhid,bhjd->bhij', qc, kc) * decay
        o = (jnp.einsum('bhck,bhkv->bhcv', qc * jnp.exp(gc)[..., None], S)
             + jnp.einsum('bhij,bhjv->bhiv', attn, v_new))
        g_last = gc[..., -1]
        S = (S * jnp.exp(g_last)[..., None, None]
             + jnp.einsum('bhck,bhcv->bhkv', kc * jnp.exp(g_last[..., None] - gc)[..., None], v_new))
        return S, o

    S, o = lax.scan(step, s0, (qb, kb, vb, gb, bb))
    o = jnp.transpose(o, (1, 0, 3, 2, 4)).reshape(B, T, H, DV)
    return o, S

def _gdn_layer(x, norm_g, w_in, w_conv, a_log, dt_bias, o_norm, w_out, conv_state, s0):
    B, T, _ = x.shape
    h = _rmsnorm(x, norm_g)
    proj = h @ w_in
    qkv, z, b, a = jnp.split(proj, [CONV_CH, CONV_CH + V_DIM, CONV_CH + V_DIM + HV], axis=-1)
    xpad = jnp.concatenate([conv_state.astype(qkv.dtype), qkv], axis=1)
    conv = xpad[:, 0:T] * w_conv[0]
    for j in range(1, CONV_W):
        conv = conv + xpad[:, j:j + T] * w_conv[j]
    conv = jax.nn.silu(conv)
    new_conv = xpad[:, T:]
    q, k, v = jnp.split(conv.astype(jnp.float32), [QK_DIM, 2 * QK_DIM], axis=-1)
    q = _l2norm(q.reshape(B, T, HK, DK)) * (DK ** -0.5)
    k = _l2norm(k.reshape(B, T, HK, DK))
    q = jnp.repeat(q, HV // HK, axis=2)
    k = jnp.repeat(k, HV // HK, axis=2)
    v = v.reshape(B, T, HV, DV)
    beta = jax.nn.sigmoid(b.astype(jnp.float32))
    g = -jnp.exp(a_log.astype(jnp.float32)) * jax.nn.softplus(a.astype(jnp.float32) + dt_bias.astype(jnp.float32))
    o, S = _gated_delta(q, k, v, g, beta, s0.astype(jnp.float32), min(CHUNK, T))
    zf = z.reshape(B, T, HV, DV).astype(jnp.float32)
    o = (_rmsnorm(o, o_norm) * jax.nn.silu(zf)).astype(x.dtype)
    return x + o.reshape(B, T, V_DIM) @ w_out, new_conv, S

def _sink_attend(q, k, v, sinks, valid):
    s = jnp.einsum('bqhgd,bkhd->bhgqk', q, k).astype(jnp.float32) * (HD ** -0.5)
    s = jnp.where(valid, s, -jnp.inf)
    sink = sinks.astype(jnp.float32)[None, :, :, None, None]
    m = jnp.maximum(jnp.max(s, axis=-1, keepdims=True), sink)
    p = jnp.exp(s - m)
    p = p / (jnp.sum(p, axis=-1, keepdims=True) + jnp.exp(sink - m))
    return jnp.einsum('bhgqk,bkhd->bqhgd', p.astype(v.dtype), v)

def _swa_prompt(q, k, v, sinks):
    B, T = q.shape[:2]
    n = T // CHUNK
    span = WINDOW + CHUNK
    kp = jnp.pad(k, ((0, 0), (WINDOW, 0), (0, 0), (0, 0)))
    vp = jnp.pad(v, ((0, 0), (WINDOW, 0), (0, 0), (0, 0)))
    qb = q.reshape(B, n, CHUNK, HKV, GQ, HD)
    offs = jnp.arange(span)

    def one(c):
        qc = lax.dynamic_index_in_dim(qb, c, axis=1, keepdims=False)
        kc = lax.dynamic_slice_in_dim(kp, c * CHUNK, span, axis=1)
        vc = lax.dynamic_slice_in_dim(vp, c * CHUNK, span, axis=1)
        valid = c * CHUNK + offs >= WINDOW
        return _sink_attend(qc, kc, vc, sinks, valid)

    o = lax.map(one, jnp.arange(n))
    return jnp.moveaxis(o, 0, 1).reshape(B, T, HQ * HD)

def _dense_ffn(x, g, w1, w3, w2):
    h = _rmsnorm(x, g)
    return x + (jax.nn.silu(h @ w1) * (h @ w3)) @ w2

def _moe_ffn(x, g, router, w1, w3, w2):
    B, T, D = x.shape
    h = _rmsnorm(x, g).reshape(-1, D)
    n = h.shape[0]
    logits = (h @ router).astype(jnp.float32)
    top_v, top_i = lax.top_k(logits, TOP_K)
    gates = jax.nn.softmax(top_v, axis=-1)
    e_flat = top_i.reshape(-1)
    order = jnp.argsort(e_flat)
    tok = order // TOP_K
    xs = h[tok]
    sizes = jnp.bincount(e_flat, length=N_EXPERTS).astype(jnp.int32)
    a = lax.ragged_dot(xs, w1, sizes)
    b = lax.ragged_dot(xs, w3, sizes)
    y = lax.ragged_dot(jax.nn.silu(a) * b, w2, sizes)
    y = y * gates.reshape(-1)[order][:, None].astype(y.dtype)
    out = jax.ops.segment_sum(y, tok, num_segments=n)
    return x + out.reshape(B, T, D).astype(x.dtype)

def _trunk(x, pos, conv0, s0, win_k, win_v, p):
    B, T, _ = x.shape
    new_conv, new_s = [], []
    k = v = None
    for layer in range(DEPTH):
        if layer < N_A:
            x, c_st, S = _gdn_layer(x, p['norm_attn'][layer], p['gdn_w_in'][layer], p['gdn_w_conv'][layer],
                                    p['gdn_a_log'][layer], p['gdn_dt_bias'][layer], p['gdn_o_norm'][layer],
                                    p['gdn_w_out'][layer], conv0[layer], s0[layer])
            new_conv.append(c_st)
            new_s.append(S)
        else:
            ib = layer - N_A
            if k is None:
                hk = _rmsnorm(x, p['kv_norm'])
                kv = hk @ p['w_kv']
                k = _rope_partial(kv[..., :HKV * HD].reshape(B, T, HKV, HD), pos)
                v = kv[..., HKV * HD:].reshape(B, T, HKV, HD)
            h = _rmsnorm(x, p['norm_attn'][layer])
            q = _rope_partial((h @ p['swa_w_q'][ib]).reshape(B, T, HQ, HD), pos)
            sinks = p['swa_sinks'][ib].reshape(HKV, GQ)
            if win_k is None:
                o = _swa_prompt(q, k, v, sinks)
            else:
                kc = jnp.concatenate([win_k.astype(k.dtype), k], axis=1)
                vc = jnp.concatenate([win_v.astype(v.dtype), v], axis=1)
                valid = jnp.ones((kc.shape[1],), dtype=bool)
                o = _sink_attend(q.reshape(B, T, HKV, GQ, HD), kc, vc, sinks, valid).reshape(B, T, HQ * HD)
            x = x + o @ p['swa_w_o'][ib]
        if layer % 2 == 0:
            i = layer // 2
            x = _dense_ffn(x, p['norm_ffn'][layer], p['ffn_w1'][i], p['ffn_w3'][i], p['ffn_w2'][i])
        else:
            i = layer // 2
            x = _moe_ffn(x, p['norm_ffn'][layer], p['moe_router'][i], p['moe_w1'][i], p['moe_w3'][i], p['moe_w2'][i])
    y = _rmsnorm(x, p['final_norm'])
    return y, jnp.stack(new_conv), jnp.stack(new_s), k, v

def setup_inputs(seed: int = 0) -> dict:
    key = jax.random.key(seed)
    ks = jax.random.split(key, 32)
    f32 = jnp.float32
    nrm = lambda k, s, sc: jax.random.normal(k, s, f32) * sc
    win_c = min(WINDOW, PAST_LEN)
    dt = jnp.exp(jax.random.uniform(ks[10], (N_A, HV), f32, np.log(1e-3), np.log(1e-1)))
    return {
        'x_prompt': nrm(ks[0], (BATCH, SEQ, D_MODEL), 1.0),
        'x_sample': nrm(ks[1], (DEC_BATCH, DEC_SEQ, D_MODEL), 1.0),
        'cache_conv': nrm(ks[2], (N_A, DEC_BATCH, CONV_W - 1, CONV_CH), 1.0),
        'state_delta': nrm(ks[3], (N_A, DEC_BATCH, HV, DK, DV), DK ** -0.5),
        'cache_k': nrm(ks[4], (DEC_BATCH, win_c, HKV, HD), 1.0),
        'cache_v': nrm(ks[5], (DEC_BATCH, win_c, HKV, HD), 1.0),
        'norm_attn': 1.0 + nrm(ks[6], (DEPTH, D_MODEL), 0.05),
        'norm_ffn': 1.0 + nrm(ks[7], (DEPTH, D_MODEL), 0.05),
        'gdn_w_in': nrm(ks[8], (N_A, D_MODEL, A_PROJ), D_MODEL ** -0.5),
        'gdn_w_conv': nrm(ks[9], (N_A, CONV_W, CONV_CH), CONV_W ** -0.5),
        'gdn_a_log': jnp.log(jax.random.uniform(ks[11], (N_A, HV), f32, 1.0, 16.0)),
        'gdn_dt_bias': dt + jnp.log(-jnp.expm1(-dt)),
        'gdn_o_norm': 1.0 + nrm(ks[12], (N_A, DV), 0.05),
        'gdn_w_out': nrm(ks[13], (N_A, V_DIM, D_MODEL), V_DIM ** -0.5),
        'kv_norm': 1.0 + nrm(ks[14], (D_MODEL,), 0.05),
        'w_kv': nrm(ks[15], (D_MODEL, 2 * HKV * HD), D_MODEL ** -0.5),
        'swa_w_q': nrm(ks[16], (N_B, D_MODEL, HQ * HD), D_MODEL ** -0.5),
        'swa_sinks': nrm(ks[17], (N_B, HQ), 1.0),
        'swa_w_o': nrm(ks[18], (N_B, HQ * HD, D_MODEL), (HQ * HD) ** -0.5),
        'ffn_w1': nrm(ks[19], (N_DENSE, D_MODEL, D_FF), D_MODEL ** -0.5),
        'ffn_w3': nrm(ks[20], (N_DENSE, D_MODEL, D_FF), D_MODEL ** -0.5),
        'ffn_w2': nrm(ks[21], (N_DENSE, D_FF, D_MODEL), D_FF ** -0.5),
        'moe_router': nrm(ks[22], (N_MOE, D_MODEL, N_EXPERTS), D_MODEL ** -0.5),
        'moe_w1': nrm(ks[23], (N_MOE, N_EXPERTS, D_MODEL, D_FF), D_MODEL ** -0.5),
        'moe_w3': nrm(ks[24], (N_MOE, N_EXPERTS, D_MODEL, D_FF), D_MODEL ** -0.5),
        'moe_w2': nrm(ks[25], (N_MOE, N_EXPERTS, D_FF, D_MODEL), D_FF ** -0.5),
        'final_norm': 1.0 + nrm(ks[26], (D_MODEL,), 0.05),
    }

def reference(x_prompt, x_sample, cache_conv, state_delta, cache_k, cache_v,
              norm_attn, norm_ffn, gdn_w_in, gdn_w_conv, gdn_a_log, gdn_dt_bias, gdn_o_norm, gdn_w_out,
              kv_norm, w_kv, swa_w_q, swa_sinks, swa_w_o,
              ffn_w1, ffn_w3, ffn_w2, moe_router, moe_w1, moe_w3, moe_w2, final_norm):
    p = dict(norm_attn=norm_attn, norm_ffn=norm_ffn, gdn_w_in=gdn_w_in, gdn_w_conv=gdn_w_conv,
             gdn_a_log=gdn_a_log, gdn_dt_bias=gdn_dt_bias, gdn_o_norm=gdn_o_norm, gdn_w_out=gdn_w_out,
             kv_norm=kv_norm, w_kv=w_kv, swa_w_q=swa_w_q, swa_sinks=swa_sinks, swa_w_o=swa_w_o,
             ffn_w1=ffn_w1, ffn_w3=ffn_w3, ffn_w2=ffn_w2, moe_router=moe_router,
             moe_w1=moe_w1, moe_w3=moe_w3, moe_w2=moe_w2, final_norm=final_norm)
    Bp, Tp, _ = x_prompt.shape
    pos_p = jnp.arange(Tp, dtype=jnp.int32)
    conv0 = jnp.zeros((N_A, Bp, CONV_W - 1, CONV_CH), x_prompt.dtype)
    s0 = jnp.zeros((N_A, Bp, HV, DK, DV), jnp.float32)
    y_prompt, conv_p, delta_p, k_full, v_full = _trunk(x_prompt, pos_p, conv0, s0, None, None, p)
    win_p = min(WINDOW, Tp)
    k_p = k_full[:, Tp - win_p:]
    v_p = v_full[:, Tp - win_p:]
    pos_s = PAST_LEN + jnp.arange(x_sample.shape[1], dtype=jnp.int32)
    y_sample, conv_s, delta_s, k_s, v_s = _trunk(x_sample, pos_s, cache_conv, state_delta, cache_k, cache_v, p)
    return (y_prompt, y_sample, conv_p, delta_p, k_p, v_p, conv_s, delta_s, k_s, v_s)


_drawn_inputs = setup_inputs


def setup_inputs(seed=0):
    import zlib

    import numpy as np

    out = dict(_drawn_inputs(seed))
    spreads = {}
    factors = {'swa_sinks': 8.0}
    for name, (base, spread) in spreads.items():
        noise = np.random.default_rng([zlib.crc32(name.encode()), seed]).standard_normal(out[name].shape)
        drawn = base * np.exp(spread * noise) if base else spread * noise
        out[name] = __import__('jax').numpy.asarray(drawn.astype(out[name].dtype))
    for name, factor in factors.items():
        out[name] = (out[name] * factor).astype(out[name].dtype)
    return out
```

```python
from contextlib import ExitStack

import numpy as np

import concourse.bass as bass
from concourse import mybir

F32 = mybir.dt.float32
I32 = mybir.dt.int32
U32 = mybir.dt.uint32
ACT = mybir.ActivationFunctionType
ALU = mybir.AluOpType
AX = mybir.AxisListType

P = 128
D = 1024
KD = D // P
PROMPT = 1024
SAMPLE = 64
TOK = PROMPT + SAMPLE
CHUNK = 64
TILES = [(s, min(P, TOK - s)) for s in range(0, TOK, P)]
NT = len(TILES)
BLK = [(0, 384), (384, 384), (768, 320)]
EPS = 1e-6

HK, HV, DK, DV = 8, 16, 128, 128
QK_DIM = HK * DK
V_DIM = HV * DV
CONV_CH = 2 * QK_DIM + V_DIM
CONV_W = 4
HIST = CONV_W - 1
PADW = HIST + PROMPT + HIST + SAMPLE
GROUPS = 4
GH = HV // GROUPS
GK = HK // GROUPS

HQ, HKV, HD = 16, 4, 64
WINDOW = 128
D_FF = 2816
KF = D_FF // P
NE = 8

G_ATTN0, G_ATTN1, G_FFN0, G_FFN1, G_KV, G_FINAL, G_ONORM = 0, 8, 16, 24, 32, 40, 48
N_GAINS = 49
LEVELS = (1, 2, 4, 8, 16, 32)
C_ID, C_ONES, C_INCL, C_LAST, C_ROT, C_STRICT = 0, 1, 2, 3, 4, 5
C_LVL = 6
N_CONST = C_LVL + len(LEVELS)
CONST_W = N_CONST * P + 16
K_GC, K_BETA, K_NGB, K_KDEC = 0, 1, 2, 3
N_COL = 4


def constants():
    j, i = np.indices((P, P))
    same = j // CHUNK == i // CHUNK
    c = np.zeros((N_CONST, P, P), np.float32)
    c[C_ID] = j == i
    c[C_ONES] = 1
    c[C_INCL] = same & (j <= i)
    c[C_LAST] = same & (j % CHUNK == CHUNK - 1)
    r, f = j % HD, i % HD
    half = HD // 8
    c[C_ROT] = (j // HD == i // HD) * ((f < half) * (r == f + half) * -1.0 + ((f >= half) & (f < 2 * half)) * (r == f - half))
    c[C_STRICT] = j < i
    for n, s in enumerate(LEVELS):
        c[C_LVL + n] = (j // (2 * s) == i // (2 * s)) & (j % (2 * s) < s) & (i % (2 * s) >= s)
    tail = np.zeros((P, 16), np.float32)
    tail[:, 0:NE] = NE - np.arange(NE)
    tail[:, NE] = np.arange(P)
    return np.concatenate([c.transpose(1, 0, 2).reshape(P, N_CONST * P), tail], axis=1)


def rope_tables():
    half = HD // 8
    inv = np.power(np.float32(500000.0), -np.arange(half, dtype=np.float32) * np.float32(2.0) / np.float32(2 * half))
    pos = np.concatenate([np.arange(PROMPT), 1024 + np.arange(SAMPLE)]).astype(np.float32)
    ang = (pos[:, None] * inv.astype(np.float32)[None, :]).astype(np.float32)
    t = np.zeros((2, P, TOK), np.float32)
    t[0] = 1
    for h in range(2):
        for f in range(2 * half):
            t[0, h * HD + f] = np.cos(ang[:, f % half])
            t[1, h * HD + f] = np.sin(ang[:, f % half])
    return t


PRE = 1


class Stage:

    def __init__(self, nc, name):
        self.nc, self.name, self.sems, self.pre = nc, name, [], []

    def __enter__(self):
        self.stack = ExitStack()
        return self

    def sb(self, name, shape, dt=F32):
        return self.stack.enter_context(self.nc.sbuf_tensor(f"{self.name}_{name}", shape, dt))

    def ps(self, name, shape, dt=F32):
        return self.stack.enter_context(self.nc.psum_tensor(f"{self.name}_{name}", shape, dt))

    def sem(self, name, pre=True):
        s = self.stack.enter_context(self.nc.semaphore(f"{self.name}_{name}"))
        self.sems.append(s)
        if pre:
            self.pre.append(s)
        return s

    def block(self):
        for s in self.pre:
            self.nc.gpsimd.sem_inc(s, PRE)
        self.nc.all_engine_barrier()
        return self.nc.Block()

    def __exit__(self, *exc):
        if exc[0] is None:
            for s in self.sems:
                self.nc.gpsimd.sem_clear(s)
        self.stack.close()


class Chain:

    def __init__(self, eng, sem, base=0):
        self.eng, self.sem, self.base, self.n = eng, sem, base, 0

    def __call__(self, ins):
        self.n += 1
        ins.then_inc(self.sem, 1)
        self.eng.wait_ge(self.sem, PRE + self.base + self.n)


def hold(eng, passed):
    eng.sem_inc(passed, 1)


def load_stage(nc, m, io):
    with Stage(nc, "load") as st:
        rows = st.sb("rows", [N_GAINS, P])
        crow = st.sb("crow", [P, P])
        hrow = st.sb("hrow", [HIST * 32, P])
        xin = st.sb("xin", [P, 2, D])
        pt = st.ps("pt", [P, 2, 2, 512])
        pg = st.ps("pg", [P, 512])
        small, xl = st.sem("small_loaded"), [st.sem(f"frames_loaded{i}") for i in range(2)]
        turned, copied, gturn, mset = st.sem("tile_turned"), st.sem("tile_copied"), st.sem("gains_turned"), st.sem("eps_set")
        tiles_x = [io["x_prompt"][0, s:s + n, :] if s < PROMPT else io["x_sample"][0, :, :] for s, n in TILES]
        with st.block() as block:
            @block.sync
            def _(sp):
                sp.dma_start(m["const"][:, :], io["consts"]).then_inc(small, 16)
                for gain, at in (("norm_attn", G_ATTN0), ("norm_ffn", G_FFN0)):
                    sp.dma_start(rows[at:at + 16, :], io[gain].rearrange("l (k p) -> (l k) p", p=P)).then_inc(small, 16)
                for gain, at in (("kv_norm", G_KV), ("final_norm", G_FINAL)):
                    sp.dma_start(rows[at:at + 8, :], io[gain].rearrange("(k p) -> k p", p=P)).then_inc(small, 16)
                sp.dma_start(rows[G_ONORM:G_ONORM + 1, :], io["gdn_o_norm"]).then_inc(small, 16)
                sp.dma_start(crow[:, :], io["gdn_w_conv"][0].rearrange("j (t p) -> (j t) p", p=P)).then_inc(small, 16)
                sp.dma_start(hrow[:, :], io["cache_conv"][0, 0].rearrange("j (t p) -> (j t) p", p=P)).then_inc(small, 16)
                for name in ("gdn_a_log", "gdn_dt_bias", "swa_sinks"):
                    sp.dma_start(m[name][:, :], io[name].broadcast_to([P, 16])).then_inc(small, 16)
                for t, (s, n) in enumerate(TILES):
                    if t >= 2:
                        sp.wait_ge(turned, PRE + 2 * (t - 1))
                    sp.dma_start(xin[0:n, t % 2, :], tiles_x[t]).then_inc(xl[t % 2], 16)

            @block.tensor
            def _(pe):
                pe.wait_ge(small, PRE + 16 * 11)
                ident = m["const"][:, 0:P]
                pe.transpose(pg[:, 0:N_GAINS], rows[:, :], ident[0:N_GAINS, 0:N_GAINS])
                pe.transpose(pg[:, 64:64 + P], crow[:, :], ident)
                pe.transpose(pg[:, 192:192 + HIST * 32], hrow[:, :], ident[0:96, 0:96]).then_inc(gturn, 1)
                for t, (s, n) in enumerate(TILES):
                    pe.wait_ge(xl[t % 2], PRE + 16 * (t // 2 + 1))
                    for h in range(2):
                        if t >= 1:
                            pe.wait_ge(copied, PRE + 2 * (t - 1) + h + 1)
                        for k in range(4):
                            last = pe.transpose(pt[:, h, 0, k * P:k * P + n], xin[0:n, t % 2, (4 * h + k) * P:(4 * h + k + 1) * P], ident[0:n, 0:n])
                        last.then_inc(turned, 1)

            @block.vector
            def _(dve):
                dve.memset(m["eps"][:, :], EPS).then_inc(mset, 1)
                dve.wait_ge(gturn, PRE + 1)
                dve.tensor_copy(m["gains"][:, :], pg[:, 0:N_GAINS])
                dve.tensor_copy(m["convw"][:, :, :], pg[:, 64:64 + P].rearrange("p (j t) -> p j t", j=4))
                dve.tensor_copy(m["hist"][:, :, :], pg[:, 192:192 + 96].rearrange("p (j t) -> p j t", j=3))
                for t, (s, n) in enumerate(TILES):
                    for h in range(2):
                        dve.wait_ge(turned, PRE + 2 * t + h + 1)
                        dve.tensor_copy(m["xT"][:, 4 * h:4 * h + 4, s:s + n], pt[:, h, 0, :].rearrange("p (k c) -> p k c", c=P)[:, :, 0:n]).then_inc(copied, 1)


def norm_stage(nc, m, name, outs):
    with Stage(nc, name) as st:
        sq = st.sb("sq", [P, 2, TOK])
        root = st.sb("root", [P, TOK])
        rinv = st.sb("rinv", [P, TOK])
        acc = st.ps("acc", [P, 3, 512])
        squared, summed, rooted, inverted = (st.sem(s) for s in ("squared", "summed", "rooted", "inverted"))
        with st.block() as block:
            @block.scalar
            def _(act):
                for k in range(KD):
                    if k >= 2:
                        act.wait_ge(summed, PRE + k - 1)
                    act.activation(sq[:, k % 2, :], m["xT"][:, k, :], ACT.Square).then_inc(squared, 1)
                act.wait_ge(summed, PRE + KD)
                for b, (s, n) in enumerate(BLK):
                    act.activation(root[:, s:s + n], acc[:, b, 0:n], ACT.Sqrt, bias=m["eps"][:, :], scale=1.0 / D).then_inc(rooted, 1)

            @block.tensor
            def _(pe):
                for k in range(KD):
                    pe.wait_ge(squared, PRE + k + 1)
                    for b, (s, n) in enumerate(BLK):
                        last = pe.matmul(acc[:, b, 0:n], m["const"][:, C_ONES * P:(C_ONES + 1) * P], sq[:, k % 2, s:s + n],
                                         start=(k == 0), stop=(k == KD - 1))
                    last.then_inc(summed, 1)

            @block.vector
            def _(dve):
                for b, (s, n) in enumerate(BLK):
                    dve.wait_ge(rooted, PRE + b + 1)
                    dve.reciprocal(rinv[:, s:s + n], root[:, s:s + n]).then_inc(inverted, 1)
                dve.wait_ge(inverted, PRE + len(BLK))
                for out, gain in outs:
                    for k in range(KD):
                        dve.scalar_tensor_tensor(out=out[:, k, :], in0=m["xT"][:, k, :], scalar=m["gains"][:, gain + k:gain + k + 1],
                                                 in1=rinv[:, :], op0=ALU.mult, op1=ALU.mult)


def gates_stage(nc, m, hT, io):
    NB = NT * HV
    with Stage(nc, "gates") as st:
        wba = st.sb("wba", [P, KD, 2 * HV])
        ba = st.sb("ba", [P, NT, 2, HV])
        beta, xa, t0, t1, g, gc = (st.sb(n, [P, NT, HV]) for n in ("beta", "xa", "t0", "t1", "g", "gc"))
        ea = st.sb("ea", [P, HV])
        rows = st.sb("rows", [HV, 2, TOK])
        pba = st.ps("pba", [P, NT, 2, HV])
        pgc, pgl = st.ps("pgc", [P, NT, HV]), st.ps("pgl", [P, NT, HV])
        prow = st.ps("prow", [HV, 3, 512])
        w_loaded, proj, dv, av = (st.sem(s) for s in ("w_loaded", "projected", "vector", "scalar"))
        cum, turned, emptied, stored, own = (st.sem(s) for s in ("cumulated", "turned", "emptied", "stored", "vector_own"))
        cst = lambda n: m["const"][:, n * P:(n + 1) * P]
        with st.block() as block:
            @block.sync
            def _(sp):
                sp.dma_start(wba[:, :, :], io["gdn_w_in"][0][:, CONV_CH + V_DIM:].rearrange("(k p) c -> p k c", p=P)).then_inc(w_loaded, 16)
                sp.wait_ge(emptied, PRE + 6)
                sp.dma_start(m["rows_dram"].rearrange("a h t -> h a t"), rows[:, :, :]).then_inc(stored, 16)
                sp.wait_ge(stored, PRE + 16)

            @block.tensor
            def _(pe):
                pe.wait_ge(w_loaded, PRE + 16)
                for t, (s, n) in enumerate(TILES):
                    for k in range(KD):
                        last = pe.matmul(pba[0:n, t, :, :], hT[:, k, s:s + n], wba[:, k, :], start=(k == 0), stop=(k == KD - 1))
                last.then_inc(proj, 1)
                pe.wait_ge(dv, PRE + 6)
                pe.matmul(pgc[:, :, :], cst(C_INCL), g[:, :, :], start=True, stop=True).then_inc(cum, 1)
                pe.wait_ge(dv, PRE + 7)
                pe.matmul(pgl[:, :, :], cst(C_LAST), gc[:, :, :], start=True, stop=True).then_inc(cum, 1)
                for a, src in enumerate((gc, beta)):
                    for b in range(3):
                        if a:
                            pe.wait_ge(emptied, PRE + b + 1)
                        for t in range(3 * b, 3 * b + 3):
                            s, n = TILES[t]
                            last = pe.transpose(prow[:, b, (t % 3) * P:(t % 3) * P + n], src[0:n, t, :], cst(C_ID)[0:n, 0:n])
                        last.then_inc(turned, 1)

            @block.scalar
            def _(act):
                acts = Chain(act, av)
                act.activation(ea[:, :], m["gdn_a_log"][:, :], ACT.Exp)
                act.wait_ge(dv, PRE + 1)
                acts(act.activation(beta[:, :, :], ba[:, :, 0, :], ACT.Exp, scale=-1.0))
                act.wait_ge(dv, PRE + 3)
                acts(act.activation(t0[:, :, :], t0[:, :, :], ACT.Exp, scale=-1.0))
                acts(act.activation(t0[:, :, :], t0[:, :, :], ACT.Ln, bias=1.0))
                act.wait_ge(dv, PRE + 8)
                acts(act.activation(m["cols"][:, :, :, K_KDEC], t1[:, :, :], ACT.Exp))
                acts(act.activation(t0[:, :, :], gc[:, :, :], ACT.Exp))

            @block.vector
            def _(dve):
                v = Chain(dve, dv)
                w = Chain(dve, own)
                w(dve.memset(ba[:, :, :, :], 0.0))
                dve.wait_ge(proj, PRE + 1)
                dve.tensor_copy(ba[:, 0:NT - 1, :, :], pba[:, 0:NT - 1, :, :])
                v(dve.tensor_copy(ba[0:64, NT - 1, :, :], pba[0:64, NT - 1, :, :]))
                v(dve.tensor_tensor(xa[:, :, :], ba[:, :, 1, :], m["gdn_dt_bias"][:, :].unsqueeze(1).broadcast_to([P, NT, HV]), ALU.add))
                w(dve.tensor_scalar(t1[:, :, :], xa[:, :, :], -1.0, None, ALU.mult))
                v(dve.tensor_tensor(t0[:, :, :], xa[:, :, :], t1[:, :, :], ALU.max))
                dve.wait_ge(av, PRE + 1)
                w(dve.tensor_scalar(beta[:, :, :], beta[:, :, :], 1.0, None, ALU.add))
                v(dve.reciprocal(beta[:, :, :], beta[:, :, :]))
                dve.wait_ge(av, PRE + 3)
                v(dve.scalar_tensor_tensor(out=t1[:, :, :], in0=xa[:, :, :], scalar=0.0, in1=t0[:, :, :], op0=ALU.max, op1=ALU.add))
                v(dve.scalar_tensor_tensor(out=g[:, :, :], in0=t1[:, :, :], scalar=-1.0, in1=ea[:, :].unsqueeze(1).broadcast_to([P, NT, HV]), op0=ALU.mult, op1=ALU.mult))
                dve.wait_ge(cum, PRE + 1)
                v(dve.tensor_copy(gc[:, :, :], pgc[:, :, :]))
                dve.wait_ge(cum, PRE + 2)
                v(dve.tensor_tensor(t1[:, :, :], pgl[:, :, :], gc[:, :, :], ALU.subtract))
                dve.tensor_copy(m["cols"][:, :, :, K_GC], gc[:, :, :])
                dve.tensor_copy(m["cols"][:, :, :, K_BETA], beta[:, :, :])
                dve.wait_ge(av, PRE + 5)
                dve.scalar_tensor_tensor(out=m["cols"][:, :, :, K_NGB], in0=t0[:, :, :], scalar=-1.0, in1=beta[:, :, :], op0=ALU.mult, op1=ALU.mult)
                for a in range(2):
                    for b in range(3):
                        dve.wait_ge(turned, PRE + 3 * a + b + 1)
                        s, n = BLK[b]
                        dve.tensor_copy(rows[:, a, s:s + n], prow[:, b, 0:n]).then_inc(emptied, 1)


def project_stage(nc, m, hT, io, g):
    qk, vT, zT = m["qk"], m["vT"], m["zT"]
    NC = 2 * GK + GH
    NM = NC + GH
    STEP = 2 * P
    with Stage(nc, "proj") as st:
        w = st.sb("w", [P, 3, KD, STEP])
        xpad = st.sb("xpad", [P, 2, PADW])
        acc = st.sb("acc", [P, 2, PADW])
        cw = st.sb("cw", [P, CONV_W, NC])
        root = acc
        pm = st.ps("pm", [P, 2, 3, 512])
        wl = [st.sem(f"w_loaded{i}") for i in range(3)]
        done, emptied, conved, silued, tails, hists, cws, own = (st.sem(s) for s in (
            "tile_summed", "tile_emptied", "convolved", "silued", "tails_kept", "hist_set", "conv_w_set", "vector_step"))
        squared, united = st.sem("squared"), st.sem("united")
        starts = [g * 256, QK_DIM + g * 256, 2 * QK_DIM + g * 512, 2 * QK_DIM + g * 512 + 256,
                  CONV_CH + g * 512, CONV_CH + g * 512 + 256]
        conv_tile = [2 * g, 2 * g + 1, 8 + 2 * g, 8 + 2 * g + 1] + [16 + 4 * g + i for i in range(4)]
        dest = [qk[:, i, :] for i in range(4)] + [vT[:, i, :] for i in range(4)]
        with st.block() as block:
            @block.sync
            def _(sp):
                for s, c in enumerate(starts):
                    if s >= 3:
                        sp.wait_ge(done, PRE + 2 * (s - 2))
                    sp.dma_start(w[:, s % 3, :, :], io["gdn_w_in"][0][:, bass.ds(c, STEP)].rearrange("(k p) c -> p k c", p=P)).then_inc(wl[s % 3], 16)

            @block.tensor
            def _(pe):
                for t in range(NM):
                    s = t // 2
                    if t % 2 == 0:
                        pe.wait_ge(wl[s % 3], PRE + 16 * (s // 3 + 1))
                    if t >= 2:
                        pe.wait_ge(emptied, PRE + t - 1)
                    for k in range(KD):
                        for b, (c, n) in enumerate(BLK):
                            last = pe.matmul(pm[:, t % 2, b, 0:n], w[:, s % 3, k, (t % 2) * P:(t % 2 + 1) * P], hT[:, k, c:c + n],
                                             start=(k == 0), stop=(k == KD - 1))
                    last.then_inc(done, 1)
                for i in range(4):
                    pe.wait_ge(squared, PRE + i + 1)
                    pe.wait_ge(emptied, PRE + NM + i - 1)
                    for b, (c, n) in enumerate(BLK):
                        last = pe.matmul(pm[:, i % 2, b, 0:n], m["const"][:, C_ONES * P:(C_ONES + 1) * P], xpad[:, i % 2, c:c + n], start=True, stop=True)
                    last.then_inc(done, 1)

            @block.gpsimd
            def _(pool):
                pool.memset(xpad[:, :, 0:HIST], 0.0).then_inc(hists, 1)
                for i in range(NC):
                    if i >= 2:
                        pool.wait_ge(conved, PRE + i - 1)
                    pool.tensor_copy(xpad[:, i % 2, HIST + PROMPT:HIST + PROMPT + HIST], m["hist"][:, :, bass.ds(conv_tile[i], 1)].rearrange("p j o -> p (j o)")).then_inc(hists, 1)
                    pool.wait_ge(emptied, PRE + i + 1)
                    pool.tensor_copy(m["tail"][:, 0, :, bass.ds(conv_tile[i], 1)].rearrange("p j o -> p (j o)"), xpad[:, i % 2, PROMPT:PROMPT + HIST])
                    pool.tensor_copy(m["tail"][:, 1, :, bass.ds(conv_tile[i], 1)].rearrange("p j o -> p (j o)"), xpad[:, i % 2, PADW - HIST:PADW]).then_inc(tails, 1)

            @block.scalar
            def _(act):
                def empty(t):
                    act.wait_ge(done, PRE + t + 1)
                    if t < NC:
                        if t >= 2:
                            act.wait_ge(conved, PRE + t - 1)
                            act.wait_ge(tails, PRE + t - 1)
                        act.activation(xpad[:, t % 2, HIST:HIST + 768].rearrange("p (b c) -> p b c", b=2), pm[:, t % 2, 0:2, 0:384], ACT.Copy)
                        act.activation(xpad[:, t % 2, HIST + 768:HIST + PROMPT], pm[:, t % 2, 2, 0:256], ACT.Copy)
                        act.activation(xpad[:, t % 2, PADW - SAMPLE:PADW], pm[:, t % 2, 2, 256:320], ACT.Copy).then_inc(emptied, 1)
                    else:
                        act.activation(zT[:, t - NC, 0:768].rearrange("p (b c) -> p b c", b=2), pm[:, t % 2, 0:2, 0:384], ACT.Silu)
                        act.activation(zT[:, t - NC, 768:TOK], pm[:, t % 2, 2, 0:320], ACT.Silu).then_inc(emptied, 1)

                def silu(i):
                    act.wait_ge(conved, PRE + i + 1)
                    act.activation(dest[i][:, 0:PROMPT], acc[:, i % 2, 0:PROMPT], ACT.Silu)
                    act.activation(dest[i][:, PROMPT:TOK], acc[:, i % 2, PROMPT + HIST:PADW - HIST], ACT.Silu).then_inc(silued, 1)

                for t in range(NM):
                    empty(t)
                    if 1 <= t <= NC:
                        silu(t - 1)
                for i in range(4):
                    act.wait_ge(done, PRE + NM + i + 1)
                    if i >= 2:
                        act.wait_ge(united, PRE + i - 1)
                    for b, (c, n) in enumerate(BLK):
                        last = act.activation(root[:, i % 2, c:c + n], pm[:, i % 2, b, 0:n], ACT.Sqrt, bias=m["eps"][:, :])
                    last.then_inc(emptied, 1)

            @block.vector
            def _(dve):
                def unit(i):
                    dve.wait_ge(emptied, PRE + NM + i + 1)
                    v(dve.reciprocal(root[:, i % 2, 0:TOK], root[:, i % 2, 0:TOK]))
                    dve.scalar_tensor_tensor(out=qk[:, i, :], in0=qk[:, i, :], scalar=DK ** -0.5 if i < GK else 1.0, in1=root[:, i % 2, 0:TOK],
                                             op0=ALU.mult, op1=ALU.mult).then_inc(united, 1)

                v = Chain(dve, own)
                dve.tensor_copy(cw[:, :, 0:2], m["convw"][:, :, bass.ds(2 * g, 2)])
                dve.tensor_copy(cw[:, :, 2:4], m["convw"][:, :, bass.ds(2 * g + 8, 2)])
                v(dve.tensor_copy(cw[:, :, 4:8], m["convw"][:, :, bass.ds(4 * g + 16, 4)]))
                PW = PADW - HIST
                for i in range(NC):
                    dve.wait_ge(emptied, PRE + i + 1)
                    dve.wait_ge(hists, PRE + i + 2)
                    if i >= 2:
                        dve.wait_ge(silued, PRE + i - 1)
                    v(dve.tensor_scalar(acc[:, i % 2, 0:PW], xpad[:, i % 2, 0:PW], cw[:, 0, i:i + 1], None, ALU.mult))
                    for j in range(1, CONV_W):
                        op = dve.scalar_tensor_tensor(out=acc[:, i % 2, 0:PW], in0=xpad[:, i % 2, j:j + PW], scalar=cw[:, j, i:i + 1],
                                                      in1=acc[:, i % 2, 0:PW], op0=ALU.mult, op1=ALU.add)
                        if j < CONV_W - 1:
                            v(op)
                    op.then_inc(conved, 1)
                for i in range(4):
                    if i == 0:
                        dve.wait_ge(conved, PRE + NC)
                        dve.wait_ge(silued, PRE + NC)
                        dve.wait_ge(tails, PRE + NC)
                    if i >= 2:
                        dve.wait_ge(done, PRE + NM + i - 1)
                    dve.tensor_tensor(xpad[:, i % 2, 0:TOK], qk[:, i, :], qk[:, i, :], ALU.mult).then_inc(squared, 1)
                    if i >= 1:
                        unit(i - 1)
                unit(3)
def delta_stage(nc, m, io, g):
    qk, vT = m["qk"], m["vT"]
    with Stage(nc, "delta") as st:
        gcB, betaB = st.sb("gcB", [P, GH, TOK]), st.sb("betaB", [P, GH, TOK])
        kst, qst, vst = st.sb("kst", [P, GK, P]), st.sb("qst", [P, GK, P]), st.sb("vst", [P, GH, P])
        cst, egl = st.sb("cst", [P, GH, N_COL]), st.sb("egl", [P, GH, 2])
        dec, attn, at, eg, qg, kd, vb, T, TT, Xs, rhs, vn = (st.sb(n, [P, GH, P]) for n in (
            "dec", "attn", "at", "eg", "qg", "kd", "vb", "T", "TT", "Xs", "rhs", "vn"))
        BT = st.sb("BT", [P, 2, GH, P])
        S = st.sb("S", [P, 2, GH, DV])
        b_turn = st.ps("turn", [P, 2, GH, P])
        b_score, b_x, b_d, b_dt, b_ks, b_vn = (st.ps(n, [P, GH, P]) for n in ("score", "x", "d", "dt", "ks", "vnew"))
        names = ("rows_loaded", "s_zeroed", "kq_staged", "v_staged", "cols_staged", "turned", "scored", "diffs", "dexp", "eg_ready",
                 "masked", "at_half", "at_ready", "qg_ready", "kd_vb_ready", "lvl_masked", "x_summed", "x_copied", "deltas", "t_new",
                 "ks_summed", "rhs_ready", "vn_summed", "vn_copied", "o_summed", "s_summed", "o_copied", "s_new",
                 "state_stored", "state_loaded", "last_stored")
        e = {n: st.sem(n) for n in names}
        passed = st.sem("passed")
        cst_sq = lambda n, r: m["const"][0:r, n * P:n * P + r]
        over_heads = lambda a, r: a.unsqueeze(1).broadcast_to([r, GH, r])
        L = len(LEVELS)
        last_t = NT - 1
        with st.block() as block:
            @block.sync
            def _(sp):
                for a, dst in ((0, gcB), (1, betaB)):
                    sp.dma_start(dst[:, :, :], m["rows_dram"][a, bass.ds(GH * g, GH), :].unsqueeze(0).broadcast_to([P, GH, TOK])).then_inc(e["rows_loaded"], 16)
                sp.wait_ge(e["s_new"], PRE + 2 * last_t)
                sp.dma_start(io["delta_p"][0, 0, bass.ds(GH * g, GH)].rearrange("h k v -> k h v"), S[:, 0, :, :]).then_inc(e["state_stored"], 16)
                sp.wait_ge(e["state_stored"], PRE + 16)
                sp.dma_start(S[:, 0, :, :], io["state_delta"][0, 0, bass.ds(GH * g, GH)].rearrange("h k v -> k h v")).then_inc(e["state_loaded"], 16)
                sp.wait_ge(e["s_new"], PRE + 2 * last_t + 1)
                sp.dma_start(io["delta_s"][0, 0, bass.ds(GH * g, GH)].rearrange("h k v -> k h v"), S[:, 1, :, :]).then_inc(e["last_stored"], 16)
                sp.wait_ge(e["last_stored"], PRE + 16)

            @block.gpsimd
            def _(pool):
                def tile(t, n):
                    pool.wait_ge(e["s_summed"], PRE + 2 * t)
                    pool.tensor_copy(vst[:, :, 0:n], vT[:, :, bass.ds(t * P, n)]).then_inc(e["v_staged"], 1)
                    pool.tensor_copy(cst[:, :, :], m["cols"][:, bass.ds(t, 1), bass.ds(GH * g, GH), :].rearrange("p o h c -> p (o h) c")).then_inc(e["cols_staged"], 1)
                    pool.wait_ge(e["at_ready"], PRE + t + 1)
                    for l in range(L):
                        if l >= 2:
                            pool.wait_ge(e["t_new"], PRE + t * L + l - 1)
                        pool.tensor_tensor(BT[0:n, l % 2, :, 0:n], at[0:n, :, 0:n], over_heads(cst_sq(C_LVL + l, n), n), ALU.mult).then_inc(e["lvl_masked"], 1)

                pool.memset(S[:, 0, :, :], 0.0).then_inc(e["s_zeroed"], 1)
                with pool.Fori(0, last_t) as t:
                    tile(t, P)
                tile(last_t, SAMPLE)

            @block.tensor
            def _(pe):
                def k_state(t, c, r):
                    pe.wait_ge(e["s_new"], PRE + 2 * t + c)
                    pe.wait_ge(e["rhs_ready"], PRE + 2 * t + c)
                    for h in range(GH):
                        last = pe.matmul(b_ks[r:r + CHUNK, h, :], kst[:, h // 2, r:r + CHUNK], S[:, c, h, :], start=True, stop=True)
                    last.then_inc(e["ks_summed"], 1)

                def tile(t, n, sample=False):
                    ident = m["const"][:, 0:P]
                    pe.wait_ge(e["kq_staged"], PRE + t + 1)
                    pe.wait_ge(e["v_staged"], PRE + t + 1)
                    pe.wait_ge(e["o_copied"], PRE + 2 * t)
                    pe.wait_ge(e["s_new"], PRE + 2 * t)
                    for k in range(GK):
                        pe.transpose(b_turn[0:n, 0, k, :], kst[:, k, 0:n], ident)
                    for h in range(GH):
                        last = pe.transpose(b_turn[0:n, 1, h, :], vst[:, h, 0:n], ident)
                    last.then_inc(e["turned"], 1)
                    pe.wait_ge(e["at_ready"], PRE + t)
                    for k in range(GK):
                        pe.matmul(b_score[0:n, k, 0:n], kst[:, k, 0:n], kst[:, k, 0:n], start=True, stop=True)
                    for k in range(GK):
                        last = pe.matmul(b_score[0:n, GK + k, 0:n], kst[:, k, 0:n], qst[:, k, 0:n], start=True, stop=True)
                    last.then_inc(e["scored"], 1)
                    if sample:
                        pe.wait_ge(e["state_loaded"], PRE + 16)
                    k_state(t, 0, 0)
                    for l in range(L):
                        pe.wait_ge(e["lvl_masked"], PRE + t * L + l + 1)
                        pe.wait_ge(e["t_new"], PRE + t * L + l)
                        for h in range(GH):
                            last = pe.matmul(b_x[0:n, h, 0:n], BT[0:n, l % 2, h, 0:n], T[0:n, h, 0:n] if l else ident[0:n, 0:n], start=True, stop=True)
                        last.then_inc(e["x_summed"], 1)
                        if l:
                            pe.wait_ge(e["x_copied"], PRE + t * (L - 1) + l)
                            for h in range(GH):
                                if l < L - 1:
                                    pe.matmul(b_d[0:n, h, 0:n], TT[0:n, h, 0:n], Xs[0:n, h, 0:n], start=True, stop=True)
                                last = pe.matmul(b_dt[0:n, h, 0:n], Xs[0:n, h, 0:n], TT[0:n, h, 0:n], start=True, stop=True)
                            last.then_inc(e["deltas"], 1)
                    for c in range(n // CHUNK):
                        r = c * CHUNK
                        if c:
                            k_state(t, c, r)
                        pe.wait_ge(e["rhs_ready"], PRE + 2 * t + c + 1)
                        pe.wait_ge(e["t_new"], PRE + (t + 1) * L)
                        pe.wait_ge(e["vn_copied"], PRE + 2 * t + c)
                        hold(pe, passed)
                        for h in range(GH):
                            last = pe.matmul(b_vn[r:r + CHUNK, h, :], TT[r:r + CHUNK, h, r:r + CHUNK], rhs[r:r + CHUNK, h, :], start=True, stop=True)
                        last.then_inc(e["vn_summed"], 1)
                        pe.wait_ge(e["kd_vb_ready"], PRE + t + 1)
                        pe.wait_ge(e["qg_ready"], PRE + t + 1)
                        pe.wait_ge(e["o_copied"], PRE + 2 * t + c)
                        pe.wait_ge(e["vn_copied"], PRE + 2 * t + c + 1)
                        for h in range(GH):
                            pe.matmul(b_turn[:, 0, h, 0:CHUNK], S[:, c, h, :], qg[:, h, r:r + CHUNK], start=True, stop=False)
                            last = pe.matmul(b_turn[:, 0, h, 0:CHUNK], vn[r:r + CHUNK, h, :], attn[r:r + CHUNK, h, r:r + CHUNK], start=False, stop=True)
                        last.then_inc(e["o_summed"], 1)
                        for h in range(GH):
                            last = pe.matmul(b_turn[:, 1, h, :], kd[r:r + CHUNK, h, :], vn[r:r + CHUNK, h, :], start=True, stop=True)
                        last.then_inc(e["s_summed"], 1)

                pe.wait_ge(e["s_zeroed"], PRE + 1)
                with pe.Fori(0, last_t) as t:
                    tile(t, P)
                tile(last_t, SAMPLE, sample=True)

            @block.scalar
            def _(act):
                def tile(t, n):
                    act.wait_ge(e["s_summed"], PRE + 2 * t)
                    act.activation(kst[:, :, 0:n], qk[:, GK:2 * GK, bass.ds(t * P, n)], ACT.Copy)
                    act.activation(qst[:, :, 0:n], qk[:, 0:GK, bass.ds(t * P, n)], ACT.Copy).then_inc(e["kq_staged"], 1)
                    act.wait_ge(e["s_new"], PRE + 2 * t)
                    for c in range(n // CHUNK):
                        act.activation(egl[:, :, c:c + 1], gcB[:, :, bass.ds(t * P + (c + 1) * CHUNK - 1, 1)], ACT.Exp)
                    act.activation(eg[:, :, 0:n], gcB[:, :, bass.ds(t * P, n)], ACT.Exp).then_inc(e["eg_ready"], 1)
                    act.wait_ge(e["diffs"], PRE + t + 1)
                    act.activation(dec[0:n, :, 0:n], dec[0:n, :, 0:n], ACT.Exp).then_inc(e["dexp"], 1)
                    act.wait_ge(e["turned"], PRE + t + 1)
                    act.wait_ge(e["cols_staged"], PRE + t + 1)
                    for h in range(GH):
                        act.activation(kd[0:n, h, :], b_turn[0:n, 0, h // 2, :], ACT.Copy, scale=cst[0:n, h, K_KDEC:K_KDEC + 1])
                    for h in range(GH):
                        last = act.activation(vb[0:n, h, :], b_turn[0:n, 1, h, :], ACT.Copy, scale=cst[0:n, h, K_BETA:K_BETA + 1])
                    last.then_inc(e["kd_vb_ready"], 1)
                    for l in range(1, L):
                        act.wait_ge(e["x_summed"], PRE + t * L + l + 1)
                        act.activation(Xs[0:n, :, 0:n], b_x[0:n, :, 0:n], ACT.Copy).then_inc(e["x_copied"], 1)
                    for c in range(n // CHUNK):
                        r = c * CHUNK
                        act.wait_ge(e["vn_summed"], PRE + 2 * t + c + 1)
                        act.activation(vn[r:r + CHUNK, :, :], b_vn[r:r + CHUNK, :, :], ACT.Copy).then_inc(e["vn_copied"], 1)
                        act.wait_ge(e["o_summed"], PRE + 2 * t + c + 1)
                        act.activation(vT[:, :, bass.ds(t * P + r, CHUNK)], b_turn[:, 0, :, 0:CHUNK], ACT.Copy).then_inc(e["o_copied"], 1)

                act.wait_ge(e["rows_loaded"], PRE + 32)
                with act.Fori(0, last_t) as t:
                    tile(t, P)
                tile(last_t, SAMPLE)

            @block.vector
            def _(dve):
                def right_side(t, c):
                    r = c * CHUNK
                    dve.wait_ge(e["ks_summed"], PRE + 2 * t + c + 1)
                    for h in range(GH):
                        last = dve.scalar_tensor_tensor(out=rhs[r:r + CHUNK, h, :], in0=b_ks[r:r + CHUNK, h, :], scalar=cst[r:r + CHUNK, h, K_NGB:K_NGB + 1],
                                                        in1=vb[r:r + CHUNK, h, :], op0=ALU.mult, op1=ALU.add)
                    last.then_inc(e["rhs_ready"], 1)

                def tile(t, n):
                    ident = over_heads(cst_sq(C_ID, n), n)
                    dve.wait_ge(e["cols_staged"], PRE + t + 1)
                    for h in range(GH):
                        last = dve.tensor_scalar(dec[0:n, h, 0:n], gcB[0:n, h, bass.ds(t * P, n)], cst[0:n, h, K_GC:K_GC + 1], 0.0, ALU.subtract, ALU.min)
                    last.then_inc(e["diffs"], 1)
                    dve.wait_ge(e["dexp"], PRE + t + 1)
                    dve.tensor_tensor(dec[0:n, :, 0:n], dec[0:n, :, 0:n], over_heads(cst_sq(C_INCL, n), n), ALU.mult).then_inc(e["masked"], 1)
                    dve.wait_ge(e["masked"], PRE + t + 1)
                    dve.wait_ge(e["scored"], PRE + t + 1)
                    for h in range(GH):
                        last = dve.tensor_tensor(at[0:n, h, 0:n], b_score[0:n, h // 2, 0:n], dec[0:n, h, 0:n], ALU.mult)
                    last.then_inc(e["at_half"], 1)
                    for h in range(GH):
                        dve.tensor_tensor(attn[0:n, h, 0:n], b_score[0:n, GK + h // 2, 0:n], dec[0:n, h, 0:n], ALU.mult)
                    dve.wait_ge(e["at_half"], PRE + t + 1)
                    dve.tensor_tensor(at[0:n, :, 0:n], at[0:n, :, 0:n], betaB[0:n, :, bass.ds(t * P, n)], ALU.mult).then_inc(e["at_ready"], 1)
                    dve.wait_ge(e["eg_ready"], PRE + t + 1)
                    for h in range(GH):
                        last = dve.tensor_tensor(qg[:, h, 0:n], qst[:, h // 2, 0:n], eg[:, h, 0:n], ALU.mult)
                    last.then_inc(e["qg_ready"], 1)
                    dve.wait_ge(e["kd_vb_ready"], PRE + t + 1)
                    right_side(t, 0)
                    dve.wait_ge(e["lvl_masked"], PRE + t * L + 1)
                    dve.tensor_tensor(TT[0:n, :, 0:n], ident, BT[0:n, 0, :, 0:n], ALU.subtract)
                    dve.wait_ge(e["x_summed"], PRE + t * L + 1)
                    dve.tensor_tensor(T[0:n, :, 0:n], ident, b_x[0:n, :, 0:n], ALU.subtract).then_inc(e["t_new"], 1)
                    dve.wait_ge(e["t_new"], PRE + t * L + 1)
                    for l in range(1, L):
                        dve.wait_ge(e["deltas"], PRE + t * (L - 1) + l)
                        if l < L - 1:
                            dve.tensor_tensor(T[0:n, :, 0:n], T[0:n, :, 0:n], b_d[0:n, :, 0:n], ALU.subtract)
                        dve.tensor_tensor(TT[0:n, :, 0:n], TT[0:n, :, 0:n], b_dt[0:n, :, 0:n], ALU.subtract).then_inc(e["t_new"], 1)
                        if l < L - 1:
                            dve.wait_ge(e["t_new"], PRE + t * L + l + 1)
                    for c in range(n // CHUNK):
                        if c:
                            right_side(t, c)
                        dve.wait_ge(e["s_summed"], PRE + 2 * t + c + 1)
                        for h in range(GH):
                            last = dve.scalar_tensor_tensor(out=S[:, 1 - c, h, :], in0=S[:, c, h, :], scalar=egl[:, h, c:c + 1], in1=b_turn[:, 1, h, :],
                                                            op0=ALU.mult, op1=ALU.add)
                        last.then_inc(e["s_new"], 1)

                dve.wait_ge(e["rows_loaded"], PRE + 32)
                with dve.Fori(0, last_t) as t:
                    tile(t, P)
                tile(last_t, SAMPLE)


def mix_out_stage(nc, m, io, g):
    oT, zT, xT = m["vT"], m["zT"], m["xT"]
    with Stage(nc, "mixout") as st:
        w = st.sb("w", [P, GH, D])
        sq, root = st.sb("sq", [P, 2, TOK]), st.sb("root", [P, 2, TOK])
        pm = st.ps("pm", [P, 2, 3, 512])
        wl, squared, summed, rooted, inverted, normed, gated, added = (st.sem(s) for s in (
            "w_loaded", "squared", "summed", "rooted", "inverted", "normed", "gated", "added"))
        with st.block() as block:
            @block.sync
            def _(sp):
                sp.dma_start(w[:, :, :], io["gdn_w_out"][0][bass.ds(g * GH * DV, GH * DV), :].rearrange("(k p) c -> p k c", p=P)).then_inc(wl, 16)

            @block.gpsimd
            def _(pool):
                for h in range(GH):
                    if h >= 2:
                        pool.wait_ge(summed, PRE + h - 1)
                    pool.tensor_tensor(sq[:, h % 2, :], oT[:, h, :], oT[:, h, :], ALU.mult).then_inc(squared, 1)

            @block.tensor
            def _(pe):
                for h in range(GH):
                    pe.wait_ge(squared, PRE + h + 1)
                    if h >= 2:
                        pe.wait_ge(rooted, PRE + h - 1)
                    for b, (c, n) in enumerate(BLK):
                        last = pe.matmul(pm[:, h % 2, b, 0:n], m["const"][:, C_ONES * P:(C_ONES + 1) * P], sq[:, h % 2, c:c + n], start=True, stop=True)
                    last.then_inc(summed, 1)
                pe.wait_ge(wl, PRE + 16)
                pe.wait_ge(gated, PRE + GH)
                pe.wait_ge(rooted, PRE + GH)
                for t in range(KD):
                    if t >= 2:
                        pe.wait_ge(added, PRE + t - 1)
                    for k in range(GH):
                        for b, (c, n) in enumerate(BLK):
                            last = pe.matmul(pm[:, t % 2, b, 0:n], w[:, k, t * P:(t + 1) * P], oT[:, k, c:c + n], start=(k == 0), stop=(k == GH - 1))
                    last.then_inc(summed, 1)

            @block.scalar
            def _(act):
                for h in range(GH):
                    act.wait_ge(summed, PRE + h + 1)
                    if h >= 2:
                        act.wait_ge(normed, PRE + h - 1)
                    for b, (c, n) in enumerate(BLK):
                        last = act.activation(root[:, h % 2, c:c + n], pm[:, h % 2, b, 0:n], ACT.Sqrt, bias=m["eps"][:, :], scale=1.0 / DV)
                    last.then_inc(rooted, 1)

            @block.vector
            def _(dve):
                for h in range(GH):
                    dve.wait_ge(rooted, PRE + h + 1)
                    dve.reciprocal(root[:, h % 2, :], root[:, h % 2, :]).then_inc(inverted, 1)
                    dve.wait_ge(inverted, PRE + h + 1)
                    dve.scalar_tensor_tensor(out=oT[:, h, :], in0=oT[:, h, :], scalar=m["gains"][:, G_ONORM:G_ONORM + 1], in1=root[:, h % 2, :],
                                             op0=ALU.mult, op1=ALU.mult).then_inc(normed, 1)
                    dve.wait_ge(normed, PRE + h + 1)
                    dve.tensor_tensor(oT[:, h, :], oT[:, h, :], zT[:, h, :], ALU.mult).then_inc(gated, 1)
                for t in range(KD):
                    dve.wait_ge(summed, PRE + GH + t + 1)
                    dve.tensor_tensor(xT[:, t, 0:768].rearrange("p (b c) -> p b c", b=2), xT[:, t, 0:768].rearrange("p (b c) -> p b c", b=2),
                                      pm[:, t % 2, 0:2, 0:384], ALU.add)
                    dve.tensor_tensor(xT[:, t, 768:TOK], xT[:, t, 768:TOK], pm[:, t % 2, 2, 0:320], ALU.add).then_inc(added, 1)


def tails_stage(nc, m, io):
    with Stage(nc, "tails") as st:
        rows = st.sb("rows", [HIST * 32, 2, P])
        pt = st.ps("pt", [HIST * 32, 2, P])
        turned, copied, stored = st.sem("turned"), st.sem("copied"), st.sem("stored")
        with st.block() as block:
            @block.tensor
            def _(pe):
                for a in range(2):
                    last = pe.transpose(pt[:, a, :], m["tail"][:, a, :, :].rearrange("p j t -> p (j t)"), m["const"][:, 0:P])
                last.then_inc(turned, 1)

            @block.vector
            def _(dve):
                dve.wait_ge(turned, PRE + 1)
                dve.tensor_copy(rows[:, :, :], pt[:, :, :]).then_inc(copied, 1)

            @block.sync
            def _(sp):
                sp.wait_ge(copied, PRE + 1)
                for a, name in enumerate(("conv_p", "conv_s")):
                    sp.dma_start(io[name][0, 0].rearrange("j (t p) -> (j t) p", p=P), rows[:, a, :]).then_inc(stored, 16)
                sp.wait_ge(stored, PRE + 32)


def blocks3(tile):
    return tile[:, 0:768].rearrange("p (b c) -> p b c", b=2), tile[:, 768:TOK]


def ffn_up_stage(nc, m, hT, hid, w1, w3):
    with Stage(nc, "ffnup") as st:
        wa, wb = st.sb("w1", [P, 2, KD, P]), st.sb("w3", [P, 2, KD, P])
        silu = st.sb("silu", [P, TOK])
        pm = st.ps("pm", [P, 2, 3, 512])
        w_loaded = [st.sem(f"w_loaded{u}") for u in range(2)]
        used = [st.sem(f"w_used{u}") for u in range(2)]
        a_done, silued, gated = st.sem("a_done"), st.sem("silued"), st.sem("gated")
        with st.block() as block:
            @block.sync
            def _(sp):
                with sp.Fori(0, KF // 2) as i:
                    for u in range(2):
                        sp.wait_ge(used[u], PRE + i)
                        for w, dst in ((w1, wa), (w3, wb)):
                            sp.dma_start(dst[:, u, :, :], w[:, bass.ds((2 * i + u) * P, P)].rearrange("(k p) c -> p k c", p=P)).then_inc(w_loaded[u], 16)

            @block.tensor
            def _(pe):
                with pe.Fori(0, KF // 2) as i:
                    for u in range(2):
                        pe.wait_ge(w_loaded[u], PRE + 32 * (i + 1))
                        for q, (w, freed, done) in enumerate(((wa, silued, a_done), (wb, gated, used[u]))):
                            pe.wait_ge(freed, PRE + 2 * i + u)
                            for k in range(KD):
                                for b, (c, n) in enumerate(BLK):
                                    last = pe.matmul(pm[:, q, b, 0:n], w[:, u, k, :], hT[:, k, c:c + n], start=(k == 0), stop=(k == KD - 1))
                            last.then_inc(done, 1)

            @block.scalar
            def _(act):
                with act.Fori(0, KF) as f:
                    act.wait_ge(a_done, PRE + f + 1)
                    act.wait_ge(gated, PRE + f)
                    two, rest = blocks3(silu)
                    act.activation(two, pm[:, 0, 0:2, 0:384], ACT.Silu)
                    act.activation(rest, pm[:, 0, 2, 0:320], ACT.Silu).then_inc(silued, 1)

            @block.vector
            def _(dve):
                with dve.Fori(0, KF // 2) as i:
                    for u in range(2):
                        dve.wait_ge(used[u], PRE + i + 1)
                        dve.wait_ge(silued, PRE + 2 * i + u + 1)
                        two, rest = blocks3(hid[:, bass.ds(2 * i + u, 1), :].rearrange("p o t -> p (o t)"))
                        stwo, srest = blocks3(silu)
                        dve.tensor_tensor(two, stwo, pm[:, 1, 0:2, 0:384], ALU.mult)
                        dve.tensor_tensor(rest, srest, pm[:, 1, 2, 0:320], ALU.mult).then_inc(gated, 1)


def add_product_stage(nc, m, name, src, kt, load, parts=1):
    xT = m["xT"]
    with Stage(nc, name) as st:
        w = st.sb("w", [P, 2, kt, P])
        pm = st.ps("pm", [P, 2, 3, 512])
        w_loaded = [st.sem(f"w_loaded{u}") for u in range(2)]
        done = [st.sem(f"tile_summed{u}") for u in range(2)]
        added = [st.sem(f"tile_added{u}") for u in range(2)]
        with st.block() as block:
            @block.sync
            def _(sp):
                with sp.Fori(0, KD // 2) as i:
                    for u in range(2):
                        sp.wait_ge(done[u], PRE + i)
                        for to, frm in load(w[:, u, :, :], 2 * i + u):
                            sp.dma_start(to, frm).then_inc(w_loaded[u], 16)

            @block.tensor
            def _(pe):
                with pe.Fori(0, KD // 2) as i:
                    for u in range(2):
                        pe.wait_ge(w_loaded[u], PRE + 16 * parts * (i + 1))
                        pe.wait_ge(added[u], PRE + i)
                        for k in range(kt):
                            for b, (c, n) in enumerate(BLK):
                                last = pe.matmul(pm[:, u, b, 0:n], w[:, u, k, :], src[:, k, c:c + n], start=(k == 0), stop=(k == kt - 1))
                        last.then_inc(done[u], 1)

            @block.vector
            def _(dve):
                with dve.Fori(0, KD // 2) as i:
                    for u in range(2):
                        dve.wait_ge(done[u], PRE + i + 1)
                        two, rest = blocks3(xT[:, bass.ds(2 * i + u, 1), :].rearrange("p o t -> p (o t)"))
                        dve.tensor_tensor(two, two, pm[:, u, 0:2, 0:384], ALU.add)
                        dve.tensor_tensor(rest, rest, pm[:, u, 2, 0:320], ALU.add).then_inc(added[u], 1)


K_CACHE = WINDOW + PROMPT
K_SAMPLE = K_CACHE + WINDOW
KEYS = K_SAMPLE + SAMPLE
KV_T = HKV * HD // P
VS = KEYS // CHUNK



def heads_stage(nc, m, name, hT, n_tiles, rotated, dests, loads, io):
    with Stage(nc, name) as st:
        w = st.sb("w", [P, 2, KD, 4 * P])
        rope = st.sb("rope", [P, 2, TOK])
        raw = st.sb("raw", [P, 2, TOK])
        sn = st.sb("sin_part", [P, TOK])
        pm = st.ps("pm", [P, 2, 3, 512])
        w_loaded = [st.sem(f"w_loaded{u}") for u in range(2)]
        rope_l, done, copied, turned, rot, ready = (st.sem(s) for s in ("rope_loaded", "tile_summed", "tile_copied", "swapped", "rotate_step", "tile_ready"))
        with st.block() as block:
            @block.sync
            def _(sp):
                sp.dma_start(rope[:, :, :], io["rope"].rearrange("a p t -> p a t")).then_inc(rope_l, 16)
                for s, load in enumerate(loads(w)):
                    for to, frm in load:
                        sp.dma_start(to, frm).then_inc(w_loaded[s], 16)

            @block.tensor
            def _(pe):
                def swap(t):
                    pe.wait_ge(copied, PRE + t + 1)
                    for b, (c, n) in enumerate(BLK):
                        last = pe.matmul(pm[:, t % 2, b, 0:n], m["const"][:, C_ROT * P:(C_ROT + 1) * P], raw[:, t % 2, c:c + n], start=True, stop=True)
                    last.then_inc(turned, 1)

                for t in range(n_tiles):
                    s = t // 4
                    if t % 4 == 0:
                        pe.wait_ge(w_loaded[s], PRE + 16 * len(loads(w)[s]))
                    if t >= 2:
                        pe.wait_ge(ready, PRE + t - 1)
                    for k in range(KD):
                        for b, (c, n) in enumerate(BLK):
                            last = pe.matmul(pm[:, t % 2, b, 0:n], w[:, s, k, (t % 4) * P:(t % 4 + 1) * P], hT[:, k, c:c + n], start=(k == 0), stop=(k == KD - 1))
                    last.then_inc(done, 1)
                    if 1 <= t <= rotated:
                        swap(t - 1)
                if rotated == n_tiles:
                    swap(n_tiles - 1)

            @block.scalar
            def _(act):
                for t in range(n_tiles):
                    act.wait_ge(done, PRE + t + 1)
                    if t >= 2:
                        act.wait_ge(ready, PRE + t - 1)
                    two, rest = blocks3(raw[:, t % 2, :])
                    act.activation(two, pm[:, t % 2, 0:2, 0:384], ACT.Copy)
                    act.activation(rest, pm[:, t % 2, 2, 0:320], ACT.Copy).then_inc(copied, 1)

            @block.vector
            def _(dve):
                dve.wait_ge(rope_l, PRE + 16)
                step = Chain(dve, rot)
                for t in range(n_tiles):
                    if t < rotated:
                        dve.wait_ge(turned, PRE + t + 1)
                        two, rest = blocks3(sn)
                        stwo, srest = blocks3(rope[:, 1, :])
                        dve.tensor_tensor(two, stwo, pm[:, t % 2, 0:2, 0:384], ALU.mult)
                        dve.tensor_tensor(rest, srest, pm[:, t % 2, 2, 0:320], ALU.mult)
                        step(dve.tensor_tensor(raw[:, t % 2, :], raw[:, t % 2, :], rope[:, 0, :], ALU.mult))
                        for to, c in dests(t):
                            n = to.shape[-1]
                            last = dve.tensor_tensor(to, raw[:, t % 2, c:c + n], sn[:, c:c + n], ALU.add)
                        last.then_inc(ready, 1)
                        dve.wait_ge(ready, PRE + t + 1)
                    else:
                        dve.wait_ge(copied, PRE + t + 1)
                        for to, c in dests(t):
                            n = to.shape[-1]
                            last = dve.tensor_copy(to, raw[:, t % 2, c:c + n])
                        last.then_inc(ready, 1)


def values_stage(nc, m, kT, vT, v128, io):
    with Stage(nc, "values") as st:
        ck = st.sb("ck", [P, HKV * HD])
        kout = st.sb("kout", [P, 2, HKV * HD])
        pv = st.ps("pv", [P, 2, 4, P])
        pk = st.ps("pk", [P, 4, P])
        loaded, turned, copied, kturned, kcopied, stored = (st.sem(s) for s in ("loaded", "v_turned", "v_copied", "k_turned", "k_copied", "stored"))
        wins = [(s, (s - 2) * CHUNK, P) for s in range(2, 17)] + [(17, PROMPT - CHUNK, CHUNK), (VS - 1, PROMPT, SAMPLE)]
        ident = m["const"][:, 0:P]
        with st.block() as block:
            @block.sync
            def _(sp):
                sp.dma_start(ck[:, :], io["cache_k"][0].rearrange("t h d -> t (h d)")).then_inc(loaded, 16)
                sp.dma_start(v128[:, VS - 3, :], io["cache_v"][0].rearrange("t h d -> t (h d)")).then_inc(loaded, 16)
                sp.wait_ge(kcopied, PRE + 3)
                sp.dma_start(io["k_p"][0].rearrange("t h d -> t (h d)"), kout[:, 0, :]).then_inc(stored, 16)
                sp.dma_start(io["k_s"][0].rearrange("t h d -> t (h d)"), kout[0:SAMPLE, 1, :]).then_inc(stored, 16)
                sp.wait_ge(copied, PRE + len(wins))
                sp.dma_start(io["v_p"][0].rearrange("t h d -> t (h d)"), v128[:, 16, :]).then_inc(stored, 16)
                sp.dma_start(io["v_s"][0].rearrange("t h d -> t (h d)"), v128[0:SAMPLE, VS - 1, :]).then_inc(stored, 16)
                sp.wait_ge(loaded, PRE + 32)
                sp.wait_ge(stored, PRE + 64)

            @block.tensor
            def _(pe):
                for i, (s, tok, n) in enumerate(wins):
                    if i >= 2:
                        pe.wait_ge(copied, PRE + i - 1)
                    for j in range(KV_T):
                        last = pe.transpose(pv[0:n, i % 2, j, :], vT[:, j, tok:tok + n], ident)
                    last.then_inc(turned, 1)
                pe.wait_ge(loaded, PRE + 32)
                for i in range(3):
                    if i:
                        pe.wait_ge(kcopied, PRE + i)
                    for j in range(KV_T):
                        last = (pe.transpose(pk[:, j, :], ck[:, j * P:(j + 1) * P], ident) if i == 0 else
                                pe.transpose(pk[:, j, :], kT[:, j, K_CACHE - WINDOW:K_CACHE], ident) if i == 1 else
                                pe.transpose(pk[0:SAMPLE, j, :], kT[:, j, K_SAMPLE:KEYS], ident))
                    last.then_inc(kturned, 1)

            @block.scalar
            def _(act):
                for i, (s, tok, n) in enumerate(wins):
                    act.wait_ge(turned, PRE + i + 1)
                    act.activation(v128[0:n, s, :].rearrange("p (j c) -> p j c", j=KV_T), pv[0:n, i % 2, 0:KV_T, :], ACT.Copy).then_inc(copied, 1)

            @block.vector
            def _(dve):
                for i, (to, n) in enumerate(((kT[:, :, K_CACHE:K_SAMPLE], P), (kout[:, 0, :].rearrange("p (j c) -> p j c", j=KV_T), P),
                                             (kout[0:SAMPLE, 1, :].rearrange("p (j c) -> p j c", j=KV_T), SAMPLE))):
                    dve.wait_ge(kturned, PRE + i + 1)
                    dve.tensor_copy(to, pk[0:n, 0:KV_T, :]).then_inc(kcopied, 1)


def attend_stage(nc, m, qT, kT, v128, aT):
    SPAN = WINDOW + CHUNK
    with Stage(nc, "attend") as st:
        qs, ks, vs = st.sb("qs", [P, 8, CHUNK]), st.sb("ks", [P, KV_T, SPAN]), st.sb("vs", [P, 2, HKV * HD])
        snk = st.sb("snk", [P, HKV, 2])
        prob = st.sb("prob", [P, HKV, 2, SPAN])
        pT = st.sb("pT", [P, 2, 4, P])
        osb = st.sb("osb", [P, HKV, 2, HD])
        mx, nmx, sm, es, rd = (st.sb(n, [P, HKV, 2]) for n in ("mx", "nmx", "sm", "es", "rd"))
        ps = st.ps("scores", [P, HKV, 512])
        pt = st.ps("turned", [P, 2, 4, P])
        po, poT = st.ps("out", [P, HKV, 2, HD]), st.ps("outT", [P, HKV, P])
        names = ("sink_set", "q_staged", "kv_staged", "scored", "max_ready", "bias_ready", "exped", "den_step", "den_ready", "p_turned", "p_copied_a", "p_copied_b",
                 "pv_summed", "o_normed", "o_turned", "o_copied")
        e = {n: st.sem(n) for n in names}
        passed = st.sem("passed")
        ident = m["const"][:, 0:P]
        aview = aT[:, :, :].rearrange("p (j l) t -> p j l t", l=2)
        with st.block() as block:
            @block.tensor
            def _(pe):
                def chunk(i, keys, v0, v1):
                    pe.wait_ge(e["q_staged"], PRE + i + 1)
                    pe.wait_ge(e["kv_staged"], PRE + i + 1)
                    for jp in range(2):
                        pe.wait_ge(e["exped"], PRE + 2 * i)
                        hold(pe, passed)
                        for b in range(2):
                            for g in range(4):
                                last = pe.matmul(ps[CHUNK * (g % 2):CHUNK * (g % 2) + CHUNK, 2 * jp + b, (g // 2) * SPAN:(g // 2) * SPAN + keys],
                                                 qs[HD * b:HD * b + HD, 4 * jp + g, :], ks[HD * b:HD * b + HD, jp, 0:keys], start=True, stop=True,
                                                 skip_group_check=True)
                        last.then_inc(e["scored"], 1)
                    for jp in range(2):
                        pe.wait_ge(e["exped"], PRE + 2 * i + jp + 1)
                        pe.wait_ge(e["p_copied_a"], PRE + 2 * i + jp)
                        pe.wait_ge(e["p_copied_b"], PRE + 2 * i + jp)
                        for x in range(4):
                            p = prob[:, 2 * jp + x // 2, x % 2, :]
                            if v0 is not None:
                                last = pe.transpose(pt[:, 0, x, :], p[:, 0:P], ident)
                            if v1 is not None:
                                last = pe.transpose(pt[0:CHUNK, 1, x, :], p[:, keys - CHUNK:keys], ident)
                        last.then_inc(e["p_turned"], 1)
                        pe.wait_ge(e["p_copied_a"], PRE + 2 * i + jp + 1)
                        pe.wait_ge(e["p_copied_b"], PRE + 2 * i + jp + 1)
                        pe.wait_ge(e["o_normed"], PRE + 2 * i + jp)
                        for x in range(4):
                            j = 2 * jp + x // 2
                            pieces = [(pT[:, 0, x, :], vs[:, 0, j * HD:(j + 1) * HD])] if v0 is not None else []
                            if v1 is not None:
                                pieces.append((pT[0:CHUNK, 1, x, :], vs[0:CHUNK, 1, j * HD:(j + 1) * HD]))
                            for n, (l, r) in enumerate(pieces):
                                last = pe.matmul(po[:, j, x % 2, :], l, r, start=(n == 0), stop=(n == len(pieces) - 1))
                        last.then_inc(e["pv_summed"], 1)
                    pe.wait_ge(e["o_normed"], PRE + 2 * i + 2)
                    pe.wait_ge(e["o_copied"], PRE + i)
                    for j in range(HKV):
                        last = pe.transpose(poT[:, j, :], osb[:, j, :, :].rearrange("p a c -> p (a c)"), ident)
                    last.then_inc(e["o_turned"], 1)

                chunk(0, CHUNK, None, True)
                chunk(1, 2 * CHUNK, True, None)
                with pe.Fori(2, 16) as c:
                    chunk(c, SPAN, True, True)
                chunk(16, SPAN, True, True)

            @block.gpsimd
            def _(pool):
                def chunk(i, keys, k0, v0, v1):
                    pool.wait_ge(e["pv_summed"], PRE + 2 * i)
                    if v0 is not None:
                        pool.tensor_copy(vs[:, 0, :], v128[:, bass.ds(v0, 1), :].rearrange("p o c -> p (o c)"))
                    if v1 is not None:
                        pool.tensor_copy(vs[0:CHUNK, 1, :], v128[0:CHUNK, bass.ds(v1, 1), :].rearrange("p o c -> p (o c)"))
                    pool.tensor_copy(ks[:, :, 0:keys], kT[:, :, bass.ds(k0, keys)]).then_inc(e["kv_staged"], 1)

                chunk(0, CHUNK, WINDOW, None, 2)
                chunk(1, 2 * CHUNK, WINDOW, 2, None)
                with pool.Fori(2, 16) as c:
                    chunk(c, SPAN, c * CHUNK, c, c + 2)
                chunk(16, SPAN, K_CACHE, VS - 3, VS - 1)

            @block.scalar
            def _(act):
                def chunk(i, keys):
                    act.wait_ge(e["scored"], PRE + 2 * i)
                    act.activation(qs[:, :, :], qT[:, :, bass.ds(i * CHUNK, CHUNK)], ACT.Copy, scale=HD ** -0.5).then_inc(e["q_staged"], 1)
                    for jp in range(2):
                        act.wait_ge(e["bias_ready"], PRE + 2 * i + jp + 1)
                        act.activation(es[:, 2 * jp:2 * jp + 2, :], es[:, 2 * jp:2 * jp + 2, :], ACT.Exp)
                        for x in range(4):
                            j = 2 * jp + x // 2
                            last = act.activation(prob[:, j, x % 2, 0:keys], ps[:, j, (x % 2) * SPAN:(x % 2) * SPAN + keys], ACT.Exp,
                                                  bias=nmx[:, j, x % 2:x % 2 + 1], accum_out=sm[:, j, x % 2:x % 2 + 1])
                        last.then_inc(e["exped"], 1)
                    for jp in range(2):
                        act.wait_ge(e["p_turned"], PRE + 2 * i + jp + 1)
                        if keys > CHUNK:
                            last = act.activation(pT[:, 0, :, :], pt[:, 0, :, :], ACT.Copy)
                            last.then_inc(e["p_copied_a"], 1)
                        else:
                            act.sem_inc(e["p_copied_a"], 1)
                    act.wait_ge(e["o_turned"], PRE + i + 1)
                    act.activation(aview[:, :, :, bass.ds(i * CHUNK, CHUNK)], poT[:, :, :].rearrange("p j (l q) -> p j l q", l=2), ACT.Copy).then_inc(e["o_copied"], 1)

                chunk(0, CHUNK)
                chunk(1, 2 * CHUNK)
                with act.Fori(2, 16) as c:
                    chunk(c, SPAN)
                chunk(16, SPAN)

            @block.vector
            def _(dve):
                STEPS = 4
                sv = m["swa_sinks"][:, :].rearrange("p (j g l) -> p j g l", g=2, l=2)
                dve.tensor_copy(snk[0:64, :, :], sv[0:64, :, :, 0])
                dve.tensor_copy(snk[64:128, :, :], sv[64:128, :, :, 1]).then_inc(e["sink_set"], 1)
                dve.wait_ge(e["sink_set"], PRE + 1)

                def chunk(i, keys):
                    step = Chain(dve, e["den_step"], i * 2 * STEPS)
                    for jp in range(2):
                        h = slice(2 * jp, 2 * jp + 2)
                        dve.wait_ge(e["scored"], PRE + 2 * i + jp + 1)
                        sc = ps[:, h, 0:2 * SPAN].rearrange("p j (g c) -> p j g c", g=2)[:, :, :, 0:keys]
                        step(dve.tensor_reduce(mx[:, h, :], sc, AX.X, ALU.max))
                        step(dve.tensor_tensor(mx[:, h, :], mx[:, h, :], snk[:, h, :], ALU.max))
                        dve.tensor_tensor(es[:, h, :], snk[:, h, :], mx[:, h, :], ALU.subtract)
                        dve.tensor_scalar(nmx[:, h, :], mx[:, h, :], -1.0, None, ALU.mult).then_inc(e["bias_ready"], 1)
                    for jp in range(2):
                        h = slice(2 * jp, 2 * jp + 2)
                        if keys != 2 * CHUNK:
                            dve.wait_ge(e["p_turned"], PRE + 2 * i + jp + 1)
                            dve.tensor_copy(pT[0:CHUNK, 1, :, :], pt[0:CHUNK, 1, :, :]).then_inc(e["p_copied_b"], 1)
                        else:
                            dve.sem_inc(e["p_copied_b"], 1)
                        dve.wait_ge(e["exped"], PRE + 2 * i + jp + 1)
                        step(dve.tensor_tensor(rd[:, h, :], sm[:, h, :], es[:, h, :], ALU.add))
                        step(dve.reciprocal(rd[:, h, :], rd[:, h, :]))
                        dve.wait_ge(e["pv_summed"], PRE + 2 * i + jp + 1)
                        dve.tensor_tensor(osb[:, h, :, :], po[:, h, :, :], rd[:, h, :].unsqueeze(3).broadcast_to([P, 2, 2, HD]), ALU.mult).then_inc(e["o_normed"], 1)

                chunk(0, CHUNK)
                chunk(1, 2 * CHUNK)
                with dve.Fori(2, 16) as c:
                    chunk(c, SPAN)
                chunk(16, SPAN)


TOP_K = 2
CAP = 320
OVER_MAX = TOP_K * TOK // CAP
JOBS = NE + OVER_MAX
MORE = (TOK - 1) // CAP
SLOTS = JOBS * CAP
CAP_T = [(s, min(P, CAP - s)) for s in range(0, CAP, P)]


def route_stage(nc, m, hT, io, r):
    ramp, pidx = m["const"][:, N_CONST * P:N_CONST * P + NE], m["const"][:, N_CONST * P + NE:N_CONST * P + NE + 1]
    with Stage(nc, "route") as st:
        wr = st.sb("wr", [P, KD, NE])
        hrow = st.sb("hrow", [P, 2, D])
        lg, one, two, tmp, tmp2, offs, rank = (st.sb(n, [P, NT, NE]) for n in ("lg", "one", "two", "tmp", "tmp2", "offs", "rank"))
        m1, m2, rt, e21 = (st.sb(n, [P, NT]) for n in ("m1", "m2", "rt", "e21"))
        total, over, ends, coef, first, t8 = (st.sb(n, [P, NE]) for n in ("total", "over", "ends", "coef", "first", "t8"))
        slotf = st.sb("slotf", [P, TOP_K, NT])
        jobsf = st.sb("jobsf", [P, 16])
        ids = st.sb("ids", [P, NT], I32)
        zero = st.sb("zero", [P, SLOTS // P], I32)
        pl, prank, ptot = (st.ps(n, [P, NT, NE]) for n in ("logits", "rank_in_tile", "tile_total"))
        ph = st.ps("ph", [P, 4, 4, P])
        w_loaded, proj, vs, es, counted, ranked = (st.sem(n) for n in ("w_loaded", "projected", "vector_step", "exped", "counted", "ranked"))
        turned, h_copied = st.sem("turned"), st.sem("h_copied")
        h_stored = [st.sem(f"h_stored{u}") for u in range(2)]
        ids_set, slots_ready = st.sem("ids_set"), st.sem("slots_ready")
        zeroed, scattered = st.sem("zeroed", pre=False), st.sem("scattered", pre=False)
        zero_set = st.sem("zero_set")
        over_tiles = lambda a: a.unsqueeze(1).broadcast_to([P, NT, NE])
        over_experts = lambda a: a.unsqueeze(2).broadcast_to([P, NT, NE])
        with st.block() as block:
            @block.sync
            def _(sp):
                sp.dma_start(wr[:, :, :], io["moe_router"][0].rearrange("(k p) e -> p k e", p=P)).then_inc(w_loaded, 16)
                for t, (s, n) in enumerate(TILES):
                    sp.wait_ge(h_copied, PRE + 2 * t + 2)
                    sp.dma_start(m["h_dram"][s:s + n, :], hrow[0:n, t % 2, :]).then_inc(h_stored[t % 2], 16)
                sp.wait_ge(h_stored[0], PRE + 16 * ((NT + 1) // 2))
                sp.wait_ge(h_stored[1], PRE + 16 * (NT // 2))

            @block.gpsimd
            def _(pool):
                pool.memset(zero[:, :], 0).then_inc(zero_set, 1)
                pool.wait_ge(zero_set, PRE + 1)
                pool.dma_start(m["slot_tok"].rearrange("(p c) o -> p (c o)", p=P), zero[:, :]).then_inc(zeroed, 16)
                pool.wait_ge(zeroed, 16)
                pool.wait_ge(ids_set, PRE + NT)
                pool.wait_ge(slots_ready, PRE + 1)
                for a in range(TOP_K):
                    for t, (s, n) in enumerate(TILES):
                        pool.indirect_dma_start(out=m["slot_tok"], out_offset=bass.IndirectOffsetOnAxis(ap=r["slot"][0:n, a, t:t + 1], axis=0),
                                                in_=ids[0:n, t:t + 1], in_offset=None).then_inc(scattered, 16)
                        pool.wait_ge(scattered, 16 * (a * NT + t + 1))

            @block.tensor
            def _(pe):
                pe.wait_ge(w_loaded, PRE + 16)
                for t, (s, n) in enumerate(TILES):
                    for k in range(KD):
                        last = pe.matmul(pl[0:n, t, :], hT[:, k, s:s + n], wr[:, k, :], start=(k == 0), stop=(k == KD - 1))
                last.then_inc(proj, 1)
                for t, (s, n) in enumerate(TILES):
                    for h in range(2):
                        i = 2 * t + h
                        if i >= 4:
                            pe.wait_ge(h_copied, PRE + i - 3)
                        for k in range(4):
                            last = pe.transpose(ph[0:n, i % 4, k, :], hT[:, 4 * h + k, s:s + n], m["const"][:, 0:P])
                        last.then_inc(turned, 1)
                pe.wait_ge(counted, PRE + 1)
                pe.matmul(prank[:, :, :], m["const"][:, C_STRICT * P:(C_STRICT + 1) * P], tmp[:, :, :], start=True, stop=True)
                pe.matmul(ptot[:, :, :], m["const"][:, C_ONES * P:(C_ONES + 1) * P], tmp[:, :, :], start=True, stop=True).then_inc(ranked, 1)

            @block.scalar
            def _(act):
                for i in range(2 * NT):
                    t, h = i // 2, i % 2
                    n = TILES[t][1]
                    if t >= 2:
                        act.wait_ge(h_stored[t % 2], PRE + 16 * (t // 2))
                    act.wait_ge(turned, PRE + i + 1)
                    act.activation(hrow[0:n, t % 2, h * 512:h * 512 + 512].rearrange("p (k c) -> p k c", c=P), ph[0:n, i % 4, :, :], ACT.Copy).then_inc(h_copied, 1)
                act.wait_ge(vs, PRE + 14)
                act.activation(e21[:, :], m2[:, :], ACT.Exp).then_inc(es, 1)

            @block.vector
            def _(dve):
                v = Chain(dve, vs)
                for t in range(NT):
                    dve.tensor_scalar(ids[:, t:t + 1], pidx, float(t * P), None, ALU.add).then_inc(ids_set, 1)
                v(dve.memset(lg[:, :, :], 0.0))
                dve.wait_ge(proj, PRE + 1)
                dve.tensor_copy(lg[:, 0:NT - 1, :], pl[:, 0:NT - 1, :])
                v(dve.tensor_copy(lg[0:64, NT - 1, :], pl[0:64, NT - 1, :]))

                def best(top, onehot):
                    v(dve.tensor_reduce(top[:, :], lg[:, :, :], AX.X, ALU.max))
                    v(dve.tensor_tensor(tmp[:, :, :], lg[:, :, :], over_experts(top[:, :]), ALU.is_equal))
                    v(dve.tensor_tensor(tmp[:, :, :], tmp[:, :, :], over_tiles(ramp), ALU.mult))
                    v(dve.tensor_reduce(rt[:, :], tmp[:, :, :], AX.X, ALU.max))
                    return dve.tensor_tensor(onehot[:, :, :], over_tiles(ramp), over_experts(rt[:, :]), ALU.is_equal)

                v(best(m1, one))
                v(dve.scalar_tensor_tensor(out=lg[:, :, :], in0=one[:, :, :], scalar=-3.0e38, in1=lg[:, :, :], op0=ALU.mult, op1=ALU.add))
                last = best(m2, two)
                v(last)
                v(dve.tensor_tensor(m2[:, :], m2[:, :], m1[:, :], ALU.subtract))
                dve.memset(one[64:128, NT - 1, :], 0.0)
                v(dve.memset(two[64:128, NT - 1, :], 0.0))
                v(dve.tensor_tensor(tmp[:, :, :], one[:, :, :], two[:, :, :], ALU.add))
                dve.sem_inc(counted, 1)
                dve.wait_ge(es, PRE + 1)
                v(dve.tensor_scalar(m1[:, :], e21[:, :], 1.0, None, ALU.add))
                v(dve.reciprocal(r["gate"][:, 0, :], m1[:, :]))
                dve.tensor_tensor(r["gate"][:, 1, :], r["gate"][:, 0, :], e21[:, :], ALU.mult)
                dve.wait_ge(ranked, PRE + 1)
                v(dve.memset(offs[:, 0, :], 0.0))
                for t in range(1, NT):
                    v(dve.tensor_tensor(offs[:, t, :], offs[:, t - 1, :], ptot[:, t - 1, :], ALU.add))
                v(dve.tensor_tensor(total[:, :], offs[:, NT - 1, :], ptot[:, NT - 1, :], ALU.add))
                v(dve.tensor_tensor(rank[:, :, :], offs[:, :, :], prank[:, :, :], ALU.add))
                v(dve.tensor_scalar(over[:, :], total[:, :], float(CAP), None, ALU.is_gt))
                for k in range(2, MORE + 1):
                    v(dve.scalar_tensor_tensor(out=over[:, :], in0=total[:, :], scalar=float(k * CAP), in1=over[:, :], op0=ALU.is_gt, op1=ALU.add))
                v(dve.tensor_copy(ends[:, 0:1], over[:, 0:1]))
                for x in range(1, NE):
                    v(dve.tensor_tensor(ends[:, x:x + 1], ends[:, x - 1:x], over[:, x:x + 1], ALU.add))
                v(dve.tensor_tensor(coef[:, :], ends[:, :], over[:, :], ALU.subtract))
                v(dve.scalar_tensor_tensor(out=coef[:, :], in0=coef[:, :], scalar=-1.0, in1=ramp, op0=ALU.add, op1=ALU.add))
                dve.tensor_scalar(first[:, :], ramp, -float(CAP), float(NE * CAP), ALU.mult, ALU.add)
                v(dve.tensor_scalar(coef[:, :], coef[:, :], float(CAP), None, ALU.mult))
                v(dve.tensor_scalar(tmp2[:, :, :], rank[:, :, :], float(CAP), None, ALU.is_ge))
                v(dve.tensor_tensor(tmp2[:, :, :], tmp2[:, :, :], over_tiles(coef[:, :]), ALU.mult))
                v(dve.tensor_tensor(tmp2[:, :, :], tmp2[:, :, :], rank[:, :, :], ALU.add))
                v(dve.tensor_tensor(tmp2[:, :, :], tmp2[:, :, :], over_tiles(first[:, :]), ALU.add))
                v(dve.tensor_tensor(one[:, :, :], one[:, :, :], tmp2[:, :, :], ALU.mult))
                v(dve.tensor_tensor(two[:, :, :], two[:, :, :], tmp2[:, :, :], ALU.mult))
                v(dve.tensor_reduce(slotf[:, 0, :], one[:, :, :], AX.X, ALU.add))
                v(dve.tensor_reduce(slotf[:, 1, :], two[:, :, :], AX.X, ALU.add))
                dve.tensor_copy(r["slot"][:, :, :], slotf[:, :, :]).then_inc(slots_ready, 1)
                v(dve.tensor_scalar(jobsf[:, 0:1], ends[:, NE - 1:NE], float(NE), None, ALU.add))
                for i in range(OVER_MAX):
                    v(dve.tensor_scalar(t8[:, 0:NE], ends[:, :], float(i), None, ALU.is_le))
                    v(dve.tensor_reduce(jobsf[:, NE + i:NE + i + 1], t8[:, 0:NE - 1], AX.X, ALU.add))
                dve.memset(jobsf[:, 1:NE], 0.0)
                v(dve.memset(jobsf[:, JOBS:16], 0.0))
                dve.tensor_copy(r["jobs"][:, :], jobsf[:, :])


def expert_stage(nc, m, io, r):
    w1, w3, w2 = io["moe_w1"][0], io["moe_w3"][0], io["moe_w2"][0]
    NF, ND = KF // 2, KD // 2
    FILLS = KD + 2 * len(CAP_T)
    with Stage(nc, "experts") as st:
        ids = st.sb("ids", [P, len(CAP_T)], I32)
        rows = st.sb("rows", [P, len(CAP_T), D])
        hx = st.sb("hx", [P, KD, CAP])
        w13 = st.sb("w13", [P, 2, 2, KD, P])
        hid = st.sb("hid", [P, KF, CAP])
        wd = st.sb("wd", [P, 2, KF, P])
        sg = st.sb("sg", [P, 2, CAP])
        yT = st.sb("yT", [P, KD, CAP])
        yrow = st.sb("yrow", [P, len(CAP_T), D])
        pa, pb, pd, pt = (st.ps(n, [P, 2, 512]) for n in ("pa", "pb", "pd", "pt"))
        zero_set, tail_zeroed, passed = st.sem("zero_set"), st.sem("tail_zeroed"), st.sem("passed")
        one = lambda n: st.sem(n)
        two = lambda n: [st.sem(f"{n}{u}") for u in range(2)]
        ids_l, gathered = st.sem("ids_loaded", pre=False), st.sem("gathered", pre=False)
        turned, t_copied, y_stored = one("turned"), one("turn_copied"), one("y_stored")
        w_l, wd_l, used, silued, gated, summed, y_copied, a_done = (two(n) for n in (
            "w_loaded", "wd_loaded", "w_used", "silued", "gated", "down_summed", "y_copied", "a_done"))

        def jobs(eng, job):
            with eng.Fori(0, NE) as j:
                job(j, j)
            n_jobs = eng.value_load(r["jobs"][0:1, 0:1], min_val=NE, max_val=JOBS)
            with eng.Fori(NE, JOBS) as j:
                with eng.If(j < n_jobs):
                    job(j, None)

        with st.block() as block:
            @block.sync
            def _(sp):
                def job(j, e):
                    if e is None:
                        e = sp.value_load(r["jobs"][0:1, bass.ds(j, 1)], min_val=0, max_val=NE - 1)
                    with sp.Fori(0, NF) as i:
                        for u in range(2):
                            sp.wait_ge(used[u], PRE + NF * j + i)
                            for x, w in enumerate((w1, w3)):
                                sp.dma_start(w13[:, u, x, :, :], w[bass.ds(e, 1), :, bass.ds((2 * i + u) * P, P)].rearrange("o (k p) c -> p (o k) c", p=P)).then_inc(w_l[u], 16)
                    with sp.Fori(0, ND) as i:
                        for u in range(2):
                            sp.wait_ge(summed[u], PRE + ND * j + i)
                            sp.dma_start(wd[:, u, :, :], w2[bass.ds(e, 1), :, bass.ds((2 * i + u) * P, P)].rearrange("o (k p) c -> p (o k) c", p=P)).then_inc(wd_l[u], 16)

                jobs(sp, job)

            @block.gpsimd
            def _(pool):
                def job(j, e):
                    for i, (s, n) in enumerate(CAP_T):
                        pool.dma_start(ids[0:n, i:i + 1], m["slot_tok"][bass.ds(j * CAP + s, n), :]).then_inc(ids_l, 16)
                    pool.wait_ge(ids_l, 48 * (j + 1))
                    pool.wait_ge(turned, PRE + FILLS * j)
                    hold(pool, passed)
                    for i, (s, n) in enumerate(CAP_T):
                        pool.indirect_dma_start(out=rows[0:n, i, :], out_offset=None, in_=m["h_dram"],
                                                in_offset=bass.IndirectOffsetOnAxis(ap=ids[0:n, i:i + 1].bitcast(U32), axis=0)).then_inc(gathered, 16)
                    pool.wait_ge(gathered, 48 * (j + 1))

                jobs(pool, job)

            @block.tensor
            def _(pe):
                ident = m["const"][:, 0:P]

                def job(j, e):
                    fill = 0
                    pe.wait_ge(gathered, 48 * (j + 1))
                    for k in range(KD):
                        pe.wait_ge(t_copied, PRE + FILLS * j + max(fill - 1, 0))
                        for i, (s, n) in enumerate(CAP_T):
                            last = pe.transpose(pt[:, fill % 2, s:s + n], rows[0:n, i, k * P:(k + 1) * P], ident[0:n, 0:n])
                        last.then_inc(turned, 1)
                        fill += 1
                    pe.wait_ge(t_copied, PRE + FILLS * j + KD)
                    hold(pe, passed)
                    with pe.Fori(0, NF) as i:
                        for u in range(2):
                            pe.wait_ge(w_l[u], PRE + 32 * (NF * j + i + 1))
                            for x, (bank, freed, done) in enumerate(((pa, silued, a_done), (pb, gated, used))):
                                pe.wait_ge(freed[u], PRE + NF * j + i)
                                for k in range(KD):
                                    last = pe.matmul(bank[:, u, 0:CAP], w13[:, u, x, k, :], hx[:, k, :], start=(k == 0), stop=(k == KD - 1))
                                last.then_inc(done[u], 1)
                    for u in range(2):
                        pe.wait_ge(gated[u], PRE + NF * (j + 1))
                    hold(pe, passed)
                    with pe.Fori(0, ND) as i:
                        for u in range(2):
                            pe.wait_ge(wd_l[u], PRE + 16 * (ND * j + i + 1))
                            pe.wait_ge(y_copied[u], PRE + ND * j + i)
                            for k in range(KF):
                                last = pe.matmul(pd[:, u, 0:CAP], wd[:, u, k, :], hid[:, k, :], start=(k == 0), stop=(k == KF - 1))
                            last.then_inc(summed[u], 1)
                    for u in range(2):
                        pe.wait_ge(y_copied[u], PRE + ND * (j + 1))
                    for i, (s, n) in enumerate(CAP_T):
                        for h in range(2):
                            pe.wait_ge(t_copied, PRE + FILLS * j + fill - 1)
                            hold(pe, passed)
                            for k in range(4):
                                last = pe.transpose(pt[0:n, fill % 2, k * P:(k + 1) * P], yT[:, 4 * h + k, s:s + n], ident)
                            last.then_inc(turned, 1)
                            fill += 1

                jobs(pe, job)

            @block.scalar
            def _(act):
                def job(j, e):
                    with act.Fori(0, NF) as i:
                        for u in range(2):
                            act.wait_ge(a_done[u], PRE + NF * j + i + 1)
                            act.wait_ge(gated[u], PRE + NF * j + i)
                            act.activation(sg[:, u, :], pa[:, u, 0:CAP], ACT.Silu).then_inc(silued[u], 1)
                    with act.Fori(0, ND) as i:
                        for u in range(2):
                            act.wait_ge(summed[u], PRE + ND * j + i + 1)
                            act.activation(yT[:, bass.ds(2 * i + u, 1), :].rearrange("p o c -> p (o c)"), pd[:, u, 0:CAP], ACT.Copy).then_inc(y_copied[u], 1)
                    act.wait_ge(t_copied, PRE + FILLS * (j + 1))
                    for i, (s, n) in enumerate(CAP_T):
                        act.dma_start(m["y_dram"][bass.ds(j * CAP + s, n), :], yrow[0:n, i, :]).then_inc(y_stored, 16)

                act.wait_ge(zero_set, PRE + 1)
                act.dma_start(m["y_dram"][NE * CAP:, :].rearrange("(a p) c -> p a c", p=P),
                              yrow[:, 0:1, :].broadcast_to([P, OVER_MAX * CAP // P, D])).then_inc(tail_zeroed, 16)
                jobs(act, job)
                n_jobs = act.value_load(r["jobs"][0:1, 0:1], min_val=NE, max_val=JOBS)
                act.wait_ge(y_stored, PRE + 48 * n_jobs)
                hold(act, passed)

            @block.vector
            def _(dve):
                def job(j, e):
                    for k in range(KD):
                        dve.wait_ge(turned, PRE + FILLS * j + k + 1)
                        dve.tensor_copy(hx[:, k, :], pt[:, k % 2, 0:CAP]).then_inc(t_copied, 1)
                    with dve.Fori(0, NF) as i:
                        for u in range(2):
                            dve.wait_ge(used[u], PRE + NF * j + i + 1)
                            dve.wait_ge(silued[u], PRE + NF * j + i + 1)
                            dve.tensor_tensor(hid[:, bass.ds(2 * i + u, 1), :].rearrange("p o c -> p (o c)"), sg[:, u, :], pb[:, u, 0:CAP], ALU.mult).then_inc(gated[u], 1)
                    dve.wait_ge(y_stored, PRE + 48 * j)
                    dve.wait_ge(tail_zeroed, PRE + 16)
                    fill = KD
                    for i, (s, n) in enumerate(CAP_T):
                        for h in range(2):
                            dve.wait_ge(turned, PRE + FILLS * j + fill + 1)
                            dve.tensor_copy(yrow[0:n, i, h * 512:h * 512 + 512], pt[0:n, fill % 2, :]).then_inc(t_copied, 1)
                            fill += 1

                dve.memset(yrow[:, 0, :], 0.0).then_inc(zero_set, 1)
                jobs(dve, job)


def final_stage(nc, m, io, r):
    outs = [io["y_prompt"][0, s:s + n, :] if s < PROMPT else io["y_sample"][0, :, :] for s, n in TILES]
    with Stage(nc, "final") as st:
        y = st.sb("y", [P, 2, TOP_K, D])
        x, sq = st.sb("x", [P, 2, D]), st.sb("sq", [P, D])
        gain = st.sb("gain", [P, D])
        ss, root, rinv = (st.sb(n, [P, NT]) for n in ("ss", "root", "rinv"))
        pt = st.ps("pt", [P, 2, 2, 512])
        g_loaded, turned, mixed, step, squared, rooted, ready = (st.sem(n) for n in ("gain_loaded", "turned", "mixed", "vector_step", "squared", "rooted", "ready"))
        gathered, stored = [st.sem(f"gathered{u}", pre=False) for u in range(2)], [st.sem(f"stored{u}") for u in range(2)]
        with st.block() as block:
            @block.gpsimd
            def _(pool):
                for t, (s, n) in enumerate(TILES):
                    if t >= 2:
                        pool.wait_ge(mixed, PRE + t - 1)
                    for a in range(TOP_K):
                        pool.indirect_dma_start(out=y[0:n, t % 2, a, :], out_offset=None, in_=m["y_dram"],
                                                in_offset=bass.IndirectOffsetOnAxis(ap=r["slot"][0:n, a, t:t + 1], axis=0)).then_inc(gathered[t % 2], 16)

            @block.sync
            def _(sp):
                sp.dma_start(gain[:, :], io["final_norm"].unsqueeze(0).broadcast_to([P, D])).then_inc(g_loaded, 16)
                for t, (s, n) in enumerate(TILES):
                    sp.wait_ge(ready, PRE + t + 1)
                    sp.dma_start(outs[t], x[0:n, t % 2, :]).then_inc(stored[t % 2], 16)
                sp.wait_ge(stored[0], PRE + 16 * ((NT + 1) // 2))
                sp.wait_ge(stored[1], PRE + 16 * (NT // 2))

            @block.tensor
            def _(pe):
                for t, (s, n) in enumerate(TILES):
                    if t >= 2:
                        pe.wait_ge(mixed, PRE + t - 1)
                    for k in range(KD):
                        last = pe.transpose(pt[0:n, t % 2, k // 4, (k % 4) * P:(k % 4 + 1) * P], m["xT"][:, k, s:s + n], m["const"][:, 0:P])
                    last.then_inc(turned, 1)

            @block.scalar
            def _(act):
                for t, (s, n) in enumerate(TILES):
                    act.wait_ge(mixed, PRE + t + 1)
                    if t:
                        act.wait_ge(rooted, PRE + t)
                    act.activation(sq[0:n, :], x[0:n, t % 2, :], ACT.Square, accum_out=ss[0:n, t:t + 1]).then_inc(squared, 1)
                    act.wait_ge(squared, PRE + t + 1)
                    act.activation(root[0:n, t:t + 1], ss[0:n, t:t + 1], ACT.Sqrt, bias=m["eps"][0:n, :], scale=1.0 / D).then_inc(rooted, 1)

            @block.vector
            def _(dve):
                v = Chain(dve, step)
                dve.wait_ge(g_loaded, PRE + 16)
                for t, (s, n) in enumerate(TILES):
                    dve.wait_ge(turned, PRE + t + 1)
                    dve.wait_ge(gathered[t % 2], 32 * (t // 2 + 1))
                    if t >= 2:
                        dve.wait_ge(stored[t % 2], PRE + 16 * (t // 2))
                    xo = x[0:n, t % 2, :].rearrange("p (h c) -> p h c", h=2)
                    yy = y[0:n, t % 2, :, :].rearrange("p a (h c) -> p a h c", h=2)
                    v(dve.scalar_tensor_tensor(out=xo, in0=yy[:, 0], scalar=r["gate"][0:n, 0, t:t + 1], in1=pt[0:n, t % 2, :, :], op0=ALU.mult, op1=ALU.add))
                    dve.scalar_tensor_tensor(out=xo, in0=yy[:, 1], scalar=r["gate"][0:n, 1, t:t + 1], in1=xo, op0=ALU.mult, op1=ALU.add).then_inc(mixed, 1)
                    dve.wait_ge(rooted, PRE + t + 1)
                    v(dve.reciprocal(rinv[0:n, t:t + 1], root[0:n, t:t + 1]))
                    dve.scalar_tensor_tensor(out=x[0:n, t % 2, :], in0=x[0:n, t % 2, :], scalar=rinv[0:n, t:t + 1], in1=gain[0:n, :], op0=ALU.mult, op1=ALU.mult).then_inc(ready, 1)


def moe_stages(nc, m, io):
    m["h_dram"] = nc.dram_tensor("h_rows", (TOK, D), F32).ap()
    m["slot_tok"] = nc.dram_tensor("slot_tokens", (SLOTS, 1), I32).ap()
    m["y_dram"] = nc.dram_tensor("slot_rows", (SLOTS, D), F32).ap()
    with nc.sbuf_tensor("gate", [P, TOP_K, NT], F32) as gate, nc.sbuf_tensor("slot", [P, TOP_K, NT], U32) as slot, \
            nc.sbuf_tensor("jobs", [P, 16], I32) as jobs:
        r = {"gate": gate, "slot": slot, "jobs": jobs}
        with nc.sbuf_tensor("h_moe", [P, KD, TOK], F32) as hT:
            norm_stage(nc, m, "norm4", [(hT, G_FFN1)])
            route_stage(nc, m, hT, io, r)
        expert_stage(nc, m, io, r)
        final_stage(nc, m, io, r)


def rest_stages(nc, m, io):
    sbt = nc.sbuf_tensor
    with sbt("hid", [P, KF, TOK], F32) as hid:
        with sbt("h_ffn", [P, KD, TOK], F32) as hT:
            norm_stage(nc, m, "norm1", [(hT, G_FFN0)])
            ffn_up_stage(nc, m, hT, hid, io["ffn_w1"][0], io["ffn_w3"][0])
        w2 = io["ffn_w2"][0]
        add_product_stage(nc, m, "ffndown", hid, KF, lambda to, t: [(to, w2[:, bass.ds(t * P, P)].rearrange("(k p) c -> p k c", p=P))])
    with sbt("kT", [P, KV_T, KEYS], F32) as kT, sbt("v128", [P, VS, HKV * HD], F32) as v128, sbt("h_att", [P, KD, TOK], F32) as hT:
        norm_stage(nc, m, "norm2", [(hT, G_KV)])
        with sbt("vTt", [P, KV_T, TOK], F32) as vT:
            heads_stage(nc, m, "kv", hT, 2 * KV_T, KV_T,
                        lambda t: [(kT[:, t, WINDOW:K_CACHE], 0), (kT[:, t, K_SAMPLE:KEYS], PROMPT)] if t < KV_T else [(vT[:, t - KV_T, :], 0)],
                        lambda w: [[(w[:, 0, :, :], io["w_kv"].rearrange("(k p) c -> p k c", p=P))]], io)
            values_stage(nc, m, kT, vT, v128, io)
        norm_stage(nc, m, "norm3", [(hT, G_ATTN1)])
        with sbt("qT", [P, 8, TOK], F32) as qT:
            wq = io["swa_w_q"][0].rearrange("(k p) (jp b c) -> jp b p k c", p=P, jp=2, b=2)

            def q_loads(w):
                return [[(w[:, jp, k, :].rearrange("p (g b c) -> p g b c", b=2, c=HD)[:, :, b, :], wq[jp, b, :, k, :].rearrange("p (g c) -> p g c", c=HD))
                         for b in range(2) for k in range(KD)] for jp in range(2)]

            heads_stage(nc, m, "q", hT, 8, 8, lambda t: [(qT[:, t, :], 0)], q_loads, io)
            attend_stage(nc, m, qT, kT, v128, hT)
        wo = io["swa_w_o"][0].rearrange("(j g l d) c -> g d j l c", j=HKV, g=2, l=2)

        def o_load(to, t):
            tv = to.rearrange("p (j l) c -> p j l c", l=2)
            return [(tv[HD * g:HD * g + HD, :, l, :], wo[g, :, :, l, bass.ds(t * P, P)]) for g in range(2) for l in range(2)]

        add_product_stage(nc, m, "attout", hT, KD, o_load, parts=4)
    moe_stages(nc, m, io)


INPUTS = ["x_prompt", "x_sample", "cache_conv", "state_delta", "cache_k", "cache_v", "norm_attn", "norm_ffn", "gdn_w_in", "gdn_w_conv",
          "gdn_a_log", "gdn_dt_bias", "gdn_o_norm", "gdn_w_out", "kv_norm", "w_kv", "swa_w_q", "swa_sinks", "swa_w_o",
          "ffn_w1", "ffn_w3", "ffn_w2", "moe_router", "moe_w1", "moe_w3", "moe_w2", "final_norm"]
OUTPUTS = [("y_prompt", (1, PROMPT, D)), ("y_sample", (1, SAMPLE, D)), ("conv_p", (1, 1, HIST, CONV_CH)), ("delta_p", (1, 1, HV, DK, DV)),
           ("k_p", (1, WINDOW, HKV, HD)), ("v_p", (1, WINDOW, HKV, HD)), ("conv_s", (1, 1, HIST, CONV_CH)), ("delta_s", (1, 1, HV, DK, DV)),
           ("k_s", (1, SAMPLE, HKV, HD)), ("v_s", (1, SAMPLE, HKV, HD))]


def build(nc, io):
    with ExitStack() as keep:
        sb = lambda name, shape, dt=F32: keep.enter_context(nc.sbuf_tensor(name, shape, dt))
        m = {"const": sb("const", [P, CONST_W]), "gains": sb("gains", [P, N_GAINS]), "convw": sb("convw", [P, CONV_W, 32]),
             "hist": sb("hist", [P, HIST, 32]), "tail": sb("tail", [P, 2, HIST, 32]), "eps": sb("eps", [P, 1]),
             "gdn_a_log": sb("a_log", [P, HV]), "gdn_dt_bias": sb("dt_bias", [P, HV]), "swa_sinks": sb("sinks", [P, HQ]),
             "xT": sb("xT", [P, KD, TOK])}
        m["rows_dram"] = nc.dram_tensor("decay_rows", (2, HV, TOK), F32).ap()
        load_stage(nc, m, io)
        with nc.sbuf_tensor("cols", [P, NT, HV, N_COL], F32) as cols, nc.sbuf_tensor("hT", [P, KD, TOK], F32) as hT:
            m["cols"] = cols
            norm_stage(nc, m, "norm0", [(hT, G_ATTN0)])
            gates_stage(nc, m, hT, io)
            with nc.Fori(0, GROUPS) as g, nc.sbuf_tensor("vT", [P, GH, TOK], F32) as vT, nc.sbuf_tensor("zT", [P, GH, TOK], F32) as zT:
                m["vT"], m["zT"] = vT, zT
                with nc.sbuf_tensor("qk", [P, 2 * GK, TOK], F32) as qk:
                    m["qk"] = qk
                    project_stage(nc, m, hT, io, g)
                    delta_stage(nc, m, io, g)
                mix_out_stage(nc, m, io, g)
        tails_stage(nc, m, io)
        rest_stages(nc, m, io)


def kernel(**inputs):
    from concourse import bacc
    from concourse.bass_utils import run_bass_kernel_spmd

    nc = bacc.Bacc("TRN2", target_bir_lowering=False, num_devices=1)
    arrays = {f"in_{n}": np.ascontiguousarray(inputs[n]) for n in INPUTS}
    arrays["in_consts"], arrays["in_rope"] = constants(), rope_tables()
    io = {n[3:]: nc.dram_tensor(n, a.shape, mybir.dt.from_np(a.dtype), kind="ExternalInput").ap() for n, a in arrays.items()}
    for n, shape in OUTPUTS:
        io[n] = nc.dram_tensor(f"out_{n}", shape, F32, kind="ExternalOutput").ap()
    build(nc, io)
    r = run_bass_kernel_spmd(nc, [arrays], core_ids=[0])
    return tuple(r.results[0][f"out_{n}"] for n, _ in OUTPUTS)
```

```python
from contextlib import ExitStack

import numpy as np

import concourse.bass as bass
from concourse import mybir

F32 = mybir.dt.float32
I32 = mybir.dt.int32
U32 = mybir.dt.uint32
ACT = mybir.ActivationFunctionType
ALU = mybir.AluOpType
AX = mybir.AxisListType

P = 128
D = 1024
KD = D // P
PROMPT = 1024
SAMPLE = 64
TOK = PROMPT + SAMPLE
CHUNK = 64
TILES = [(s, min(P, TOK - s)) for s in range(0, TOK, P)]
NT = len(TILES)
BLK = [(0, 384), (384, 384), (768, 320)]
EPS = 1e-6

HK, HV, DK, DV = 8, 16, 128, 128
QK_DIM = HK * DK
V_DIM = HV * DV
CONV_CH = 2 * QK_DIM + V_DIM
CONV_W = 4
HIST = CONV_W - 1
PADW = HIST + PROMPT + HIST + SAMPLE
GROUPS = 4
GH = HV // GROUPS
GK = HK // GROUPS

HQ, HKV, HD = 16, 4, 64
WINDOW = 128
D_FF = 2816
KF = D_FF // P
NE = 8

G_ATTN0, G_ATTN1, G_FFN0, G_FFN1, G_KV, G_FINAL, G_ONORM = 0, 8, 16, 24, 32, 40, 48
N_GAINS = 49
LEVELS = (1, 2, 4, 8, 16, 32)
C_ID, C_ONES, C_INCL, C_LAST, C_ROT, C_STRICT, C_NID = 0, 1, 2, 3, 4, 5, 6
C_LVL = 7
N_CONST = C_LVL + len(LEVELS)
CONST_W = N_CONST * P + 16
K_GC, K_BETA, K_NGB, K_KDEC = 0, 1, 2, 3
N_COL = 4


def constants():
    j, i = np.indices((P, P))
    same = j // CHUNK == i // CHUNK
    c = np.zeros((N_CONST, P, P), np.float32)
    c[C_ID] = j == i
    c[C_ONES] = 1
    c[C_INCL] = same & (j <= i)
    c[C_LAST] = same & (j % CHUNK == CHUNK - 1)
    r, f = j % HD, i % HD
    half = HD // 8
    c[C_ROT] = (j // HD == i // HD) * ((f < half) * (r == f + half) * -1.0 + ((f >= half) & (f < 2 * half)) * (r == f - half))
    c[C_STRICT] = j < i
    c[C_NID] = j % CHUNK == i
    for n, s in enumerate(LEVELS):
        c[C_LVL + n] = (j // (2 * s) == i // (2 * s)) & (j % (2 * s) < s) & (i % (2 * s) >= s)
    tail = np.zeros((P, 16), np.float32)
    tail[:, 0:NE] = NE - np.arange(NE)
    tail[:, NE] = np.arange(P)
    return np.concatenate([c.transpose(1, 0, 2).reshape(P, N_CONST * P), tail], axis=1)


def rope_tables():
    half = HD // 8
    inv = np.power(np.float32(500000.0), -np.arange(half, dtype=np.float32) * np.float32(2.0) / np.float32(2 * half))
    pos = np.concatenate([np.arange(PROMPT), 1024 + np.arange(SAMPLE)]).astype(np.float32)
    ang = (pos[:, None] * inv.astype(np.float32)[None, :]).astype(np.float32)
    t = np.zeros((2, P, TOK), np.float32)
    t[0] = 1
    for h in range(2):
        for f in range(2 * half):
            t[0, h * HD + f] = np.cos(ang[:, f % half])
            t[1, h * HD + f] = np.sin(ang[:, f % half])
    return t


PRE = 1


class Stage:

    def __init__(self, nc, name):
        self.nc, self.name, self.sems, self.pre = nc, name, [], []

    def __enter__(self):
        self.stack = ExitStack()
        return self

    def sb(self, name, shape, dt=F32):
        return self.stack.enter_context(self.nc.sbuf_tensor(f"{self.name}_{name}", shape, dt))

    def ps(self, name, shape, dt=F32):
        return self.stack.enter_context(self.nc.psum_tensor(f"{self.name}_{name}", shape, dt))

    def sem(self, name, pre=True):
        s = self.stack.enter_context(self.nc.semaphore(f"{self.name}_{name}"))
        self.sems.append(s)
        if pre:
            self.pre.append(s)
        return s

    def block(self):
        for s in self.pre:
            self.nc.gpsimd.sem_inc(s, PRE)
        self.nc.all_engine_barrier()
        return self.nc.Block()

    def __exit__(self, *exc):
        if exc[0] is None:
            for s in self.sems:
                self.nc.gpsimd.sem_clear(s)
        self.stack.close()


class Chain:

    def __init__(self, eng, sem, base=0):
        self.eng, self.sem, self.base, self.n = eng, sem, base, 0

    def __call__(self, ins):
        self.n += 1
        ins.then_inc(self.sem, 1)
        self.eng.wait_ge(self.sem, PRE + self.base + self.n)


def hold(eng, passed):
    eng.sem_inc(passed, 1)


def load_stage(nc, m, io):
    with Stage(nc, "load") as st:
        rows = st.sb("rows", [N_GAINS, P])
        crow = st.sb("crow", [P, P])
        hrow = st.sb("hrow", [HIST * 32, P])
        xin = st.sb("xin", [P, 2, D])
        pt = st.ps("pt", [P, 2, 2, 512])
        pg = st.ps("pg", [P, 512])
        small, xl = st.sem("small_loaded"), [st.sem(f"frames_loaded{i}") for i in range(2)]
        turned, copied, gturn, mset = st.sem("tile_turned"), st.sem("tile_copied"), st.sem("gains_turned"), st.sem("eps_set")
        tiles_x = [io["x_prompt"][0, s:s + n, :] if s < PROMPT else io["x_sample"][0, :, :] for s, n in TILES]
        with st.block() as block:
            @block.sync
            def _(sp):
                sp.dma_start(m["const"][:, :], io["consts"]).then_inc(small, 16)
                for gain, at in (("norm_attn", G_ATTN0), ("norm_ffn", G_FFN0)):
                    sp.dma_start(rows[at:at + 16, :], io[gain].rearrange("l (k p) -> (l k) p", p=P)).then_inc(small, 16)
                for gain, at in (("kv_norm", G_KV), ("final_norm", G_FINAL)):
                    sp.dma_start(rows[at:at + 8, :], io[gain].rearrange("(k p) -> k p", p=P)).then_inc(small, 16)
                sp.dma_start(rows[G_ONORM:G_ONORM + 1, :], io["gdn_o_norm"]).then_inc(small, 16)
                sp.dma_start(crow[:, :], io["gdn_w_conv"][0].rearrange("j (t p) -> (j t) p", p=P)).then_inc(small, 16)
                sp.dma_start(hrow[:, :], io["cache_conv"][0, 0].rearrange("j (t p) -> (j t) p", p=P)).then_inc(small, 16)
                for name in ("gdn_a_log", "gdn_dt_bias", "swa_sinks"):
                    sp.dma_start(m[name][:, :], io[name].broadcast_to([P, 16])).then_inc(small, 16)
                for t, (s, n) in enumerate(TILES):
                    if t >= 2:
                        sp.wait_ge(turned, PRE + 2 * (t - 1))
                    sp.dma_start(xin[0:n, t % 2, :], tiles_x[t]).then_inc(xl[t % 2], 16)

            @block.tensor
            def _(pe):
                pe.wait_ge(small, PRE + 16 * 11)
                ident = m["const"][:, 0:P]
                pe.transpose(pg[:, 0:N_GAINS], rows[:, :], ident[0:N_GAINS, 0:N_GAINS])
                pe.transpose(pg[:, 64:64 + P], crow[:, :], ident)
                pe.transpose(pg[:, 192:192 + HIST * 32], hrow[:, :], ident[0:96, 0:96]).then_inc(gturn, 1)
                for t, (s, n) in enumerate(TILES):
                    pe.wait_ge(xl[t % 2], PRE + 16 * (t // 2 + 1))
                    for h in range(2):
                        if t >= 1:
                            pe.wait_ge(copied, PRE + 2 * (t - 1) + h + 1)
                        for k in range(4):
                            last = pe.transpose(pt[:, h, 0, k * P:k * P + n], xin[0:n, t % 2, (4 * h + k) * P:(4 * h + k + 1) * P], ident[0:n, 0:n])
                        last.then_inc(turned, 1)

            @block.vector
            def _(dve):
                dve.memset(m["eps"][:, :], EPS).then_inc(mset, 1)
                dve.wait_ge(gturn, PRE + 1)
                dve.tensor_copy(m["gains"][:, :], pg[:, 0:N_GAINS])
                dve.tensor_copy(m["convw"][:, :, :], pg[:, 64:64 + P].rearrange("p (j t) -> p j t", j=4))
                dve.tensor_copy(m["hist"][:, :, :], pg[:, 192:192 + 96].rearrange("p (j t) -> p j t", j=3))
                for t, (s, n) in enumerate(TILES):
                    for h in range(2):
                        dve.wait_ge(turned, PRE + 2 * t + h + 1)
                        dve.tensor_copy(m["xT"][:, 4 * h:4 * h + 4, s:s + n], pt[:, h, 0, :].rearrange("p (k c) -> p k c", c=P)[:, :, 0:n]).then_inc(copied, 1)


def norm_stage(nc, m, name, outs):
    with Stage(nc, name) as st:
        sq = st.sb("sq", [P, 2, TOK])
        root = st.sb("root", [P, TOK])
        rinv = st.sb("rinv", [P, TOK])
        acc = st.ps("acc", [P, 3, 512])
        squared, summed, rooted, inverted = (st.sem(s) for s in ("squared", "summed", "rooted", "inverted"))
        with st.block() as block:
            @block.scalar
            def _(act):
                for k in range(KD):
                    if k >= 2:
                        act.wait_ge(summed, PRE + k - 1)
                    act.activation(sq[:, k % 2, :], m["xT"][:, k, :], ACT.Square).then_inc(squared, 1)
                act.wait_ge(summed, PRE + KD)
                for b, (s, n) in enumerate(BLK):
                    act.activation(root[:, s:s + n], acc[:, b, 0:n], ACT.Sqrt, bias=m["eps"][:, :], scale=1.0 / D).then_inc(rooted, 1)

            @block.tensor
            def _(pe):
                for k in range(KD):
                    pe.wait_ge(squared, PRE + k + 1)
                    for b, (s, n) in enumerate(BLK):
                        last = pe.matmul(acc[:, b, 0:n], m["const"][:, C_ONES * P:(C_ONES + 1) * P], sq[:, k % 2, s:s + n],
                                         start=(k == 0), stop=(k == KD - 1))
                    last.then_inc(summed, 1)

            @block.vector
            def _(dve):
                for b, (s, n) in enumerate(BLK):
                    dve.wait_ge(rooted, PRE + b + 1)
                    dve.reciprocal(rinv[:, s:s + n], root[:, s:s + n]).then_inc(inverted, 1)
                dve.wait_ge(inverted, PRE + len(BLK))
                for out, gain in outs:
                    for k in range(KD):
                        dve.scalar_tensor_tensor(out=out[:, k, :], in0=m["xT"][:, k, :], scalar=m["gains"][:, gain + k:gain + k + 1],
                                                 in1=rinv[:, :], op0=ALU.mult, op1=ALU.mult)


def gates_stage(nc, m, hT, io):
    NB = NT * HV
    with Stage(nc, "gates") as st:
        wba = st.sb("wba", [P, KD, 2 * HV])
        ba = st.sb("ba", [P, NT, 2, HV])
        beta, xa, t0, t1, g, gc = (st.sb(n, [P, NT, HV]) for n in ("beta", "xa", "t0", "t1", "g", "gc"))
        ea = st.sb("ea", [P, HV])
        rows = st.sb("rows", [HV, 2, TOK])
        pba = st.ps("pba", [P, NT, 2, HV])
        pgc, pgl = st.ps("pgc", [P, NT, HV]), st.ps("pgl", [P, NT, HV])
        prow = st.ps("prow", [HV, 3, 512])
        w_loaded, proj, dv, av = (st.sem(s) for s in ("w_loaded", "projected", "vector", "scalar"))
        cum, turned, emptied, stored, own = (st.sem(s) for s in ("cumulated", "turned", "emptied", "stored", "vector_own"))
        cst = lambda n: m["const"][:, n * P:(n + 1) * P]
        with st.block() as block:
            @block.sync
            def _(sp):
                sp.dma_start(wba[:, :, :], io["gdn_w_in"][0][:, CONV_CH + V_DIM:].rearrange("(k p) c -> p k c", p=P)).then_inc(w_loaded, 16)
                sp.wait_ge(emptied, PRE + 6)
                sp.dma_start(m["rows_dram"].rearrange("a h t -> h a t"), rows[:, :, :]).then_inc(stored, 16)
                sp.wait_ge(stored, PRE + 16)

            @block.tensor
            def _(pe):
                pe.wait_ge(w_loaded, PRE + 16)
                for t, (s, n) in enumerate(TILES):
                    for k in range(KD):
                        last = pe.matmul(pba[0:n, t, :, :], hT[:, k, s:s + n], wba[:, k, :], start=(k == 0), stop=(k == KD - 1))
                last.then_inc(proj, 1)
                pe.wait_ge(dv, PRE + 6)
                pe.matmul(pgc[:, :, :], cst(C_INCL), g[:, :, :], start=True, stop=True).then_inc(cum, 1)
                pe.wait_ge(dv, PRE + 7)
                pe.matmul(pgl[:, :, :], cst(C_LAST), gc[:, :, :], start=True, stop=True).then_inc(cum, 1)
                for a, src in enumerate((gc, beta)):
                    for b in range(3):
                        if a:
                            pe.wait_ge(emptied, PRE + b + 1)
                        for t in range(3 * b, 3 * b + 3):
                            s, n = TILES[t]
                            last = pe.transpose(prow[:, b, (t % 3) * P:(t % 3) * P + n], src[0:n, t, :], cst(C_ID)[0:n, 0:n])
                        last.then_inc(turned, 1)

            @block.scalar
            def _(act):
                acts = Chain(act, av)
                act.activation(ea[:, :], m["gdn_a_log"][:, :], ACT.Exp)
                act.wait_ge(dv, PRE + 1)
                acts(act.activation(beta[:, :, :], ba[:, :, 0, :], ACT.Exp, scale=-1.0))
                act.wait_ge(dv, PRE + 3)
                acts(act.activation(t0[:, :, :], t0[:, :, :], ACT.Exp, scale=-1.0))
                acts(act.activation(t0[:, :, :], t0[:, :, :], ACT.Ln, bias=1.0))
                act.wait_ge(dv, PRE + 8)
                acts(act.activation(m["cols"][:, :, :, K_KDEC], t1[:, :, :], ACT.Exp))
                acts(act.activation(t0[:, :, :], gc[:, :, :], ACT.Exp))

            @block.vector
            def _(dve):
                v = Chain(dve, dv)
                w = Chain(dve, own)
                w(dve.memset(ba[:, :, :, :], 0.0))
                dve.wait_ge(proj, PRE + 1)
                dve.tensor_copy(ba[:, 0:NT - 1, :, :], pba[:, 0:NT - 1, :, :])
                v(dve.tensor_copy(ba[0:64, NT - 1, :, :], pba[0:64, NT - 1, :, :]))
                v(dve.tensor_tensor(xa[:, :, :], ba[:, :, 1, :], m["gdn_dt_bias"][:, :].unsqueeze(1).broadcast_to([P, NT, HV]), ALU.add))
                w(dve.tensor_scalar(t1[:, :, :], xa[:, :, :], -1.0, None, ALU.mult))
                v(dve.tensor_tensor(t0[:, :, :], xa[:, :, :], t1[:, :, :], ALU.max))
                dve.wait_ge(av, PRE + 1)
                w(dve.tensor_scalar(beta[:, :, :], beta[:, :, :], 1.0, None, ALU.add))
                v(dve.reciprocal(beta[:, :, :], beta[:, :, :]))
                dve.wait_ge(av, PRE + 3)
                v(dve.scalar_tensor_tensor(out=t1[:, :, :], in0=xa[:, :, :], scalar=0.0, in1=t0[:, :, :], op0=ALU.max, op1=ALU.add))
                v(dve.scalar_tensor_tensor(out=g[:, :, :], in0=t1[:, :, :], scalar=-1.0, in1=ea[:, :].unsqueeze(1).broadcast_to([P, NT, HV]), op0=ALU.mult, op1=ALU.mult))
                dve.wait_ge(cum, PRE + 1)
                v(dve.tensor_copy(gc[:, :, :], pgc[:, :, :]))
                dve.wait_ge(cum, PRE + 2)
                v(dve.tensor_tensor(t1[:, :, :], pgl[:, :, :], gc[:, :, :], ALU.subtract))
                dve.tensor_copy(m["cols"][:, :, :, K_GC], gc[:, :, :])
                dve.tensor_copy(m["cols"][:, :, :, K_BETA], beta[:, :, :])
                dve.wait_ge(av, PRE + 5)
                dve.scalar_tensor_tensor(out=m["cols"][:, :, :, K_NGB], in0=t0[:, :, :], scalar=-1.0, in1=beta[:, :, :], op0=ALU.mult, op1=ALU.mult)
                for a in range(2):
                    for b in range(3):
                        dve.wait_ge(turned, PRE + 3 * a + b + 1)
                        s, n = BLK[b]
                        dve.tensor_copy(rows[:, a, s:s + n], prow[:, b, 0:n]).then_inc(emptied, 1)


def project_stage(nc, m, hT, io):
    NC, NQK = CONV_CH // P, 2 * HK
    N = NC + HV
    PW = PADW - HIST
    with Stage(nc, "proj") as st:
        w = st.sb("w", [P, 2, KD, P])
        xpad, acc = st.sb("xpad", [P, 2, PADW]), st.sb("acc", [P, 2, PADW])
        out, sq, root = st.sb("out", [P, 2, TOK]), st.sb("sq", [P, 2, TOK]), st.sb("root", [P, 2, TOK])
        cw = st.sb("cw", [P, 2, CONV_W])
        pm = st.ps("pm", [P, 2, 3, 512])
        pn = st.ps("pn", [P, 2, 512])
        two = lambda n: [st.sem(f"{n}{u}") for u in range(2)]
        w_loaded, done, emptied, conved, silued, kept, hist_set, squared, inverted, united, stored = (two(n) for n in (
            "w_loaded", "tile_summed", "tile_emptied", "convolved", "silued", "tails_kept", "hist_set", "squared", "inverted", "united", "stored"))
        zeroed, nsummed, rooted, own = (st.sem(n) for n in ("pad_zeroed", "norms_summed", "rooted", "vector_step"))
        dram = m["proj_dram"]
        with st.block() as block:
            @block.sync
            def _(sp):
                def load(t, u):
                    sp.dma_start(w[:, u, :, :], io["gdn_w_in"][0][:, bass.ds(t * P, P)].rearrange("(k p) c -> p k c", p=P)).then_inc(w_loaded[u], 16)

                def store(i, u, ready):
                    sp.wait_ge(ready[u], PRE + i + 1)
                    sp.dma_start(dram[bass.ds(2 * i + u, 1)].rearrange("o p t -> p (o t)"), out[:, u, :]).then_inc(stored[u], 16)

                def steps(i, ready):
                    for u in range(2):
                        sp.wait_ge(done[u], PRE + i + 1)
                        load(2 * i + 2 + u, u)
                        store(i, u, ready)

                load(0, 0)
                load(1, 1)
                with sp.Fori(0, NQK // 2) as i:
                    steps(i, united)
                with sp.Fori(NQK // 2, N // 2 - 1) as i:
                    steps(i, silued)
                for u in range(2):
                    store(N // 2 - 1, u, silued)
                    sp.wait_ge(stored[u], PRE + 16 * (N // 2))

            @block.tensor
            def _(pe):
                def product(i, u):
                    pe.wait_ge(w_loaded[u], PRE + 16 * (i + 1))
                    pe.wait_ge(emptied[u], PRE + i)
                    for k in range(KD):
                        for b, (c, n) in enumerate(BLK):
                            last = pe.matmul(pm[:, u, b, 0:n], w[:, u, k, :], hT[:, k, c:c + n], start=(k == 0), stop=(k == KD - 1))
                    last.then_inc(done[u], 1)

                def norms(i, u):
                    pe.wait_ge(squared[u], PRE + i + 1)
                    for b, (c, n) in enumerate(BLK):
                        pe.wait_ge(rooted, PRE + 6 * i + 3 * u + max(b - 1, 0))
                        pe.matmul(pn[:, (3 * u + b) % 2, 0:n], m["const"][:, C_ONES * P:(C_ONES + 1) * P], sq[:, u, c:c + n],
                                  start=True, stop=True).then_inc(nsummed, 1)

                product(0, 0)
                product(0, 1)
                norms(0, 0)
                with pe.Fori(1, NQK // 2) as i:
                    product(i, 0)
                    norms(i - 1, 1)
                    product(i, 1)
                    norms(i, 0)
                product(NQK // 2, 0)
                norms(NQK // 2 - 1, 1)
                product(NQK // 2, 1)
                with pe.Fori(NQK // 2 + 1, N // 2) as i:
                    for u in range(2):
                        product(i, u)

            @block.gpsimd
            def _(pool):
                def history(i, u):
                    t = 2 * i + u
                    pool.wait_ge(conved[u], PRE + i)
                    pool.tensor_copy(xpad[:, u, HIST + PROMPT:HIST + PROMPT + HIST], m["hist"][:, :, bass.ds(t, 1)].rearrange("p j o -> p (j o)"))
                    pool.tensor_copy(cw[:, u, :], m["convw"][:, :, bass.ds(t, 1)].rearrange("p j o -> p (j o)")).then_inc(hist_set[u], 1)
                    pool.wait_ge(emptied[u], PRE + i + 1)
                    pool.tensor_copy(m["tail"][:, 0, :, bass.ds(t, 1)].rearrange("p j o -> p (j o)"), xpad[:, u, PROMPT:PROMPT + HIST])
                    pool.tensor_copy(m["tail"][:, 1, :, bass.ds(t, 1)].rearrange("p j o -> p (j o)"), xpad[:, u, PADW - HIST:PADW]).then_inc(kept[u], 1)

                pool.memset(xpad[:, :, 0:HIST], 0.0).then_inc(zeroed, 1)
                with pool.Fori(0, NC // 2) as i:
                    for u in range(2):
                        history(i, u)

            @block.scalar
            def _(act):
                def empty(i, u):
                    act.wait_ge(done[u], PRE + i + 1)
                    act.wait_ge(conved[u], PRE + i)
                    act.wait_ge(kept[u], PRE + i)
                    act.activation(xpad[:, u, HIST:HIST + 768].rearrange("p (b c) -> p b c", b=2), pm[:, u, 0:2, 0:384], ACT.Copy)
                    act.activation(xpad[:, u, HIST + 768:HIST + PROMPT], pm[:, u, 2, 0:256], ACT.Copy)
                    act.activation(xpad[:, u, PADW - SAMPLE:PADW], pm[:, u, 2, 256:320], ACT.Copy).then_inc(emptied[u], 1)

                def silu(i, u):
                    act.wait_ge(conved[u], PRE + i + 1)
                    act.wait_ge(stored[u], PRE + 16 * i)
                    act.activation(out[:, u, 0:PROMPT], acc[:, u, 0:PROMPT], ACT.Silu)
                    act.activation(out[:, u, PROMPT:TOK], acc[:, u, PROMPT + HIST:PW], ACT.Silu).then_inc(silued[u], 1)

                def square(i, u):
                    act.wait_ge(silued[u], PRE + i + 1)
                    act.activation(sq[:, u, :], out[:, u, :], ACT.Square).then_inc(squared[u], 1)

                def roots(i, u):
                    if isinstance(i, int) and i == 0:
                        pass
                    else:
                        act.wait_ge(united[u], PRE + i)
                    for b, (c, n) in enumerate(BLK):
                        act.wait_ge(nsummed, PRE + 6 * i + 3 * u + b + 1)
                        act.activation(root[:, u, c:c + n], pn[:, (3 * u + b) % 2, 0:n], ACT.Sqrt, bias=m["eps"][:, :]).then_inc(rooted, 1)

                def gate(i, u):
                    act.wait_ge(done[u], PRE + i + 1)
                    act.wait_ge(stored[u], PRE + 16 * i)
                    act.activation(out[:, u, 0:768].rearrange("p (b c) -> p b c", b=2), pm[:, u, 0:2, 0:384], ACT.Silu)
                    act.activation(out[:, u, 768:TOK], pm[:, u, 2, 0:320], ACT.Silu).then_inc(emptied[u], 1)
                    act.wait_ge(emptied[u], PRE + i + 1)
                    act.sem_inc(silued[u], 1)

                empty(0, 0)
                silu(0, 0)
                square(0, 0)
                empty(0, 1)
                roots(0, 0)
                silu(0, 1)
                square(0, 1)
                with act.Fori(1, NQK // 2) as i:
                    empty(i, 0)
                    roots(i - 1, 1)
                    silu(i, 0)
                    square(i, 0)
                    empty(i, 1)
                    roots(i, 0)
                    silu(i, 1)
                    square(i, 1)
                empty(NQK // 2, 0)
                roots(NQK // 2 - 1, 1)
                silu(NQK // 2, 0)
                empty(NQK // 2, 1)
                silu(NQK // 2, 1)
                with act.Fori(NQK // 2 + 1, NC // 2) as i:
                    for u in range(2):
                        empty(i, u)
                        silu(i, u)
                with act.Fori(NC // 2, N // 2) as i:
                    for u in range(2):
                        gate(i, u)

            @block.vector
            def _(dve):
                def conv(i, u):
                    v = Chain(dve, own, 3 * (2 * i + u))
                    dve.wait_ge(emptied[u], PRE + i + 1)
                    dve.wait_ge(hist_set[u], PRE + i + 1)
                    dve.wait_ge(silued[u], PRE + i)
                    v(dve.tensor_scalar(acc[:, u, 0:PW], xpad[:, u, 0:PW], cw[:, u, 0:1], None, ALU.mult))
                    for j in range(1, CONV_W):
                        op = dve.scalar_tensor_tensor(out=acc[:, u, 0:PW], in0=xpad[:, u, j:j + PW], scalar=cw[:, u, j:j + 1],
                                                      in1=acc[:, u, 0:PW], op0=ALU.mult, op1=ALU.add)
                        if j < CONV_W - 1:
                            v(op)
                    op.then_inc(conved[u], 1)

                def unit(i, u, scale):
                    dve.wait_ge(rooted, PRE + 6 * i + 3 * u + 3)
                    dve.reciprocal(root[:, u, :], root[:, u, :]).then_inc(inverted[u], 1)
                    dve.wait_ge(inverted[u], PRE + i + 1)
                    dve.scalar_tensor_tensor(out=out[:, u, :], in0=out[:, u, :], scalar=scale, in1=root[:, u, :], op0=ALU.mult, op1=ALU.mult).then_inc(united[u], 1)

                Q, K = DK ** -0.5, 1.0
                dve.wait_ge(zeroed, PRE + 1)
                conv(0, 0)
                conv(0, 1)
                unit(0, 0, Q)
                with dve.Fori(1, HK // 2) as i:
                    conv(i, 0)
                    unit(i - 1, 1, Q)
                    conv(i, 1)
                    unit(i, 0, Q)
                conv(HK // 2, 0)
                unit(HK // 2 - 1, 1, Q)
                conv(HK // 2, 1)
                unit(HK // 2, 0, K)
                with dve.Fori(HK // 2 + 1, HK) as i:
                    conv(i, 0)
                    unit(i - 1, 1, K)
                    conv(i, 1)
                    unit(i, 0, K)
                conv(HK, 0)
                unit(HK - 1, 1, K)
                conv(HK, 1)
                with dve.Fori(HK + 1, NC // 2) as i:
                    for u in range(2):
                        conv(i, u)


ORDER = ("stage", "R0", "scores", "R1", "level0", "x1", "R2", "d1", "x2", "R3", "d2", "x3", "R4", "d3", "x4", "R5", "d4", "x5", "d5")
CHAINS = 2


def in_order(steps, rec, prep):
    for what in ORDER:
        for ch in range(CHAINS):
            if what[0] == "R":
                c, part = divmod(int(what[1]), 3)
                if rec is not None and c * CHUNK < rec[2]:
                    steps[f"R{part}"](ch, rec[0], rec[1], c)
            elif prep is not None:
                t, par, n = prep
                if what[0] in "xd":
                    steps[what[0]](ch, t, par, n, int(what[1]))
                else:
                    steps[what](ch, t, par, n)


def delta_tiles(eng, steps):
    in_order(steps, None, (0, 0, P))
    with eng.Fori(0, NT // 2 - 1) as i:
        for u in range(2):
            in_order(steps, (2 * i + u, u, P), (2 * i + u + 1, 1 - u, P))
    in_order(steps, (NT - 3, 0, P), (NT - 2, 1, P))
    in_order(steps, (NT - 2, 1, P), (NT - 1, 0, SAMPLE))
    in_order(steps, (NT - 1, 0, SAMPLE), None)


def delta_stage(nc, m, io, pas):
    proj = m["proj_dram"]
    with Stage(nc, "delta") as st:
        C = range(CHAINS)
        each = lambda n, shape: [st.sb(f"{n}{ch}", shape) for ch in C]
        gb = each("gb", [P, 2, 2, GH, P])
        kst, qst, vst = each("kst", [P, 2, GK, P]), each("qst", [P, 2, GK, P]), each("vst", [P, 2, GH, P])
        cst, egl = each("cst", [P, 2, GH, N_COL]), each("egl", [P, 2, GH, 2])
        attn, qg, kd, vb, TT, out = (each(n, [P, 2, GH, P]) for n in ("attn", "qg", "kd", "vb", "TT", "out"))
        dec, at, eg, X, rhs, vn = (each(n, [P, GH, P]) for n in ("dec", "at", "eg", "X", "rhs", "vn"))
        Tn, Xn = (each(n, [P, GH, CHUNK]) for n in ("Tn", "Xn"))
        TTn = each("TTn", [P, 2, GH, CHUNK])
        BT = each("BT", [P, 2, GH, P])
        S = each("S", [P, 2, GH, DV])
        b_x, b_d, b_w, b_s = ([st.ps(f"{n}{ch}", [P, GH, P]) for ch in C] for n in ("bank_x", "bank_d", "bank_w", "bank_s"))
        names = ("rows_loaded0", "rows_loaded1", "qkv_loaded0", "qkv_loaded1", "state_set", "cols_staged", "v_turned", "k_turned", "scored",
                 "diffs", "dexp", "eg_ready", "masked", "at_half", "attn_ready", "at_ready", "qg_ready", "vb_ready", "kd_ready", "lvl_masked", "x_summed",
                 "x_copied", "deltas", "t_new", "ks_summed", "rhs_ready", "vn_summed", "vn_copied", "o_summed", "s_summed", "o_copied", "s_new",
                 "state_stored", "state_loaded", "out_stored0", "out_stored1")
        sems = [{n: st.sem(f"{n}_{ch}") for n in names} for ch in C]
        passed = st.sem("passed")
        cst_sq = lambda n, r: m["const"][0:r, n * P:n * P + r]
        narrow_id = lambda q: m["const"][q, C_NID * P:C_NID * P + CHUNK]
        over_heads = lambda a: a.unsqueeze(1).broadcast_to([a.shape[0], GH, a.shape[1]])
        group = lambda ch: 2 * pas + ch
        L = len(LEVELS)
        last_t = NT - 1
        quads = lambda n: [slice(r, r + CHUNK) for r in range(0, n, CHUNK)]
        is_first = lambda t: isinstance(t, int) and t == 0
        skip = lambda *a: None
        with st.block() as block:
            @block.sync
            def _(sp):
                def load(t, par, n):
                    for ch in C:
                        e, g = sems[ch], group(ch)
                        for dst, first, count in ((kst, HK + GK * g, GK), (qst, GK * g, GK), (vst, 2 * HK + GH * g, GH)):
                            sp.dma_start(dst[ch][:, par, :, 0:n], proj[bass.ds(first, count), :, bass.ds(t * P, n)].rearrange("h p t -> p h t")).then_inc(e[f"qkv_loaded{par}"], 16)
                        for a in range(2):
                            sp.dma_start(gb[ch][:, par, a, :, 0:n], m["rows_dram"][a, bass.ds(GH * g, GH), bass.ds(t * P, n)].unsqueeze(0)
                                         .broadcast_to([P, GH, n])).then_inc(e[f"rows_loaded{par}"], 16)

                def next_load(t, par, n):
                    for ch in C:
                        e = sems[ch]
                        sp.wait_ge(e["at_ready"], PRE + t - 1)
                        sp.wait_ge(e["eg_ready"], PRE + t - 1)
                        sp.wait_ge(e["o_summed"], PRE + 2 * (t - 1))
                    load(t, par, n)

                load(0, 0, P)
                load(1, 1, P)
                with sp.Fori(1, NT // 2) as i:
                    for u in range(2):
                        next_load(2 * i + u, u, P)
                next_load(last_t, 0, SAMPLE)
                for ch in C:
                    e, heads = sems[ch], bass.ds(GH * group(ch), GH)
                    sp.wait_ge(e["s_new"], PRE + 2 * last_t)
                    sp.dma_start(io["delta_p"][0, 0, heads].rearrange("h k v -> k h v"), S[ch][:, 0, :, :]).then_inc(e["state_stored"], 16)
                for ch in C:
                    e, heads = sems[ch], bass.ds(GH * group(ch), GH)
                    sp.wait_ge(e["state_stored"], PRE + 16)
                    sp.dma_start(S[ch][:, 0, :, :], io["state_delta"][0, 0, heads].rearrange("h k v -> k h v")).then_inc(e["state_loaded"], 16)
                for ch in C:
                    e, heads = sems[ch], bass.ds(GH * group(ch), GH)
                    sp.wait_ge(e["s_new"], PRE + 2 * last_t + 1)
                    sp.dma_start(io["delta_s"][0, 0, heads].rearrange("h k v -> k h v"), S[ch][:, 1, :, :]).then_inc(e["state_stored"], 16)
                for ch in C:
                    sp.wait_ge(sems[ch]["state_stored"], PRE + 32)

            @block.gpsimd
            def _(pool):
                def stage(ch, t, par, n):
                    e = sems[ch]
                    if not is_first(t):
                        pool.wait_ge(e["s_summed"], PRE + 2 * (t - 1))
                    pool.tensor_copy(cst[ch][:, par, :, :], m["cols"][:, bass.ds(t, 1), bass.ds(GH * group(ch), GH), :].rearrange("p o h c -> p (o h) c")).then_inc(e["cols_staged"], 1)

                def masks(ch, t, par, n, l):
                    e = sems[ch]
                    if l == 0:
                        pool.wait_ge(e["at_ready"], PRE + t + 1)
                    else:
                        pool.wait_ge(e["t_new"], PRE + t * L + l - 1)
                    pool.tensor_tensor(BT[ch][0:n, l % 2, :, 0:n], at[ch][0:n, :, 0:n], over_heads(cst_sq(C_LVL + l, n)), ALU.mult).then_inc(e["lvl_masked"], 1)

                def level0(ch, t, par, n):
                    masks(ch, t, par, n, 0)
                    masks(ch, t, par, n, 1)

                def x(ch, t, par, n, l):
                    if l + 1 < L:
                        masks(ch, t, par, n, l + 1)

                for ch in C:
                    pool.memset(S[ch][:, 0, :, :], 0.0)
                    pool.memset(X[ch][:, :, :], 0.0).then_inc(sems[ch]["state_set"], 1)
                delta_tiles(pool, {"stage": stage, "scores": skip, "level0": level0, "x": x, "d": skip, "R0": skip, "R1": skip, "R2": skip})

            @block.tensor
            def _(pe):
                ident = m["const"][:, 0:P]

                def stage(ch, t, par, n):
                    e = sems[ch]
                    pe.wait_ge(e["t_new"], PRE + t * L)
                    pe.wait_ge(e[f"qkv_loaded{par}"], PRE + 24 * t + 48 - 24 * par)
                    for h in range(GH):
                        last = pe.transpose(b_d[ch][0:n, h, :], vst[ch][:, par, h, 0:n], ident)
                    last.then_inc(e["v_turned"], 1)
                    for k in range(GK):
                        pe.matmul(b_x[ch][0:n, k, 0:n], kst[ch][:, par, k, 0:n], kst[ch][:, par, k, 0:n], start=True, stop=True)
                    for k in range(GK):
                        last = pe.matmul(b_x[ch][0:n, GK + k, 0:n], kst[ch][:, par, k, 0:n], qst[ch][:, par, k, 0:n], start=True, stop=True)
                    last.then_inc(e["scored"], 1)

                def scores(ch, t, par, n):
                    e = sems[ch]
                    pe.wait_ge(e["vb_ready"], PRE + t + 1)
                    for k in range(GK):
                        last = pe.transpose(b_d[ch][0:n, k, :], kst[ch][:, par, k, 0:n], ident)
                    last.then_inc(e["k_turned"], 1)

                def level0(ch, t, par, n):
                    e = sems[ch]
                    pe.wait_ge(e["attn_ready"], PRE + t + 1)
                    pe.wait_ge(e["lvl_masked"], PRE + t * L + 1)
                    for h in range(GH):
                        last = pe.matmul(b_x[ch][0:n, h, 0:CHUNK], BT[ch][0:n, 0, h, 0:n], narrow_id(slice(0, n)), start=True, stop=True)
                    last.then_inc(e["x_summed"], 1)

                def x(ch, t, par, n, l):
                    e = sems[ch]
                    pe.wait_ge(e["lvl_masked"], PRE + t * L + l + 1)
                    pe.wait_ge(e["t_new"], PRE + t * L + l)
                    for h in range(GH):
                        last = pe.matmul(b_x[ch][0:n, h, 0:CHUNK], BT[ch][0:n, l % 2, h, 0:n], Tn[ch][0:n, h, :], start=True, stop=True)
                    last.then_inc(e["x_summed"], 1)

                def d(ch, t, par, n, l):
                    e = sems[ch]
                    if l == 1:
                        pe.wait_ge(e["kd_ready"], PRE + t + 1)
                    pe.wait_ge(e["x_copied"], PRE + t * (L - 1) + l)
                    for h in range(GH):
                        if l < L - 1:
                            pe.matmul(b_d[ch][0:n, h, 0:CHUNK], TT[ch][0:n, par, h, 0:n], Xn[ch][0:n, h, :], start=True, stop=True)
                        last = pe.matmul(b_d[ch][0:n, h, CHUNK:P], X[ch][0:n, h, 0:n], TTn[ch][0:n, (l - 1) % 2, h, :], start=True, stop=True)
                    last.then_inc(e["deltas"], 1)

                def k_state(ch, t, par, c):
                    e, r = sems[ch], c * CHUNK
                    if isinstance(t, int) and t == last_t:
                        pe.wait_ge(e["state_loaded"], PRE + 16)
                    pe.wait_ge(e["s_new"], PRE + 2 * t + c)
                    pe.wait_ge(e["vn_copied"], PRE + 2 * t + c)
                    for h in range(GH):
                        last = pe.matmul(b_w[ch][r:r + CHUNK, h, :], kst[ch][:, par, h // 2, r:r + CHUNK], S[ch][:, c, h, :], start=True, stop=True)
                    last.then_inc(e["ks_summed"], 1)

                def v_new(ch, t, par, c):
                    e, r = sems[ch], c * CHUNK
                    pe.wait_ge(e["t_new"], PRE + (t + 1) * L)
                    pe.wait_ge(e["rhs_ready"], PRE + 2 * t + c + 1)
                    hold(pe, passed)
                    for h in range(GH):
                        last = pe.matmul(b_w[ch][r:r + CHUNK, h, :], TT[ch][r:r + CHUNK, par, h, r:r + CHUNK], rhs[ch][r:r + CHUNK, h, :], start=True, stop=True)
                    last.then_inc(e["vn_summed"], 1)

                def out_and_state(ch, t, par, c):
                    e, r = sems[ch], c * CHUNK
                    pe.wait_ge(e["qg_ready"], PRE + t + 1)
                    pe.wait_ge(e["o_copied"], PRE + 2 * t + c)
                    pe.wait_ge(e["vn_copied"], PRE + 2 * t + c + 1)
                    for h in range(GH):
                        last = pe.matmul(b_s[ch][:, h, :], kd[ch][r:r + CHUNK, par, h, :], vn[ch][r:r + CHUNK, h, :], start=True, stop=True)
                    last.then_inc(e["s_summed"], 1)
                    if ch == CHAINS - 1:
                        for other in C:
                            outputs(other, t, par, c)

                def outputs(ch, t, par, c):
                    e, r = sems[ch], c * CHUNK
                    pe.wait_ge(e["s_new"], PRE + 2 * t + c + 1)
                    for h in range(GH):
                        pe.matmul(b_s[ch][:, h, 0:CHUNK], S[ch][:, c, h, :], qg[ch][:, par, h, r:r + CHUNK], start=True, stop=False)
                        last = pe.matmul(b_s[ch][:, h, 0:CHUNK], vn[ch][r:r + CHUNK, h, :], attn[ch][r:r + CHUNK, par, h, r:r + CHUNK], start=False, stop=True)
                    last.then_inc(e["o_summed"], 1)

                for ch in C:
                    pe.wait_ge(sems[ch]["state_set"], PRE + 1)
                delta_tiles(pe, {"stage": stage, "scores": scores, "level0": level0, "x": x, "d": d, "R0": k_state, "R1": v_new, "R2": out_and_state})

            @block.scalar
            def _(act):
                def stage(ch, t, par, n):
                    e = sems[ch]
                    if not is_first(t):
                        act.wait_ge(e["s_new"], PRE + 2 * (t - 1))
                    act.wait_ge(e[f"rows_loaded{par}"], PRE + 16 * t + 32 - 16 * par)
                    for c in range(n // CHUNK):
                        act.activation(egl[ch][:, par, :, c:c + 1], gb[ch][:, par, 0, :, (c + 1) * CHUNK - 1:(c + 1) * CHUNK], ACT.Exp)
                    act.wait_ge(e["qg_ready"], PRE + t)
                    act.activation(eg[ch][:, :, 0:n], gb[ch][:, par, 0, :, 0:n], ACT.Exp).then_inc(e["eg_ready"], 1)
                    act.wait_ge(e["diffs"], PRE + t + 1)
                    act.activation(dec[ch][0:n, :, 0:n], dec[ch][0:n, :, 0:n], ACT.Exp).then_inc(e["dexp"], 1)

                def scores(ch, t, par, n):
                    e = sems[ch]
                    if not is_first(t):
                        act.wait_ge(e["s_summed"], PRE + 2 * (t - 1))
                    act.wait_ge(e["v_turned"], PRE + t + 1)
                    act.wait_ge(e["cols_staged"], PRE + t + 1)
                    for h in range(GH):
                        last = act.activation(vb[ch][0:n, par, h, :], b_d[ch][0:n, h, :], ACT.Copy, scale=cst[ch][0:n, par, h, K_BETA:K_BETA + 1])
                    last.then_inc(e["vb_ready"], 1)

                def level0(ch, t, par, n):
                    e = sems[ch]
                    act.wait_ge(e["k_turned"], PRE + t + 1)
                    for h in range(GH):
                        last = act.activation(kd[ch][0:n, par, h, :], b_d[ch][0:n, h // 2, :], ACT.Copy, scale=cst[ch][0:n, par, h, K_KDEC:K_KDEC + 1])
                    last.then_inc(e["kd_ready"], 1)

                def x(ch, t, par, n, l):
                    e = sems[ch]
                    act.wait_ge(e["x_summed"], PRE + t * L + l + 1)
                    act.activation(Xn[ch][0:n, :, :], b_x[ch][0:n, :, 0:CHUNK], ACT.Copy)
                    for q in quads(n):
                        last = act.activation(X[ch][q, :, q], b_x[ch][q, :, 0:CHUNK], ACT.Copy)
                    last.then_inc(e["x_copied"], 1)

                def v_copy(ch, t, par, c):
                    e, r = sems[ch], c * CHUNK
                    act.wait_ge(e["o_summed"], PRE + 2 * t + c)
                    act.wait_ge(e["vn_summed"], PRE + 2 * t + c + 1)
                    act.activation(vn[ch][r:r + CHUNK, :, :], b_w[ch][r:r + CHUNK, :, :], ACT.Copy).then_inc(e["vn_copied"], 1)

                def o_copy(ch, t, par, c):
                    if ch < CHAINS - 1:
                        return
                    for other in C:
                        e, r = sems[other], c * CHUNK
                        if c == 0:
                            act.wait_ge(e[f"out_stored{par}"], PRE + 8 * t - 8 * par)
                        act.wait_ge(e["o_summed"], PRE + 2 * t + c + 1)
                        act.activation(out[other][:, par, :, r:r + CHUNK], b_s[other][:, :, 0:CHUNK], ACT.Copy).then_inc(e["o_copied"], 1)
                        n = SAMPLE if isinstance(t, int) and t == last_t else P
                        if r + CHUNK == n:
                            act.wait_ge(e["o_copied"], PRE + 2 * t + c + 1)
                            act.dma_start(m["o_dram"][bass.ds(GH * group(other), GH), :, bass.ds(t * P, n)].rearrange("h p t -> p h t"),
                                          out[other][:, par, :, 0:n]).then_inc(e[f"out_stored{par}"], 16)

                for ch in C:
                    act.wait_ge(sems[ch]["state_set"], PRE + 1)
                delta_tiles(act, {"stage": stage, "scores": scores, "level0": level0, "x": x, "d": skip, "R0": skip, "R1": v_copy, "R2": o_copy})
                for ch in C:
                    act.wait_ge(sems[ch]["out_stored0"], PRE + 16 * ((NT + 1) // 2))
                    act.wait_ge(sems[ch]["out_stored1"], PRE + 16 * (NT // 2))

            @block.vector
            def _(dve):
                def stage(ch, t, par, n):
                    e = sems[ch]
                    dve.wait_ge(e["cols_staged"], PRE + t + 1)
                    dve.wait_ge(e[f"rows_loaded{par}"], PRE + 16 * t + 32 - 16 * par)
                    for h in range(GH):
                        last = dve.tensor_scalar(dec[ch][0:n, h, 0:n], gb[ch][0:n, par, 0, h, 0:n], cst[ch][0:n, par, h, K_GC:K_GC + 1], 0.0, ALU.subtract, ALU.min)
                    last.then_inc(e["diffs"], 1)

                def scores(ch, t, par, n):
                    e = sems[ch]
                    dve.wait_ge(e["dexp"], PRE + t + 1)
                    dve.tensor_tensor(dec[ch][0:n, :, 0:n], dec[ch][0:n, :, 0:n], over_heads(cst_sq(C_INCL, n)), ALU.mult).then_inc(e["masked"], 1)
                    dve.wait_ge(e["lvl_masked"], PRE + L * t)
                    dve.wait_ge(e["masked"], PRE + t + 1)
                    dve.wait_ge(e["scored"], PRE + t + 1)
                    pairs = lambda a: a[0:n, :, 0:n].rearrange("p (k two) c -> p k two c", two=2)
                    score = lambda k: b_x[ch][0:n, k:k + GK, 0:n].unsqueeze(2).broadcast_to([n, GK, 2, n])
                    dve.tensor_tensor(pairs(at[ch]), score(0), pairs(dec[ch]), ALU.mult).then_inc(e["at_half"], 1)
                    if not is_first(t):
                        dve.wait_ge(e["o_summed"], PRE + 2 * (t - 1))
                    dve.tensor_tensor(pairs(attn[ch][:, par]), score(GK), pairs(dec[ch]), ALU.mult).then_inc(e["attn_ready"], 1)
                    dve.wait_ge(e["at_half"], PRE + t + 1)
                    dve.tensor_tensor(at[ch][0:n, :, 0:n], at[ch][0:n, :, 0:n], gb[ch][0:n, par, 1, :, 0:n], ALU.mult).then_inc(e["at_ready"], 1)
                    dve.wait_ge(e["eg_ready"], PRE + t + 1)
                    dve.wait_ge(e[f"qkv_loaded{par}"], PRE + 24 * t + 48 - 24 * par)
                    twice = lambda a: a.rearrange("p (k two) c -> p k two c", two=2)
                    dve.tensor_tensor(twice(qg[ch][:, par, :, 0:n]), qst[ch][:, par, :, 0:n].unsqueeze(2).broadcast_to([P, GK, 2, n]), twice(eg[ch][:, :, 0:n]), ALU.mult).then_inc(e["qg_ready"], 1)

                def level0(ch, t, par, n):
                    e = sems[ch]
                    dve.wait_ge(e["t_new"], PRE + t * L)
                    dve.wait_ge(e["lvl_masked"], PRE + t * L + 1)
                    dve.tensor_tensor(TT[ch][0:n, par, :, 0:n], over_heads(cst_sq(C_ID, n)), BT[ch][0:n, 0, :, 0:n], ALU.subtract)
                    for q in quads(n):
                        dve.tensor_tensor(TTn[ch][q, 0, :, :], over_heads(narrow_id(q)), BT[ch][q, 0, :, q], ALU.subtract)
                    dve.wait_ge(e["x_summed"], PRE + t * L + 1)
                    dve.tensor_tensor(Tn[ch][0:n, :, :], over_heads(narrow_id(slice(0, n))), b_x[ch][0:n, :, 0:CHUNK], ALU.subtract).then_inc(e["t_new"], 1)

                def d(ch, t, par, n, l):
                    e = sems[ch]
                    dve.wait_ge(e["t_new"], PRE + t * L + l)
                    dve.wait_ge(e["deltas"], PRE + t * (L - 1) + l)
                    if l < L - 1:
                        dve.tensor_tensor(Tn[ch][0:n, :, :], Tn[ch][0:n, :, :], b_d[ch][0:n, :, 0:CHUNK], ALU.subtract)
                    for q in quads(n):
                        last = dve.tensor_tensor(TT[ch][q, par, :, q], TTn[ch][q, (l - 1) % 2, :, :], b_d[ch][q, :, CHUNK:P], ALU.subtract)
                    if l < L - 1:
                        last = dve.tensor_tensor(TTn[ch][0:n, l % 2, :, :], TTn[ch][0:n, (l - 1) % 2, :, :], b_d[ch][0:n, :, CHUNK:P], ALU.subtract)
                    last.then_inc(e["t_new"], 1)

                def right_side(ch, t, par, c):
                    e, r = sems[ch], c * CHUNK
                    dve.wait_ge(e["vb_ready"], PRE + t + 1)
                    dve.wait_ge(e["ks_summed"], PRE + 2 * t + c + 1)
                    for h in range(GH):
                        last = dve.scalar_tensor_tensor(out=rhs[ch][r:r + CHUNK, h, :], in0=b_w[ch][r:r + CHUNK, h, :], scalar=cst[ch][r:r + CHUNK, par, h, K_NGB:K_NGB + 1],
                                                        in1=vb[ch][r:r + CHUNK, par, h, :], op0=ALU.mult, op1=ALU.add)
                    last.then_inc(e["rhs_ready"], 1)

                def new_state(ch, t, par, c):
                    e = sems[ch]
                    dve.wait_ge(e["s_summed"], PRE + 2 * t + c + 1)
                    for h in range(GH):
                        last = dve.scalar_tensor_tensor(out=S[ch][:, 1 - c, h, :], in0=S[ch][:, c, h, :], scalar=egl[ch][:, par, h, c:c + 1], in1=b_s[ch][:, h, :],
                                                        op0=ALU.mult, op1=ALU.add)
                    last.then_inc(e["s_new"], 1)

                delta_tiles(dve, {"stage": stage, "scores": scores, "level0": level0, "x": skip, "d": d, "R0": right_side, "R1": skip, "R2": new_state})


def mix_stage(nc, m, og):
    with Stage(nc, "mix") as st:
        o, z = st.sb("o", [P, 2, TOK]), st.sb("z", [P, 2, TOK])
        sq, root = st.sb("sq", [P, 2, TOK]), st.sb("root", [P, 2, TOK])
        pm = st.ps("pm", [P, 2, 3, 512])
        two = lambda n: [st.sem(f"{n}{u}") for u in range(2)]
        loaded, squared, summed, rooted, inverted, normed, gated = (two(n) for n in ("loaded", "squared", "summed", "rooted", "inverted", "normed", "gated"))
        with st.block() as block:
            @block.sync
            def _(sp):
                with sp.Fori(0, HV // 2) as i:
                    for u in range(2):
                        sp.wait_ge(gated[u], PRE + i)
                        for dst, src, t in ((o, m["o_dram"], 2 * i + u), (z, m["proj_dram"], CONV_CH // P + 2 * i + u)):
                            sp.dma_start(dst[:, u, :], src[bass.ds(t, 1)].rearrange("o p t -> p (o t)")).then_inc(loaded[u], 16)

            @block.gpsimd
            def _(pool):
                with pool.Fori(0, HV // 2) as i:
                    for u in range(2):
                        pool.wait_ge(loaded[u], PRE + 32 * (i + 1))
                        pool.wait_ge(summed[u], PRE + i)
                        pool.tensor_tensor(sq[:, u, :], o[:, u, :], o[:, u, :], ALU.mult).then_inc(squared[u], 1)

            @block.tensor
            def _(pe):
                with pe.Fori(0, HV // 2) as i:
                    for u in range(2):
                        pe.wait_ge(squared[u], PRE + i + 1)
                        pe.wait_ge(rooted[u], PRE + i)
                        for b, (c, n) in enumerate(BLK):
                            last = pe.matmul(pm[:, u, b, 0:n], m["const"][:, C_ONES * P:(C_ONES + 1) * P], sq[:, u, c:c + n], start=True, stop=True)
                        last.then_inc(summed[u], 1)

            @block.scalar
            def _(act):
                with act.Fori(0, HV // 2) as i:
                    for u in range(2):
                        act.wait_ge(summed[u], PRE + i + 1)
                        act.wait_ge(normed[u], PRE + i)
                        for b, (c, n) in enumerate(BLK):
                            last = act.activation(root[:, u, c:c + n], pm[:, u, b, 0:n], ACT.Sqrt, bias=m["eps"][:, :], scale=1.0 / DV)
                        last.then_inc(rooted[u], 1)

            @block.vector
            def _(dve):
                with dve.Fori(0, HV // 2) as i:
                    for u in range(2):
                        dve.wait_ge(rooted[u], PRE + i + 1)
                        dve.reciprocal(root[:, u, :], root[:, u, :]).then_inc(inverted[u], 1)
                        dve.wait_ge(loaded[u], PRE + 32 * (i + 1))
                        dve.wait_ge(inverted[u], PRE + i + 1)
                        dve.scalar_tensor_tensor(out=o[:, u, :], in0=o[:, u, :], scalar=m["gains"][:, G_ONORM:G_ONORM + 1], in1=root[:, u, :],
                                                 op0=ALU.mult, op1=ALU.mult).then_inc(normed[u], 1)
                        dve.wait_ge(normed[u], PRE + i + 1)
                        dve.tensor_tensor(og[:, bass.ds(2 * i + u, 1), :].rearrange("p o t -> p (o t)"), o[:, u, :], z[:, u, :], ALU.mult).then_inc(gated[u], 1)


def tails_stage(nc, m, io):
    with Stage(nc, "tails") as st:
        rows = st.sb("rows", [HIST * 32, 2, P])
        pt = st.ps("pt", [HIST * 32, 2, P])
        turned, copied, stored = st.sem("turned"), st.sem("copied"), st.sem("stored")
        with st.block() as block:
            @block.tensor
            def _(pe):
                for a in range(2):
                    last = pe.transpose(pt[:, a, :], m["tail"][:, a, :, :].rearrange("p j t -> p (j t)"), m["const"][:, 0:P])
                last.then_inc(turned, 1)

            @block.vector
            def _(dve):
                dve.wait_ge(turned, PRE + 1)
                dve.tensor_copy(rows[:, :, :], pt[:, :, :]).then_inc(copied, 1)

            @block.sync
            def _(sp):
                sp.wait_ge(copied, PRE + 1)
                for a, name in enumerate(("conv_p", "conv_s")):
                    sp.dma_start(io[name][0, 0].rearrange("j (t p) -> (j t) p", p=P), rows[:, a, :]).then_inc(stored, 16)
                sp.wait_ge(stored, PRE + 32)


def blocks3(tile):
    return tile[:, 0:768].rearrange("p (b c) -> p b c", b=2), tile[:, 768:TOK]


def ffn_up_stage(nc, m, hT, hid, w1, w3):
    with Stage(nc, "ffnup") as st:
        wa, wb = st.sb("w1", [P, 2, KD, P]), st.sb("w3", [P, 2, KD, P])
        silu = st.sb("silu", [P, TOK])
        pm = st.ps("pm", [P, 2, 3, 512])
        w_loaded = [st.sem(f"w_loaded{u}") for u in range(2)]
        used = [st.sem(f"w_used{u}") for u in range(2)]
        a_done, silued, gated = st.sem("a_done"), st.sem("silued"), st.sem("gated")
        with st.block() as block:
            @block.sync
            def _(sp):
                with sp.Fori(0, KF // 2) as i:
                    for u in range(2):
                        sp.wait_ge(used[u], PRE + i)
                        for w, dst in ((w1, wa), (w3, wb)):
                            sp.dma_start(dst[:, u, :, :], w[:, bass.ds((2 * i + u) * P, P)].rearrange("(k p) c -> p k c", p=P)).then_inc(w_loaded[u], 16)

            @block.tensor
            def _(pe):
                with pe.Fori(0, KF // 2) as i:
                    for u in range(2):
                        pe.wait_ge(w_loaded[u], PRE + 32 * (i + 1))
                        for q, (w, freed, done) in enumerate(((wa, silued, a_done), (wb, gated, used[u]))):
                            pe.wait_ge(freed, PRE + 2 * i + u)
                            for k in range(KD):
                                for b, (c, n) in enumerate(BLK):
                                    last = pe.matmul(pm[:, q, b, 0:n], w[:, u, k, :], hT[:, k, c:c + n], start=(k == 0), stop=(k == KD - 1))
                            last.then_inc(done, 1)

            @block.scalar
            def _(act):
                with act.Fori(0, KF) as f:
                    act.wait_ge(a_done, PRE + f + 1)
                    act.wait_ge(gated, PRE + f)
                    two, rest = blocks3(silu)
                    act.activation(two, pm[:, 0, 0:2, 0:384], ACT.Silu)
                    act.activation(rest, pm[:, 0, 2, 0:320], ACT.Silu).then_inc(silued, 1)

            @block.vector
            def _(dve):
                with dve.Fori(0, KF // 2) as i:
                    for u in range(2):
                        dve.wait_ge(used[u], PRE + i + 1)
                        dve.wait_ge(silued, PRE + 2 * i + u + 1)
                        two, rest = blocks3(hid[:, bass.ds(2 * i + u, 1), :].rearrange("p o t -> p (o t)"))
                        stwo, srest = blocks3(silu)
                        dve.tensor_tensor(two, stwo, pm[:, 1, 0:2, 0:384], ALU.mult)
                        dve.tensor_tensor(rest, srest, pm[:, 1, 2, 0:320], ALU.mult).then_inc(gated, 1)


def add_product_stage(nc, m, name, src, kt, load, parts=1):
    xT = m["xT"]
    with Stage(nc, name) as st:
        w = st.sb("w", [P, 2, kt, P])
        pm = st.ps("pm", [P, 2, 3, 512])
        w_loaded = [st.sem(f"w_loaded{u}") for u in range(2)]
        done = [st.sem(f"tile_summed{u}") for u in range(2)]
        added = [st.sem(f"tile_added{u}") for u in range(2)]
        with st.block() as block:
            @block.sync
            def _(sp):
                with sp.Fori(0, KD // 2) as i:
                    for u in range(2):
                        sp.wait_ge(done[u], PRE + i)
                        for to, frm in load(w[:, u, :, :], 2 * i + u):
                            sp.dma_start(to, frm).then_inc(w_loaded[u], 16)

            @block.tensor
            def _(pe):
                with pe.Fori(0, KD // 2) as i:
                    for u in range(2):
                        pe.wait_ge(w_loaded[u], PRE + 16 * parts * (i + 1))
                        pe.wait_ge(added[u], PRE + i)
                        for k in range(kt):
                            for b, (c, n) in enumerate(BLK):
                                last = pe.matmul(pm[:, u, b, 0:n], w[:, u, k, :], src[:, k, c:c + n], start=(k == 0), stop=(k == kt - 1))
                        last.then_inc(done[u], 1)

            @block.vector
            def _(dve):
                with dve.Fori(0, KD // 2) as i:
                    for u in range(2):
                        dve.wait_ge(done[u], PRE + i + 1)
                        two, rest = blocks3(xT[:, bass.ds(2 * i + u, 1), :].rearrange("p o t -> p (o t)"))
                        dve.tensor_tensor(two, two, pm[:, u, 0:2, 0:384], ALU.add)
                        dve.tensor_tensor(rest, rest, pm[:, u, 2, 0:320], ALU.add).then_inc(added[u], 1)


K_CACHE = WINDOW + PROMPT
K_SAMPLE = K_CACHE + WINDOW
KEYS = K_SAMPLE + SAMPLE
KV_T = HKV * HD // P
VS = KEYS // CHUNK



def heads_stage(nc, m, name, hT, n_tiles, rotated, dests, loads, io):
    with Stage(nc, name) as st:
        w = st.sb("w", [P, 2, KD, 4 * P])
        rope = st.sb("rope", [P, 2, TOK])
        raw = st.sb("raw", [P, 2, TOK])
        sn = st.sb("sin_part", [P, TOK])
        pm = st.ps("pm", [P, 2, 3, 512])
        w_loaded = [st.sem(f"w_loaded{u}") for u in range(2)]
        rope_l, done, copied, turned, rot, ready = (st.sem(s) for s in ("rope_loaded", "tile_summed", "tile_copied", "swapped", "rotate_step", "tile_ready"))
        with st.block() as block:
            @block.sync
            def _(sp):
                sp.dma_start(rope[:, :, :], io["rope"].rearrange("a p t -> p a t")).then_inc(rope_l, 16)
                for s, load in enumerate(loads(w)):
                    for to, frm in load:
                        sp.dma_start(to, frm).then_inc(w_loaded[s], 16)

            @block.tensor
            def _(pe):
                def swap(t):
                    pe.wait_ge(copied, PRE + t + 1)
                    for b, (c, n) in enumerate(BLK):
                        last = pe.matmul(pm[:, t % 2, b, 0:n], m["const"][:, C_ROT * P:(C_ROT + 1) * P], raw[:, t % 2, c:c + n], start=True, stop=True)
                    last.then_inc(turned, 1)

                for t in range(n_tiles):
                    s = t // 4
                    if t % 4 == 0:
                        pe.wait_ge(w_loaded[s], PRE + 16 * len(loads(w)[s]))
                    if t >= 2:
                        pe.wait_ge(ready, PRE + t - 1)
                    for k in range(KD):
                        for b, (c, n) in enumerate(BLK):
                            last = pe.matmul(pm[:, t % 2, b, 0:n], w[:, s, k, (t % 4) * P:(t % 4 + 1) * P], hT[:, k, c:c + n], start=(k == 0), stop=(k == KD - 1))
                    last.then_inc(done, 1)
                    if 1 <= t <= rotated:
                        swap(t - 1)
                if rotated == n_tiles:
                    swap(n_tiles - 1)

            @block.scalar
            def _(act):
                for t in range(n_tiles):
                    act.wait_ge(done, PRE + t + 1)
                    if t >= 2:
                        act.wait_ge(ready, PRE + t - 1)
                    two, rest = blocks3(raw[:, t % 2, :])
                    act.activation(two, pm[:, t % 2, 0:2, 0:384], ACT.Copy)
                    act.activation(rest, pm[:, t % 2, 2, 0:320], ACT.Copy).then_inc(copied, 1)

            @block.vector
            def _(dve):
                dve.wait_ge(rope_l, PRE + 16)
                step = Chain(dve, rot)
                for t in range(n_tiles):
                    if t < rotated:
                        dve.wait_ge(turned, PRE + t + 1)
                        two, rest = blocks3(sn)
                        stwo, srest = blocks3(rope[:, 1, :])
                        dve.tensor_tensor(two, stwo, pm[:, t % 2, 0:2, 0:384], ALU.mult)
                        dve.tensor_tensor(rest, srest, pm[:, t % 2, 2, 0:320], ALU.mult)
                        step(dve.tensor_tensor(raw[:, t % 2, :], raw[:, t % 2, :], rope[:, 0, :], ALU.mult))
                        for to, c in dests(t):
                            n = to.shape[-1]
                            last = dve.tensor_tensor(to, raw[:, t % 2, c:c + n], sn[:, c:c + n], ALU.add)
                        last.then_inc(ready, 1)
                        dve.wait_ge(ready, PRE + t + 1)
                    else:
                        dve.wait_ge(copied, PRE + t + 1)
                        for to, c in dests(t):
                            n = to.shape[-1]
                            last = dve.tensor_copy(to, raw[:, t % 2, c:c + n])
                        last.then_inc(ready, 1)


def values_stage(nc, m, kT, vT, v128, io):
    with Stage(nc, "values") as st:
        ck = st.sb("ck", [P, HKV * HD])
        kout = st.sb("kout", [P, 2, HKV * HD])
        pv = st.ps("pv", [P, 2, 4, P])
        pk = st.ps("pk", [P, 4, P])
        loaded, turned, copied, kturned, kcopied, stored = (st.sem(s) for s in ("loaded", "v_turned", "v_copied", "k_turned", "k_copied", "stored"))
        wins = [(s, (s - 2) * CHUNK, P) for s in range(2, 17)] + [(17, PROMPT - CHUNK, CHUNK), (VS - 1, PROMPT, SAMPLE)]
        ident = m["const"][:, 0:P]
        with st.block() as block:
            @block.sync
            def _(sp):
                sp.dma_start(ck[:, :], io["cache_k"][0].rearrange("t h d -> t (h d)")).then_inc(loaded, 16)
                sp.dma_start(v128[:, VS - 3, :], io["cache_v"][0].rearrange("t h d -> t (h d)")).then_inc(loaded, 16)
                sp.wait_ge(kcopied, PRE + 3)
                sp.dma_start(io["k_p"][0].rearrange("t h d -> t (h d)"), kout[:, 0, :]).then_inc(stored, 16)
                sp.dma_start(io["k_s"][0].rearrange("t h d -> t (h d)"), kout[0:SAMPLE, 1, :]).then_inc(stored, 16)
                sp.wait_ge(copied, PRE + len(wins))
                sp.dma_start(io["v_p"][0].rearrange("t h d -> t (h d)"), v128[:, 16, :]).then_inc(stored, 16)
                sp.dma_start(io["v_s"][0].rearrange("t h d -> t (h d)"), v128[0:SAMPLE, VS - 1, :]).then_inc(stored, 16)
                sp.wait_ge(loaded, PRE + 32)
                sp.wait_ge(stored, PRE + 64)

            @block.tensor
            def _(pe):
                for i, (s, tok, n) in enumerate(wins):
                    if i >= 2:
                        pe.wait_ge(copied, PRE + i - 1)
                    for j in range(KV_T):
                        last = pe.transpose(pv[0:n, i % 2, j, :], vT[:, j, tok:tok + n], ident)
                    last.then_inc(turned, 1)
                pe.wait_ge(loaded, PRE + 32)
                for i in range(3):
                    if i:
                        pe.wait_ge(kcopied, PRE + i)
                    for j in range(KV_T):
                        last = (pe.transpose(pk[:, j, :], ck[:, j * P:(j + 1) * P], ident) if i == 0 else
                                pe.transpose(pk[:, j, :], kT[:, j, K_CACHE - WINDOW:K_CACHE], ident) if i == 1 else
                                pe.transpose(pk[0:SAMPLE, j, :], kT[:, j, K_SAMPLE:KEYS], ident))
                    last.then_inc(kturned, 1)

            @block.scalar
            def _(act):
                for i, (s, tok, n) in enumerate(wins):
                    act.wait_ge(turned, PRE + i + 1)
                    act.activation(v128[0:n, s, :].rearrange("p (j c) -> p j c", j=KV_T), pv[0:n, i % 2, 0:KV_T, :], ACT.Copy).then_inc(copied, 1)

            @block.vector
            def _(dve):
                for i, (to, n) in enumerate(((kT[:, :, K_CACHE:K_SAMPLE], P), (kout[:, 0, :].rearrange("p (j c) -> p j c", j=KV_T), P),
                                             (kout[0:SAMPLE, 1, :].rearrange("p (j c) -> p j c", j=KV_T), SAMPLE))):
                    dve.wait_ge(kturned, PRE + i + 1)
                    dve.tensor_copy(to, pk[0:n, 0:KV_T, :]).then_inc(kcopied, 1)


def attend_stage(nc, m, qT, kT, v128, aT):
    SPAN = WINDOW + CHUNK
    with Stage(nc, "attend") as st:
        qs, ks, vs = st.sb("qs", [P, 8, CHUNK]), st.sb("ks", [P, KV_T, SPAN]), st.sb("vs", [P, 2, HKV * HD])
        snk = st.sb("snk", [P, HKV, 2])
        prob = st.sb("prob", [P, HKV, 2, SPAN])
        pT = st.sb("pT", [P, 2, 4, P])
        osb = st.sb("osb", [P, HKV, 2, HD])
        mx, nmx, sm, es, rd = (st.sb(n, [P, HKV, 2]) for n in ("mx", "nmx", "sm", "es", "rd"))
        ps = st.ps("scores", [P, HKV, 512])
        pt = st.ps("turned", [P, 2, 4, P])
        po, poT = st.ps("out", [P, HKV, 2, HD]), st.ps("outT", [P, HKV, P])
        names = ("sink_set", "q_staged", "kv_staged", "scored", "max_ready", "bias_ready", "exped", "den_step", "den_ready", "p_turned", "p_copied_a", "p_copied_b",
                 "pv_summed", "o_normed", "o_turned", "o_copied")
        e = {n: st.sem(n) for n in names}
        passed = st.sem("passed")
        ident = m["const"][:, 0:P]
        aview = aT[:, :, :].rearrange("p (j l) t -> p j l t", l=2)
        with st.block() as block:
            @block.tensor
            def _(pe):
                def chunk(i, keys, v0, v1):
                    pe.wait_ge(e["q_staged"], PRE + i + 1)
                    pe.wait_ge(e["kv_staged"], PRE + i + 1)
                    for jp in range(2):
                        pe.wait_ge(e["exped"], PRE + 2 * i)
                        hold(pe, passed)
                        for b in range(2):
                            for g in range(4):
                                last = pe.matmul(ps[CHUNK * (g % 2):CHUNK * (g % 2) + CHUNK, 2 * jp + b, (g // 2) * SPAN:(g // 2) * SPAN + keys],
                                                 qs[HD * b:HD * b + HD, 4 * jp + g, :], ks[HD * b:HD * b + HD, jp, 0:keys], start=True, stop=True,
                                                 skip_group_check=True)
                        last.then_inc(e["scored"], 1)
                    for jp in range(2):
                        pe.wait_ge(e["exped"], PRE + 2 * i + jp + 1)
                        pe.wait_ge(e["p_copied_a"], PRE + 2 * i + jp)
                        pe.wait_ge(e["p_copied_b"], PRE + 2 * i + jp)
                        for x in range(4):
                            p = prob[:, 2 * jp + x // 2, x % 2, :]
                            if v0 is not None:
                                last = pe.transpose(pt[:, 0, x, :], p[:, 0:P], ident)
                            if v1 is not None:
                                last = pe.transpose(pt[0:CHUNK, 1, x, :], p[:, keys - CHUNK:keys], ident)
                        last.then_inc(e["p_turned"], 1)
                        pe.wait_ge(e["p_copied_a"], PRE + 2 * i + jp + 1)
                        pe.wait_ge(e["p_copied_b"], PRE + 2 * i + jp + 1)
                        pe.wait_ge(e["o_normed"], PRE + 2 * i + jp)
                        for x in range(4):
                            j = 2 * jp + x // 2
                            pieces = [(pT[:, 0, x, :], vs[:, 0, j * HD:(j + 1) * HD])] if v0 is not None else []
                            if v1 is not None:
                                pieces.append((pT[0:CHUNK, 1, x, :], vs[0:CHUNK, 1, j * HD:(j + 1) * HD]))
                            for n, (l, r) in enumerate(pieces):
                                last = pe.matmul(po[:, j, x % 2, :], l, r, start=(n == 0), stop=(n == len(pieces) - 1))
                        last.then_inc(e["pv_summed"], 1)
                    pe.wait_ge(e["o_normed"], PRE + 2 * i + 2)
                    pe.wait_ge(e["o_copied"], PRE + i)
                    for j in range(HKV):
                        last = pe.transpose(poT[:, j, :], osb[:, j, :, :].rearrange("p a c -> p (a c)"), ident)
                    last.then_inc(e["o_turned"], 1)

                chunk(0, CHUNK, None, True)
                chunk(1, 2 * CHUNK, True, None)
                with pe.Fori(2, 16) as c:
                    chunk(c, SPAN, True, True)
                chunk(16, SPAN, True, True)

            @block.gpsimd
            def _(pool):
                def chunk(i, keys, k0, v0, v1):
                    pool.wait_ge(e["pv_summed"], PRE + 2 * i)
                    if v0 is not None:
                        pool.tensor_copy(vs[:, 0, :], v128[:, bass.ds(v0, 1), :].rearrange("p o c -> p (o c)"))
                    if v1 is not None:
                        pool.tensor_copy(vs[0:CHUNK, 1, :], v128[0:CHUNK, bass.ds(v1, 1), :].rearrange("p o c -> p (o c)"))
                    pool.tensor_copy(ks[:, :, 0:keys], kT[:, :, bass.ds(k0, keys)]).then_inc(e["kv_staged"], 1)

                chunk(0, CHUNK, WINDOW, None, 2)
                chunk(1, 2 * CHUNK, WINDOW, 2, None)
                with pool.Fori(2, 16) as c:
                    chunk(c, SPAN, c * CHUNK, c, c + 2)
                chunk(16, SPAN, K_CACHE, VS - 3, VS - 1)

            @block.scalar
            def _(act):
                def chunk(i, keys):
                    act.wait_ge(e["scored"], PRE + 2 * i)
                    act.activation(qs[:, :, :], qT[:, :, bass.ds(i * CHUNK, CHUNK)], ACT.Copy, scale=HD ** -0.5).then_inc(e["q_staged"], 1)
                    for jp in range(2):
                        act.wait_ge(e["bias_ready"], PRE + 2 * i + jp + 1)
                        act.activation(es[:, 2 * jp:2 * jp + 2, :], es[:, 2 * jp:2 * jp + 2, :], ACT.Exp)
                        for x in range(4):
                            j = 2 * jp + x // 2
                            last = act.activation(prob[:, j, x % 2, 0:keys], ps[:, j, (x % 2) * SPAN:(x % 2) * SPAN + keys], ACT.Exp,
                                                  bias=nmx[:, j, x % 2:x % 2 + 1], accum_out=sm[:, j, x % 2:x % 2 + 1])
                        last.then_inc(e["exped"], 1)
                    for jp in range(2):
                        act.wait_ge(e["p_turned"], PRE + 2 * i + jp + 1)
                        if keys > CHUNK:
                            last = act.activation(pT[:, 0, :, :], pt[:, 0, :, :], ACT.Copy)
                            last.then_inc(e["p_copied_a"], 1)
                        else:
                            act.sem_inc(e["p_copied_a"], 1)
                    act.wait_ge(e["o_turned"], PRE + i + 1)
                    act.activation(aview[:, :, :, bass.ds(i * CHUNK, CHUNK)], poT[:, :, :].rearrange("p j (l q) -> p j l q", l=2), ACT.Copy).then_inc(e["o_copied"], 1)

                chunk(0, CHUNK)
                chunk(1, 2 * CHUNK)
                with act.Fori(2, 16) as c:
                    chunk(c, SPAN)
                chunk(16, SPAN)

            @block.vector
            def _(dve):
                STEPS = 4
                sv = m["swa_sinks"][:, :].rearrange("p (j g l) -> p j g l", g=2, l=2)
                dve.tensor_copy(snk[0:64, :, :], sv[0:64, :, :, 0])
                dve.tensor_copy(snk[64:128, :, :], sv[64:128, :, :, 1]).then_inc(e["sink_set"], 1)
                dve.wait_ge(e["sink_set"], PRE + 1)

                def chunk(i, keys):
                    step = Chain(dve, e["den_step"], i * 2 * STEPS)
                    for jp in range(2):
                        h = slice(2 * jp, 2 * jp + 2)
                        dve.wait_ge(e["scored"], PRE + 2 * i + jp + 1)
                        sc = ps[:, h, 0:2 * SPAN].rearrange("p j (g c) -> p j g c", g=2)[:, :, :, 0:keys]
                        step(dve.tensor_reduce(mx[:, h, :], sc, AX.X, ALU.max))
                        step(dve.tensor_tensor(mx[:, h, :], mx[:, h, :], snk[:, h, :], ALU.max))
                        dve.tensor_tensor(es[:, h, :], snk[:, h, :], mx[:, h, :], ALU.subtract)
                        dve.tensor_scalar(nmx[:, h, :], mx[:, h, :], -1.0, None, ALU.mult).then_inc(e["bias_ready"], 1)
                    for jp in range(2):
                        h = slice(2 * jp, 2 * jp + 2)
                        if keys != 2 * CHUNK:
                            dve.wait_ge(e["p_turned"], PRE + 2 * i + jp + 1)
                            dve.tensor_copy(pT[0:CHUNK, 1, :, :], pt[0:CHUNK, 1, :, :]).then_inc(e["p_copied_b"], 1)
                        else:
                            dve.sem_inc(e["p_copied_b"], 1)
                        dve.wait_ge(e["exped"], PRE + 2 * i + jp + 1)
                        step(dve.tensor_tensor(rd[:, h, :], sm[:, h, :], es[:, h, :], ALU.add))
                        step(dve.reciprocal(rd[:, h, :], rd[:, h, :]))
                        dve.wait_ge(e["pv_summed"], PRE + 2 * i + jp + 1)
                        dve.tensor_tensor(osb[:, h, :, :], po[:, h, :, :], rd[:, h, :].unsqueeze(3).broadcast_to([P, 2, 2, HD]), ALU.mult).then_inc(e["o_normed"], 1)

                chunk(0, CHUNK)
                chunk(1, 2 * CHUNK)
                with dve.Fori(2, 16) as c:
                    chunk(c, SPAN)
                chunk(16, SPAN)


TOP_K = 2
CAP = 320
OVER_MAX = TOP_K * TOK // CAP
JOBS = NE + OVER_MAX
MORE = (TOK - 1) // CAP
SLOTS = JOBS * CAP
CAP_T = [(s, min(P, CAP - s)) for s in range(0, CAP, P)]


def route_stage(nc, m, hT, io, r):
    ramp, pidx = m["const"][:, N_CONST * P:N_CONST * P + NE], m["const"][:, N_CONST * P + NE:N_CONST * P + NE + 1]
    with Stage(nc, "route") as st:
        wr = st.sb("wr", [P, KD, NE])
        hrow = st.sb("hrow", [P, 2, D])
        lg, one, two, tmp, tmp2, offs, rank = (st.sb(n, [P, NT, NE]) for n in ("lg", "one", "two", "tmp", "tmp2", "offs", "rank"))
        m1, m2, rt, e21 = (st.sb(n, [P, NT]) for n in ("m1", "m2", "rt", "e21"))
        total, over, ends, coef, first, t8 = (st.sb(n, [P, NE]) for n in ("total", "over", "ends", "coef", "first", "t8"))
        slotf = st.sb("slotf", [P, TOP_K, NT])
        jobsf = st.sb("jobsf", [P, 16])
        ids = st.sb("ids", [P, NT], I32)
        zero = st.sb("zero", [P, SLOTS // P], I32)
        pl, prank, ptot = (st.ps(n, [P, NT, NE]) for n in ("logits", "rank_in_tile", "tile_total"))
        ph = st.ps("ph", [P, 4, 4, P])
        w_loaded, proj, vs, es, counted, ranked = (st.sem(n) for n in ("w_loaded", "projected", "vector_step", "exped", "counted", "ranked"))
        turned, h_copied = st.sem("turned"), st.sem("h_copied")
        h_stored = [st.sem(f"h_stored{u}") for u in range(2)]
        ids_set, slots_ready = st.sem("ids_set"), st.sem("slots_ready")
        zeroed, scattered = st.sem("zeroed", pre=False), st.sem("scattered", pre=False)
        zero_set = st.sem("zero_set")
        over_tiles = lambda a: a.unsqueeze(1).broadcast_to([P, NT, NE])
        over_experts = lambda a: a.unsqueeze(2).broadcast_to([P, NT, NE])
        with st.block() as block:
            @block.sync
            def _(sp):
                sp.dma_start(wr[:, :, :], io["moe_router"][0].rearrange("(k p) e -> p k e", p=P)).then_inc(w_loaded, 16)
                for t, (s, n) in enumerate(TILES):
                    sp.wait_ge(h_copied, PRE + 2 * t + 2)
                    sp.dma_start(m["h_dram"][s:s + n, :], hrow[0:n, t % 2, :]).then_inc(h_stored[t % 2], 16)
                sp.wait_ge(h_stored[0], PRE + 16 * ((NT + 1) // 2))
                sp.wait_ge(h_stored[1], PRE + 16 * (NT // 2))

            @block.gpsimd
            def _(pool):
                pool.memset(zero[:, :], 0).then_inc(zero_set, 1)
                pool.wait_ge(zero_set, PRE + 1)
                pool.dma_start(m["slot_tok"].rearrange("(p c) o -> p (c o)", p=P), zero[:, :]).then_inc(zeroed, 16)
                pool.wait_ge(zeroed, 16)
                pool.wait_ge(ids_set, PRE + NT)
                pool.wait_ge(slots_ready, PRE + 1)
                for a in range(TOP_K):
                    for t, (s, n) in enumerate(TILES):
                        pool.indirect_dma_start(out=m["slot_tok"], out_offset=bass.IndirectOffsetOnAxis(ap=r["slot"][0:n, a, t:t + 1], axis=0),
                                                in_=ids[0:n, t:t + 1], in_offset=None).then_inc(scattered, 16)
                        pool.wait_ge(scattered, 16 * (a * NT + t + 1))

            @block.tensor
            def _(pe):
                pe.wait_ge(w_loaded, PRE + 16)
                for t, (s, n) in enumerate(TILES):
                    for k in range(KD):
                        last = pe.matmul(pl[0:n, t, :], hT[:, k, s:s + n], wr[:, k, :], start=(k == 0), stop=(k == KD - 1))
                last.then_inc(proj, 1)
                for t, (s, n) in enumerate(TILES):
                    for h in range(2):
                        i = 2 * t + h
                        if i >= 4:
                            pe.wait_ge(h_copied, PRE + i - 3)
                        for k in range(4):
                            last = pe.transpose(ph[0:n, i % 4, k, :], hT[:, 4 * h + k, s:s + n], m["const"][:, 0:P])
                        last.then_inc(turned, 1)
                pe.wait_ge(counted, PRE + 1)
                pe.matmul(prank[:, :, :], m["const"][:, C_STRICT * P:(C_STRICT + 1) * P], tmp[:, :, :], start=True, stop=True)
                pe.matmul(ptot[:, :, :], m["const"][:, C_ONES * P:(C_ONES + 1) * P], tmp[:, :, :], start=True, stop=True).then_inc(ranked, 1)

            @block.scalar
            def _(act):
                for i in range(2 * NT):
                    t, h = i // 2, i % 2
                    n = TILES[t][1]
                    if t >= 2:
                        act.wait_ge(h_stored[t % 2], PRE + 16 * (t // 2))
                    act.wait_ge(turned, PRE + i + 1)
                    act.activation(hrow[0:n, t % 2, h * 512:h * 512 + 512].rearrange("p (k c) -> p k c", c=P), ph[0:n, i % 4, :, :], ACT.Copy).then_inc(h_copied, 1)
                act.wait_ge(vs, PRE + 14)
                act.activation(e21[:, :], m2[:, :], ACT.Exp).then_inc(es, 1)

            @block.vector
            def _(dve):
                v = Chain(dve, vs)
                for t in range(NT):
                    dve.tensor_scalar(ids[:, t:t + 1], pidx, float(t * P), None, ALU.add).then_inc(ids_set, 1)
                v(dve.memset(lg[:, :, :], 0.0))
                dve.wait_ge(proj, PRE + 1)
                dve.tensor_copy(lg[:, 0:NT - 1, :], pl[:, 0:NT - 1, :])
                v(dve.tensor_copy(lg[0:64, NT - 1, :], pl[0:64, NT - 1, :]))

                def best(top, onehot):
                    v(dve.tensor_reduce(top[:, :], lg[:, :, :], AX.X, ALU.max))
                    v(dve.tensor_tensor(tmp[:, :, :], lg[:, :, :], over_experts(top[:, :]), ALU.is_equal))
                    v(dve.tensor_tensor(tmp[:, :, :], tmp[:, :, :], over_tiles(ramp), ALU.mult))
                    v(dve.tensor_reduce(rt[:, :], tmp[:, :, :], AX.X, ALU.max))
                    return dve.tensor_tensor(onehot[:, :, :], over_tiles(ramp), over_experts(rt[:, :]), ALU.is_equal)

                v(best(m1, one))
                v(dve.scalar_tensor_tensor(out=lg[:, :, :], in0=one[:, :, :], scalar=-3.0e38, in1=lg[:, :, :], op0=ALU.mult, op1=ALU.add))
                last = best(m2, two)
                v(last)
                v(dve.tensor_tensor(m2[:, :], m2[:, :], m1[:, :], ALU.subtract))
                dve.memset(one[64:128, NT - 1, :], 0.0)
                v(dve.memset(two[64:128, NT - 1, :], 0.0))
                v(dve.tensor_tensor(tmp[:, :, :], one[:, :, :], two[:, :, :], ALU.add))
                dve.sem_inc(counted, 1)
                dve.wait_ge(es, PRE + 1)
                v(dve.tensor_scalar(m1[:, :], e21[:, :], 1.0, None, ALU.add))
                v(dve.reciprocal(r["gate"][:, 0, :], m1[:, :]))
                dve.tensor_tensor(r["gate"][:, 1, :], r["gate"][:, 0, :], e21[:, :], ALU.mult)
                dve.wait_ge(ranked, PRE + 1)
                v(dve.memset(offs[:, 0, :], 0.0))
                for t in range(1, NT):
                    v(dve.tensor_tensor(offs[:, t, :], offs[:, t - 1, :], ptot[:, t - 1, :], ALU.add))
                v(dve.tensor_tensor(total[:, :], offs[:, NT - 1, :], ptot[:, NT - 1, :], ALU.add))
                v(dve.tensor_tensor(rank[:, :, :], offs[:, :, :], prank[:, :, :], ALU.add))
                v(dve.tensor_scalar(over[:, :], total[:, :], float(CAP), None, ALU.is_gt))
                for k in range(2, MORE + 1):
                    v(dve.scalar_tensor_tensor(out=over[:, :], in0=total[:, :], scalar=float(k * CAP), in1=over[:, :], op0=ALU.is_gt, op1=ALU.add))
                v(dve.tensor_copy(ends[:, 0:1], over[:, 0:1]))
                for x in range(1, NE):
                    v(dve.tensor_tensor(ends[:, x:x + 1], ends[:, x - 1:x], over[:, x:x + 1], ALU.add))
                v(dve.tensor_tensor(coef[:, :], ends[:, :], over[:, :], ALU.subtract))
                v(dve.scalar_tensor_tensor(out=coef[:, :], in0=coef[:, :], scalar=-1.0, in1=ramp, op0=ALU.add, op1=ALU.add))
                dve.tensor_scalar(first[:, :], ramp, -float(CAP), float(NE * CAP), ALU.mult, ALU.add)
                v(dve.tensor_scalar(coef[:, :], coef[:, :], float(CAP), None, ALU.mult))
                v(dve.tensor_scalar(tmp2[:, :, :], rank[:, :, :], float(CAP), None, ALU.is_ge))
                v(dve.tensor_tensor(tmp2[:, :, :], tmp2[:, :, :], over_tiles(coef[:, :]), ALU.mult))
                v(dve.tensor_tensor(tmp2[:, :, :], tmp2[:, :, :], rank[:, :, :], ALU.add))
                v(dve.tensor_tensor(tmp2[:, :, :], tmp2[:, :, :], over_tiles(first[:, :]), ALU.add))
                v(dve.tensor_tensor(one[:, :, :], one[:, :, :], tmp2[:, :, :], ALU.mult))
                v(dve.tensor_tensor(two[:, :, :], two[:, :, :], tmp2[:, :, :], ALU.mult))
                v(dve.tensor_reduce(slotf[:, 0, :], one[:, :, :], AX.X, ALU.add))
                v(dve.tensor_reduce(slotf[:, 1, :], two[:, :, :], AX.X, ALU.add))
                dve.tensor_copy(r["slot"][:, :, :], slotf[:, :, :]).then_inc(slots_ready, 1)
                v(dve.tensor_scalar(jobsf[:, 0:1], ends[:, NE - 1:NE], float(NE), None, ALU.add))
                for i in range(OVER_MAX):
                    v(dve.tensor_scalar(t8[:, 0:NE], ends[:, :], float(i), None, ALU.is_le))
                    v(dve.tensor_reduce(jobsf[:, NE + i:NE + i + 1], t8[:, 0:NE - 1], AX.X, ALU.add))
                dve.memset(jobsf[:, 1:NE], 0.0)
                v(dve.memset(jobsf[:, JOBS:16], 0.0))
                dve.tensor_copy(r["jobs"][:, :], jobsf[:, :])


def expert_stage(nc, m, io, r):
    w1, w3, w2 = io["moe_w1"][0], io["moe_w3"][0], io["moe_w2"][0]
    NF, ND = KF // 2, KD // 2
    FILLS = KD + 2 * len(CAP_T)
    with Stage(nc, "experts") as st:
        ids = st.sb("ids", [P, len(CAP_T)], I32)
        rows = st.sb("rows", [P, len(CAP_T), D])
        hx = st.sb("hx", [P, KD, CAP])
        w13 = st.sb("w13", [P, 2, 2, KD, P])
        hid = st.sb("hid", [P, KF, CAP])
        wd = st.sb("wd", [P, 2, KF, P])
        sg = st.sb("sg", [P, 2, CAP])
        yT = st.sb("yT", [P, KD, CAP])
        yrow = st.sb("yrow", [P, len(CAP_T), D])
        pa, pb, pd, pt = (st.ps(n, [P, 2, 512]) for n in ("pa", "pb", "pd", "pt"))
        zero_set, tail_zeroed, passed = st.sem("zero_set"), st.sem("tail_zeroed"), st.sem("passed")
        one = lambda n: st.sem(n)
        two = lambda n: [st.sem(f"{n}{u}") for u in range(2)]
        ids_l, gathered = st.sem("ids_loaded", pre=False), st.sem("gathered", pre=False)
        turned, t_copied, y_stored = one("turned"), one("turn_copied"), one("y_stored")
        w_l, wd_l, used, silued, gated, summed, y_copied, a_done = (two(n) for n in (
            "w_loaded", "wd_loaded", "w_used", "silued", "gated", "down_summed", "y_copied", "a_done"))

        def jobs(eng, job):
            with eng.Fori(0, NE) as j:
                job(j, j)
            n_jobs = eng.value_load(r["jobs"][0:1, 0:1], min_val=NE, max_val=JOBS)
            with eng.Fori(NE, JOBS) as j:
                with eng.If(j < n_jobs):
                    job(j, None)

        with st.block() as block:
            @block.sync
            def _(sp):
                def job(j, e):
                    if e is None:
                        e = sp.value_load(r["jobs"][0:1, bass.ds(j, 1)], min_val=0, max_val=NE - 1)
                    with sp.Fori(0, NF) as i:
                        for u in range(2):
                            sp.wait_ge(used[u], PRE + NF * j + i)
                            for x, w in enumerate((w1, w3)):
                                sp.dma_start(w13[:, u, x, :, :], w[bass.ds(e, 1), :, bass.ds((2 * i + u) * P, P)].rearrange("o (k p) c -> p (o k) c", p=P)).then_inc(w_l[u], 16)
                    with sp.Fori(0, ND) as i:
                        for u in range(2):
                            sp.wait_ge(summed[u], PRE + ND * j + i)
                            sp.dma_start(wd[:, u, :, :], w2[bass.ds(e, 1), :, bass.ds((2 * i + u) * P, P)].rearrange("o (k p) c -> p (o k) c", p=P)).then_inc(wd_l[u], 16)

                jobs(sp, job)

            @block.gpsimd
            def _(pool):
                def job(j, e):
                    for i, (s, n) in enumerate(CAP_T):
                        pool.dma_start(ids[0:n, i:i + 1], m["slot_tok"][bass.ds(j * CAP + s, n), :]).then_inc(ids_l, 16)
                    pool.wait_ge(ids_l, 48 * (j + 1))
                    pool.wait_ge(turned, PRE + FILLS * j)
                    hold(pool, passed)
                    for i, (s, n) in enumerate(CAP_T):
                        pool.indirect_dma_start(out=rows[0:n, i, :], out_offset=None, in_=m["h_dram"],
                                                in_offset=bass.IndirectOffsetOnAxis(ap=ids[0:n, i:i + 1].bitcast(U32), axis=0)).then_inc(gathered, 16)
                    pool.wait_ge(gathered, 48 * (j + 1))

                jobs(pool, job)

            @block.tensor
            def _(pe):
                ident = m["const"][:, 0:P]

                def job(j, e):
                    fill = 0
                    pe.wait_ge(gathered, 48 * (j + 1))
                    for k in range(KD):
                        pe.wait_ge(t_copied, PRE + FILLS * j + max(fill - 1, 0))
                        for i, (s, n) in enumerate(CAP_T):
                            last = pe.transpose(pt[:, fill % 2, s:s + n], rows[0:n, i, k * P:(k + 1) * P], ident[0:n, 0:n])
                        last.then_inc(turned, 1)
                        fill += 1
                    pe.wait_ge(t_copied, PRE + FILLS * j + KD)
                    hold(pe, passed)
                    with pe.Fori(0, NF) as i:
                        for u in range(2):
                            pe.wait_ge(w_l[u], PRE + 32 * (NF * j + i + 1))
                            for x, (bank, freed, done) in enumerate(((pa, silued, a_done), (pb, gated, used))):
                                pe.wait_ge(freed[u], PRE + NF * j + i)
                                for k in range(KD):
                                    last = pe.matmul(bank[:, u, 0:CAP], w13[:, u, x, k, :], hx[:, k, :], start=(k == 0), stop=(k == KD - 1))
                                last.then_inc(done[u], 1)
                    for u in range(2):
                        pe.wait_ge(gated[u], PRE + NF * (j + 1))
                    hold(pe, passed)
                    with pe.Fori(0, ND) as i:
                        for u in range(2):
                            pe.wait_ge(wd_l[u], PRE + 16 * (ND * j + i + 1))
                            pe.wait_ge(y_copied[u], PRE + ND * j + i)
                            for k in range(KF):
                                last = pe.matmul(pd[:, u, 0:CAP], wd[:, u, k, :], hid[:, k, :], start=(k == 0), stop=(k == KF - 1))
                            last.then_inc(summed[u], 1)
                    for u in range(2):
                        pe.wait_ge(y_copied[u], PRE + ND * (j + 1))
                    for i, (s, n) in enumerate(CAP_T):
                        for h in range(2):
                            pe.wait_ge(t_copied, PRE + FILLS * j + fill - 1)
                            hold(pe, passed)
                            for k in range(4):
                                last = pe.transpose(pt[0:n, fill % 2, k * P:(k + 1) * P], yT[:, 4 * h + k, s:s + n], ident)
                            last.then_inc(turned, 1)
                            fill += 1

                jobs(pe, job)

            @block.scalar
            def _(act):
                def job(j, e):
                    with act.Fori(0, NF) as i:
                        for u in range(2):
                            act.wait_ge(a_done[u], PRE + NF * j + i + 1)
                            act.wait_ge(gated[u], PRE + NF * j + i)
                            act.activation(sg[:, u, :], pa[:, u, 0:CAP], ACT.Silu).then_inc(silued[u], 1)
                    with act.Fori(0, ND) as i:
                        for u in range(2):
                            act.wait_ge(summed[u], PRE + ND * j + i + 1)
                            act.activation(yT[:, bass.ds(2 * i + u, 1), :].rearrange("p o c -> p (o c)"), pd[:, u, 0:CAP], ACT.Copy).then_inc(y_copied[u], 1)
                    act.wait_ge(t_copied, PRE + FILLS * (j + 1))
                    for i, (s, n) in enumerate(CAP_T):
                        act.dma_start(m["y_dram"][bass.ds(j * CAP + s, n), :], yrow[0:n, i, :]).then_inc(y_stored, 16)

                act.wait_ge(zero_set, PRE + 1)
                act.dma_start(m["y_dram"][NE * CAP:, :].rearrange("(a p) c -> p a c", p=P),
                              yrow[:, 0:1, :].broadcast_to([P, OVER_MAX * CAP // P, D])).then_inc(tail_zeroed, 16)
                jobs(act, job)
                n_jobs = act.value_load(r["jobs"][0:1, 0:1], min_val=NE, max_val=JOBS)
                act.wait_ge(y_stored, PRE + 48 * n_jobs)
                hold(act, passed)

            @block.vector
            def _(dve):
                def job(j, e):
                    for k in range(KD):
                        dve.wait_ge(turned, PRE + FILLS * j + k + 1)
                        dve.tensor_copy(hx[:, k, :], pt[:, k % 2, 0:CAP]).then_inc(t_copied, 1)
                    with dve.Fori(0, NF) as i:
                        for u in range(2):
                            dve.wait_ge(used[u], PRE + NF * j + i + 1)
                            dve.wait_ge(silued[u], PRE + NF * j + i + 1)
                            dve.tensor_tensor(hid[:, bass.ds(2 * i + u, 1), :].rearrange("p o c -> p (o c)"), sg[:, u, :], pb[:, u, 0:CAP], ALU.mult).then_inc(gated[u], 1)
                    dve.wait_ge(y_stored, PRE + 48 * j)
                    dve.wait_ge(tail_zeroed, PRE + 16)
                    fill = KD
                    for i, (s, n) in enumerate(CAP_T):
                        for h in range(2):
                            dve.wait_ge(turned, PRE + FILLS * j + fill + 1)
                            dve.tensor_copy(yrow[0:n, i, h * 512:h * 512 + 512], pt[0:n, fill % 2, :]).then_inc(t_copied, 1)
                            fill += 1

                dve.memset(yrow[:, 0, :], 0.0).then_inc(zero_set, 1)
                jobs(dve, job)


def final_stage(nc, m, io, r):
    outs = [io["y_prompt"][0, s:s + n, :] if s < PROMPT else io["y_sample"][0, :, :] for s, n in TILES]
    with Stage(nc, "final") as st:
        y = st.sb("y", [P, 2, TOP_K, D])
        x, sq = st.sb("x", [P, 2, D]), st.sb("sq", [P, D])
        gain = st.sb("gain", [P, D])
        ss, root, rinv = (st.sb(n, [P, NT]) for n in ("ss", "root", "rinv"))
        pt = st.ps("pt", [P, 2, 2, 512])
        g_loaded, turned, mixed, step, squared, rooted, ready = (st.sem(n) for n in ("gain_loaded", "turned", "mixed", "vector_step", "squared", "rooted", "ready"))
        gathered, stored = [st.sem(f"gathered{u}", pre=False) for u in range(2)], [st.sem(f"stored{u}") for u in range(2)]
        with st.block() as block:
            @block.gpsimd
            def _(pool):
                for t, (s, n) in enumerate(TILES):
                    if t >= 2:
                        pool.wait_ge(mixed, PRE + t - 1)
                    for a in range(TOP_K):
                        pool.indirect_dma_start(out=y[0:n, t % 2, a, :], out_offset=None, in_=m["y_dram"],
                                                in_offset=bass.IndirectOffsetOnAxis(ap=r["slot"][0:n, a, t:t + 1], axis=0)).then_inc(gathered[t % 2], 16)

            @block.sync
            def _(sp):
                sp.dma_start(gain[:, :], io["final_norm"].unsqueeze(0).broadcast_to([P, D])).then_inc(g_loaded, 16)
                for t, (s, n) in enumerate(TILES):
                    sp.wait_ge(ready, PRE + t + 1)
                    sp.dma_start(outs[t], x[0:n, t % 2, :]).then_inc(stored[t % 2], 16)
                sp.wait_ge(stored[0], PRE + 16 * ((NT + 1) // 2))
                sp.wait_ge(stored[1], PRE + 16 * (NT // 2))

            @block.tensor
            def _(pe):
                for t, (s, n) in enumerate(TILES):
                    if t >= 2:
                        pe.wait_ge(mixed, PRE + t - 1)
                    for k in range(KD):
                        last = pe.transpose(pt[0:n, t % 2, k // 4, (k % 4) * P:(k % 4 + 1) * P], m["xT"][:, k, s:s + n], m["const"][:, 0:P])
                    last.then_inc(turned, 1)

            @block.scalar
            def _(act):
                for t, (s, n) in enumerate(TILES):
                    act.wait_ge(mixed, PRE + t + 1)
                    if t:
                        act.wait_ge(rooted, PRE + t)
                    act.activation(sq[0:n, :], x[0:n, t % 2, :], ACT.Square, accum_out=ss[0:n, t:t + 1]).then_inc(squared, 1)
                    act.wait_ge(squared, PRE + t + 1)
                    act.activation(root[0:n, t:t + 1], ss[0:n, t:t + 1], ACT.Sqrt, bias=m["eps"][0:n, :], scale=1.0 / D).then_inc(rooted, 1)

            @block.vector
            def _(dve):
                v = Chain(dve, step)
                dve.wait_ge(g_loaded, PRE + 16)
                for t, (s, n) in enumerate(TILES):
                    dve.wait_ge(turned, PRE + t + 1)
                    dve.wait_ge(gathered[t % 2], 32 * (t // 2 + 1))
                    if t >= 2:
                        dve.wait_ge(stored[t % 2], PRE + 16 * (t // 2))
                    xo = x[0:n, t % 2, :].rearrange("p (h c) -> p h c", h=2)
                    yy = y[0:n, t % 2, :, :].rearrange("p a (h c) -> p a h c", h=2)
                    v(dve.scalar_tensor_tensor(out=xo, in0=yy[:, 0], scalar=r["gate"][0:n, 0, t:t + 1], in1=pt[0:n, t % 2, :, :], op0=ALU.mult, op1=ALU.add))
                    dve.scalar_tensor_tensor(out=xo, in0=yy[:, 1], scalar=r["gate"][0:n, 1, t:t + 1], in1=xo, op0=ALU.mult, op1=ALU.add).then_inc(mixed, 1)
                    dve.wait_ge(rooted, PRE + t + 1)
                    v(dve.reciprocal(rinv[0:n, t:t + 1], root[0:n, t:t + 1]))
                    dve.scalar_tensor_tensor(out=x[0:n, t % 2, :], in0=x[0:n, t % 2, :], scalar=rinv[0:n, t:t + 1], in1=gain[0:n, :], op0=ALU.mult, op1=ALU.mult).then_inc(ready, 1)


def moe_stages(nc, m, io):
    m["h_dram"] = nc.dram_tensor("h_rows", (TOK, D), F32).ap()
    m["slot_tok"] = nc.dram_tensor("slot_tokens", (SLOTS, 1), I32).ap()
    m["y_dram"] = nc.dram_tensor("slot_rows", (SLOTS, D), F32).ap()
    with nc.sbuf_tensor("gate", [P, TOP_K, NT], F32) as gate, nc.sbuf_tensor("slot", [P, TOP_K, NT], U32) as slot, \
            nc.sbuf_tensor("jobs", [P, 16], I32) as jobs:
        r = {"gate": gate, "slot": slot, "jobs": jobs}
        with nc.sbuf_tensor("h_moe", [P, KD, TOK], F32) as hT:
            norm_stage(nc, m, "norm4", [(hT, G_FFN1)])
            route_stage(nc, m, hT, io, r)
        expert_stage(nc, m, io, r)
        final_stage(nc, m, io, r)


def rest_stages(nc, m, io):
    sbt = nc.sbuf_tensor
    with sbt("hid", [P, KF, TOK], F32) as hid:
        with sbt("h_ffn", [P, KD, TOK], F32) as hT:
            norm_stage(nc, m, "norm1", [(hT, G_FFN0)])
            ffn_up_stage(nc, m, hT, hid, io["ffn_w1"][0], io["ffn_w3"][0])
        w2 = io["ffn_w2"][0]
        add_product_stage(nc, m, "ffndown", hid, KF, lambda to, t: [(to, w2[:, bass.ds(t * P, P)].rearrange("(k p) c -> p k c", p=P))])
    with sbt("kT", [P, KV_T, KEYS], F32) as kT, sbt("v128", [P, VS, HKV * HD], F32) as v128, sbt("h_att", [P, KD, TOK], F32) as hT:
        norm_stage(nc, m, "norm2", [(hT, G_KV)])
        with sbt("vTt", [P, KV_T, TOK], F32) as vT:
            heads_stage(nc, m, "kv", hT, 2 * KV_T, KV_T,
                        lambda t: [(kT[:, t, WINDOW:K_CACHE], 0), (kT[:, t, K_SAMPLE:KEYS], PROMPT)] if t < KV_T else [(vT[:, t - KV_T, :], 0)],
                        lambda w: [[(w[:, 0, :, :], io["w_kv"].rearrange("(k p) c -> p k c", p=P))]], io)
            values_stage(nc, m, kT, vT, v128, io)
        norm_stage(nc, m, "norm3", [(hT, G_ATTN1)])
        with sbt("qT", [P, 8, TOK], F32) as qT:
            wq = io["swa_w_q"][0].rearrange("(k p) (jp b c) -> jp b p k c", p=P, jp=2, b=2)

            def q_loads(w):
                return [[(w[:, jp, k, :].rearrange("p (g b c) -> p g b c", b=2, c=HD)[:, :, b, :], wq[jp, b, :, k, :].rearrange("p (g c) -> p g c", c=HD))
                         for b in range(2) for k in range(KD)] for jp in range(2)]

            heads_stage(nc, m, "q", hT, 8, 8, lambda t: [(qT[:, t, :], 0)], q_loads, io)
            attend_stage(nc, m, qT, kT, v128, hT)
        wo = io["swa_w_o"][0].rearrange("(j g l d) c -> g d j l c", j=HKV, g=2, l=2)

        def o_load(to, t):
            tv = to.rearrange("p (j l) c -> p j l c", l=2)
            return [(tv[HD * g:HD * g + HD, :, l, :], wo[g, :, :, l, bass.ds(t * P, P)]) for g in range(2) for l in range(2)]

        add_product_stage(nc, m, "attout", hT, KD, o_load, parts=4)
    moe_stages(nc, m, io)


INPUTS = ["x_prompt", "x_sample", "cache_conv", "state_delta", "cache_k", "cache_v", "norm_attn", "norm_ffn", "gdn_w_in", "gdn_w_conv",
          "gdn_a_log", "gdn_dt_bias", "gdn_o_norm", "gdn_w_out", "kv_norm", "w_kv", "swa_w_q", "swa_sinks", "swa_w_o",
          "ffn_w1", "ffn_w3", "ffn_w2", "moe_router", "moe_w1", "moe_w3", "moe_w2", "final_norm"]
OUTPUTS = [("y_prompt", (1, PROMPT, D)), ("y_sample", (1, SAMPLE, D)), ("conv_p", (1, 1, HIST, CONV_CH)), ("delta_p", (1, 1, HV, DK, DV)),
           ("k_p", (1, WINDOW, HKV, HD)), ("v_p", (1, WINDOW, HKV, HD)), ("conv_s", (1, 1, HIST, CONV_CH)), ("delta_s", (1, 1, HV, DK, DV)),
           ("k_s", (1, SAMPLE, HKV, HD)), ("v_s", (1, SAMPLE, HKV, HD))]


def build(nc, io):
    with ExitStack() as keep:
        sb = lambda name, shape, dt=F32: keep.enter_context(nc.sbuf_tensor(name, shape, dt))
        m = {"const": sb("const", [P, CONST_W]), "gains": sb("gains", [P, N_GAINS]), "convw": sb("convw", [P, CONV_W, 32]),
             "hist": sb("hist", [P, HIST, 32]), "tail": sb("tail", [P, 2, HIST, 32]), "eps": sb("eps", [P, 1]),
             "gdn_a_log": sb("a_log", [P, HV]), "gdn_dt_bias": sb("dt_bias", [P, HV]), "swa_sinks": sb("sinks", [P, HQ]),
             "xT": sb("xT", [P, KD, TOK])}
        m["rows_dram"] = nc.dram_tensor("decay_rows", (2, HV, TOK), F32).ap()
        m["proj_dram"] = nc.dram_tensor("projected", (CONV_CH // P + HV, P, TOK), F32).ap()
        m["o_dram"] = nc.dram_tensor("head_outputs", (HV, P, TOK), F32).ap()
        load_stage(nc, m, io)
        with nc.sbuf_tensor("cols", [P, NT, HV, N_COL], F32) as cols:
            m["cols"] = cols
            with nc.sbuf_tensor("hT", [P, KD, TOK], F32) as hT:
                norm_stage(nc, m, "norm0", [(hT, G_ATTN0)])
                gates_stage(nc, m, hT, io)
                project_stage(nc, m, hT, io)
            with nc.Fori(0, GROUPS // CHAINS) as pas:
                delta_stage(nc, m, io, pas)
        with nc.sbuf_tensor("og", [P, HV, TOK], F32) as og:
            mix_stage(nc, m, og)
            w_out = io["gdn_w_out"][0]
            add_product_stage(nc, m, "mixout", og, HV, lambda to, t: [(to, w_out[:, bass.ds(t * P, P)].rearrange("(k p) c -> p k c", p=P))])
        tails_stage(nc, m, io)
        rest_stages(nc, m, io)


def kernel(**inputs):
    from concourse import bacc
    from concourse.bass_utils import run_bass_kernel_spmd

    nc = bacc.Bacc("TRN2", target_bir_lowering=False, num_devices=1)
    arrays = {f"in_{n}": np.ascontiguousarray(inputs[n]) for n in INPUTS}
    arrays["in_consts"], arrays["in_rope"] = constants(), rope_tables()
    io = {n[3:]: nc.dram_tensor(n, a.shape, mybir.dt.from_np(a.dtype), kind="ExternalInput").ap() for n, a in arrays.items()}
    for n, shape in OUTPUTS:
        io[n] = nc.dram_tensor(f"out_{n}", shape, F32, kind="ExternalOutput").ap()
    build(nc, io)
    r = run_bass_kernel_spmd(nc, [arrays], core_ids=[0])
    return tuple(r.results[0][f"out_{n}"] for n, _ in OUTPUTS)
```

```python
from contextlib import ExitStack

import numpy as np

import concourse.bass as bass
from concourse import mybir

F32 = mybir.dt.float32
F32R = mybir.dt.float32r
I32 = mybir.dt.int32
U32 = mybir.dt.uint32
ACT = mybir.ActivationFunctionType
ALU = mybir.AluOpType
AX = mybir.AxisListType

P = 128
D = 1024
KD = D // P
PROMPT = 1024
SAMPLE = 64
TOK = PROMPT + SAMPLE
CHUNK = 64
TILES = [(s, min(P, TOK - s)) for s in range(0, TOK, P)]
NT = len(TILES)
BLK = [(0, 384), (384, 384), (768, 320)]
EPS = 1e-6

HK, HV, DK, DV = 8, 16, 128, 128
QK_DIM = HK * DK
V_DIM = HV * DV
CONV_CH = 2 * QK_DIM + V_DIM
CONV_W = 4
HIST = CONV_W - 1
PADW = HIST + PROMPT + HIST + SAMPLE
GROUPS = 4
GH = HV // GROUPS
GK = HK // GROUPS

HQ, HKV, HD = 16, 4, 64
WINDOW = 128
D_FF = 2816
KF = D_FF // P
NE = 8

G_ATTN0, G_ATTN1, G_FFN0, G_FFN1, G_KV, G_FINAL, G_ONORM = 0, 8, 16, 24, 32, 40, 48
N_GAINS = 49
LEVELS = (1, 2, 4, 8, 16, 32)
C_ID, C_ONES, C_INCL, C_LAST, C_ROT, C_STRICT = 0, 1, 2, 3, 4, 5
C_LVL = 6
N_CONST = C_LVL + len(LEVELS)
CONST_W = N_CONST * P + 16
K_GC, K_BETA, K_NGB, K_KDEC = 0, 1, 2, 3
N_COL = 4


def constants():
    j, i = np.indices((P, P))
    same = j // CHUNK == i // CHUNK
    c = np.zeros((N_CONST, P, P), np.float32)
    c[C_ID] = j == i
    c[C_ONES] = 1
    c[C_INCL] = same & (j <= i)
    c[C_LAST] = same & (j % CHUNK == CHUNK - 1)
    r, f = j % HD, i % HD
    half = HD // 8
    c[C_ROT] = (j // HD == i // HD) * ((f < half) * (r == f + half) * -1.0 + ((f >= half) & (f < 2 * half)) * (r == f - half))
    c[C_STRICT] = j < i
    for n, s in enumerate(LEVELS):
        c[C_LVL + n] = (j // (2 * s) == i // (2 * s)) & (j % (2 * s) < s) & (i % (2 * s) >= s)
    tail = np.zeros((P, 16), np.float32)
    tail[:, 0:NE] = NE - np.arange(NE)
    tail[:, NE] = np.arange(P)
    return np.concatenate([c.transpose(1, 0, 2).reshape(P, N_CONST * P), tail], axis=1)


def rope_tables():
    half = HD // 8
    inv = np.power(np.float32(500000.0), -np.arange(half, dtype=np.float32) * np.float32(2.0) / np.float32(2 * half))
    pos = np.concatenate([np.arange(PROMPT), 1024 + np.arange(SAMPLE)]).astype(np.float32)
    ang = (pos[:, None] * inv.astype(np.float32)[None, :]).astype(np.float32)
    t = np.zeros((2, P, TOK), np.float32)
    t[0] = 1
    for h in range(2):
        for f in range(2 * half):
            t[0, h * HD + f] = np.cos(ang[:, f % half])
            t[1, h * HD + f] = np.sin(ang[:, f % half])
    return t


PRE = 1


class Stage:

    def __init__(self, nc, name):
        self.nc, self.name, self.sems, self.pre = nc, name, [], []

    def __enter__(self):
        self.stack = ExitStack()
        return self

    def sb(self, name, shape, dt=F32):
        return self.stack.enter_context(self.nc.sbuf_tensor(f"{self.name}_{name}", shape, dt))

    def ps(self, name, shape, dt=F32):
        return self.stack.enter_context(self.nc.psum_tensor(f"{self.name}_{name}", shape, dt))

    def sem(self, name, pre=True):
        s = self.stack.enter_context(self.nc.semaphore(f"{self.name}_{name}"))
        self.sems.append(s)
        if pre:
            self.pre.append(s)
        return s

    def block(self):
        for s in self.pre:
            self.nc.gpsimd.sem_inc(s, PRE)
        self.nc.all_engine_barrier()
        return self.nc.Block()

    def __exit__(self, *exc):
        if exc[0] is None:
            for s in self.sems:
                self.nc.gpsimd.sem_clear(s)
        self.stack.close()


class Chain:

    def __init__(self, eng, sem, base=0):
        self.eng, self.sem, self.base, self.n = eng, sem, base, 0

    def __call__(self, ins):
        self.n += 1
        ins.then_inc(self.sem, 1)
        self.eng.wait_ge(self.sem, PRE + self.base + self.n)


def hold(eng, passed):
    eng.sem_inc(passed, 1)


def as_r(a):
    return a.bitcast(F32R)


def split_product(pe, out, w_hi, w_lo, x_hi, x_lo, first, last):
    pe.matmul(out, as_r(w_hi), as_r(x_hi), start=first, stop=False)
    pe.matmul(out, as_r(w_hi), as_r(x_lo), start=False, stop=False)
    return pe.matmul(out, as_r(w_lo), as_r(x_hi), start=False, stop=last)


def split_weights(eng, w, w_hi, w_lo, rounded, split, nth):
    eng.tensor_copy(as_r(w_hi), w).then_inc(rounded, 1)
    eng.wait_ge(rounded, PRE + nth + 1)
    eng.tensor_tensor(as_r(w_lo), w, w_hi, ALU.subtract).then_inc(split, 1)


def load_stage(nc, m, io):
    with Stage(nc, "load") as st:
        rows = st.sb("rows", [N_GAINS, P])
        crow = st.sb("crow", [P, P])
        hrow = st.sb("hrow", [HIST * 32, P])
        xin = st.sb("xin", [P, 2, D])
        pt = st.ps("pt", [P, 2, 2, 512])
        pg = st.ps("pg", [P, 512])
        small, xl = st.sem("small_loaded"), [st.sem(f"frames_loaded{i}") for i in range(2)]
        turned, copied, gturn, mset = st.sem("tile_turned"), st.sem("tile_copied"), st.sem("gains_turned"), st.sem("eps_set")
        tiles_x = [io["x_prompt"][0, s:s + n, :] if s < PROMPT else io["x_sample"][0, :, :] for s, n in TILES]
        with st.block() as block:
            @block.sync
            def _(sp):
                sp.dma_start(m["const"][:, :], io["consts"]).then_inc(small, 16)
                for gain, at in (("norm_attn", G_ATTN0), ("norm_ffn", G_FFN0)):
                    sp.dma_start(rows[at:at + 16, :], io[gain].rearrange("l (k p) -> (l k) p", p=P)).then_inc(small, 16)
                for gain, at in (("kv_norm", G_KV), ("final_norm", G_FINAL)):
                    sp.dma_start(rows[at:at + 8, :], io[gain].rearrange("(k p) -> k p", p=P)).then_inc(small, 16)
                sp.dma_start(rows[G_ONORM:G_ONORM + 1, :], io["gdn_o_norm"]).then_inc(small, 16)
                sp.dma_start(crow[:, :], io["gdn_w_conv"][0].rearrange("j (t p) -> (j t) p", p=P)).then_inc(small, 16)
                sp.dma_start(hrow[:, :], io["cache_conv"][0, 0].rearrange("j (t p) -> (j t) p", p=P)).then_inc(small, 16)
                for name in ("gdn_a_log", "gdn_dt_bias", "swa_sinks"):
                    sp.dma_start(m[name][:, :], io[name].broadcast_to([P, 16])).then_inc(small, 16)
                for t, (s, n) in enumerate(TILES):
                    if t >= 2:
                        sp.wait_ge(turned, PRE + 2 * (t - 1))
                    sp.dma_start(xin[0:n, t % 2, :], tiles_x[t]).then_inc(xl[t % 2], 16)

            @block.tensor
            def _(pe):
                pe.wait_ge(small, PRE + 16 * 11)
                ident = m["const"][:, 0:P]
                pe.transpose(pg[:, 0:N_GAINS], rows[:, :], ident[0:N_GAINS, 0:N_GAINS])
                pe.transpose(pg[:, 64:64 + P], crow[:, :], ident)
                pe.transpose(pg[:, 192:192 + HIST * 32], hrow[:, :], ident[0:96, 0:96]).then_inc(gturn, 1)
                for t, (s, n) in enumerate(TILES):
                    pe.wait_ge(xl[t % 2], PRE + 16 * (t // 2 + 1))
                    for h in range(2):
                        if t >= 1:
                            pe.wait_ge(copied, PRE + 2 * (t - 1) + h + 1)
                        for k in range(4):
                            last = pe.transpose(pt[:, h, 0, k * P:k * P + n], xin[0:n, t % 2, (4 * h + k) * P:(4 * h + k + 1) * P], ident[0:n, 0:n])
                        last.then_inc(turned, 1)

            @block.vector
            def _(dve):
                dve.memset(m["eps"][:, :], EPS).then_inc(mset, 1)
                dve.wait_ge(gturn, PRE + 1)
                dve.tensor_copy(m["gains"][:, :], pg[:, 0:N_GAINS])
                dve.tensor_copy(m["convw"][:, :, :], pg[:, 64:64 + P].rearrange("p (j t) -> p j t", j=4))
                dve.tensor_copy(m["hist"][:, :, :], pg[:, 192:192 + 96].rearrange("p (j t) -> p j t", j=3))
                for t, (s, n) in enumerate(TILES):
                    for h in range(2):
                        dve.wait_ge(turned, PRE + 2 * t + h + 1)
                        dve.tensor_copy(m["xT"][:, 4 * h:4 * h + 4, s:s + n], pt[:, h, 0, :].rearrange("p (k c) -> p k c", c=P)[:, :, 0:n]).then_inc(copied, 1)


def norm_stage(nc, m, name, out, gain, halves=False, rinv=None, known=False):
    with Stage(nc, name) as st:
        sq = None if known else st.sb("sq", [P, 2, 2, TOK])
        logs = None if known else st.sb("logs", [P, TOK])
        rinv = rinv if rinv is not None else st.sb("rinv", [P, TOK])
        h = st.sb("h", [P, 2, TOK]) if halves else None
        acc = st.ps("acc", [P, 3, 512])
        squared, paired, summed, logged, inverted, normed, rounded, lowered = (st.sem(s) for s in (
            "squared", "paired", "summed", "logged", "inverted", "normed", "rounded", "lowered"))
        with st.block() as block:
            @block.scalar
            def _(act):
                if not known:
                    for k in range(KD):
                        if k >= 4:
                            act.wait_ge(summed, PRE + k // 2 - 1)
                        act.activation(sq[:, k // 2 % 2, k % 2, :], m["xT"][:, k, :], ACT.Square).then_inc(squared, 1)
                    act.wait_ge(summed, PRE + KD // 2)
                    for b, (s, n) in enumerate(BLK):
                        act.activation(logs[:, s:s + n], acc[:, b, 0:n], ACT.Ln, bias=m["eps"][:, :], scale=1.0 / D).then_inc(logged, 1)
                    act.wait_ge(logged, PRE + len(BLK))
                    act.activation(rinv[:, :], logs[:, :], ACT.Exp, scale=-0.5).then_inc(inverted, 1)
                if halves:
                    for k in range(KD):
                        act.wait_ge(normed, PRE + k + 1)
                        act.activation(as_r(out[:, 0, k, :]), h[:, k % 2, :], ACT.Copy).then_inc(rounded, 1)

            @block.tensor
            def _(pe):
                for j in range(0 if known else KD // 2):
                    pe.wait_ge(paired, PRE + j + 1)
                    for b, (s, n) in enumerate(BLK):
                        last = pe.matmul(acc[:, b, 0:n], m["const"][:, C_ONES * P:(C_ONES + 1) * P], sq[:, j % 2, 0, s:s + n],
                                         start=(j == 0), stop=(j == KD // 2 - 1))
                    last.then_inc(summed, 1)

            @block.vector
            def _(dve):
                if not known:
                    for j in range(KD // 2):
                        dve.wait_ge(squared, PRE + 2 * j + 2)
                        dve.tensor_tensor(sq[:, j % 2, 0, :], sq[:, j % 2, 0, :], sq[:, j % 2, 1, :], ALU.add).then_inc(paired, 1)
                    dve.wait_ge(inverted, PRE + 1)
                for k in range(KD + 1):
                    if halves and 2 <= k < KD:
                        dve.wait_ge(lowered, PRE + k - 1)
                    if k < KD:
                        to = h[:, k % 2, :] if halves else out[:, k, :]
                        dve.scalar_tensor_tensor(out=to, in0=m["xT"][:, k, :], scalar=m["gains"][:, gain + k:gain + k + 1],
                                                 in1=rinv[:, :], op0=ALU.mult, op1=ALU.mult).then_inc(normed, 1)
                    if halves and k:
                        dve.wait_ge(rounded, PRE + k)
                        dve.tensor_tensor(as_r(out[:, 1, k - 1, :]), h[:, (k - 1) % 2, :], out[:, 0, k - 1, :], ALU.subtract).then_inc(lowered, 1)


def gates_stage(nc, m, hT, io):
    with Stage(nc, "gates") as st:
        wba, wba_hi, wba_lo = (st.sb(n, [P, KD, 2 * HV]) for n in ("wba", "wba_hi", "wba_lo"))
        ba = st.sb("ba", [P, NT, 2, HV])
        beta, xa, t0, t1, g, gc = (st.sb(n, [P, NT, HV]) for n in ("beta", "xa", "t0", "t1", "g", "gc"))
        ea = st.sb("ea", [P, HV])
        rows = st.sb("rows", [HV, 2, TOK])
        pba = st.ps("pba", [P, NT, 2, HV])
        pgc, pgl = st.ps("pgc", [P, NT, HV]), st.ps("pgl", [P, NT, HV])
        prow = st.ps("prow", [HV, 3, 512])
        w_loaded, proj, dv, av = (st.sem(s) for s in ("w_loaded", "projected", "vector", "scalar"))
        w_rounded, w_split = st.sem("w_rounded"), st.sem("w_split")
        cum, turned, emptied, stored, own = (st.sem(s) for s in ("cumulated", "turned", "emptied", "stored", "vector_own"))
        cst = lambda n: m["const"][:, n * P:(n + 1) * P]
        with st.block() as block:
            @block.sync
            def _(sp):
                sp.dma_start(wba[:, :, :], io["gdn_w_in"][0][:, CONV_CH + V_DIM:].rearrange("(k p) c -> p k c", p=P)).then_inc(w_loaded, 16)
                sp.wait_ge(emptied, PRE + 6)
                sp.dma_start(m["rows_dram"].rearrange("a h t -> h a t"), rows[:, :, :]).then_inc(stored, 16)
                sp.wait_ge(stored, PRE + 16)

            @block.tensor
            def _(pe):
                pe.wait_ge(w_split, PRE + 1)
                for t, (s, n) in enumerate(TILES):
                    for k in range(KD):
                        last = split_product(pe, pba[0:n, t, :, :], hT[:, 0, k, s:s + n], hT[:, 1, k, s:s + n], wba_hi[:, k, :], wba_lo[:, k, :], k == 0, k == KD - 1)
                last.then_inc(proj, 1)
                pe.wait_ge(dv, PRE + 6)
                pe.matmul(pgc[:, :, :], cst(C_INCL), g[:, :, :], start=True, stop=True).then_inc(cum, 1)
                pe.wait_ge(dv, PRE + 7)
                pe.matmul(pgl[:, :, :], cst(C_LAST), gc[:, :, :], start=True, stop=True).then_inc(cum, 1)
                for a, src in enumerate((gc, beta)):
                    for b in range(3):
                        if a:
                            pe.wait_ge(emptied, PRE + b + 1)
                        for t in range(3 * b, 3 * b + 3):
                            s, n = TILES[t]
                            last = pe.transpose(prow[:, b, (t % 3) * P:(t % 3) * P + n], src[0:n, t, :], cst(C_ID)[0:n, 0:n])
                        last.then_inc(turned, 1)

            @block.scalar
            def _(act):
                acts = Chain(act, av)
                act.activation(ea[:, :], m["gdn_a_log"][:, :], ACT.Exp)
                act.wait_ge(dv, PRE + 1)
                acts(act.activation(beta[:, :, :], ba[:, :, 0, :], ACT.Exp, scale=-1.0))
                act.wait_ge(dv, PRE + 3)
                acts(act.activation(t0[:, :, :], t0[:, :, :], ACT.Exp, scale=-1.0))
                acts(act.activation(t0[:, :, :], t0[:, :, :], ACT.Ln, bias=1.0))
                act.wait_ge(dv, PRE + 8)
                acts(act.activation(m["cols"][:, :, :, K_KDEC], t1[:, :, :], ACT.Exp))
                acts(act.activation(t0[:, :, :], gc[:, :, :], ACT.Exp))

            @block.vector
            def _(dve):
                v = Chain(dve, dv)
                w = Chain(dve, own)
                w(dve.memset(ba[:, :, :, :], 0.0))
                dve.wait_ge(w_loaded, PRE + 16)
                split_weights(dve, wba[:, :, :], wba_hi[:, :, :], wba_lo[:, :, :], w_rounded, w_split, 0)
                dve.wait_ge(proj, PRE + 1)
                dve.tensor_copy(ba[:, 0:NT - 1, :, :], pba[:, 0:NT - 1, :, :])
                v(dve.tensor_copy(ba[0:64, NT - 1, :, :], pba[0:64, NT - 1, :, :]))
                v(dve.tensor_tensor(xa[:, :, :], ba[:, :, 1, :], m["gdn_dt_bias"][:, :].unsqueeze(1).broadcast_to([P, NT, HV]), ALU.add))
                w(dve.tensor_scalar(t1[:, :, :], xa[:, :, :], -1.0, None, ALU.mult))
                v(dve.tensor_tensor(t0[:, :, :], xa[:, :, :], t1[:, :, :], ALU.max))
                dve.wait_ge(av, PRE + 1)
                w(dve.tensor_scalar(beta[:, :, :], beta[:, :, :], 1.0, None, ALU.add))
                v(dve.reciprocal(beta[:, :, :], beta[:, :, :]))
                dve.wait_ge(av, PRE + 3)
                v(dve.scalar_tensor_tensor(out=t1[:, :, :], in0=xa[:, :, :], scalar=0.0, in1=t0[:, :, :], op0=ALU.max, op1=ALU.add))
                v(dve.scalar_tensor_tensor(out=g[:, :, :], in0=t1[:, :, :], scalar=-1.0, in1=ea[:, :].unsqueeze(1).broadcast_to([P, NT, HV]), op0=ALU.mult, op1=ALU.mult))
                dve.wait_ge(cum, PRE + 1)
                v(dve.tensor_copy(gc[:, :, :], pgc[:, :, :]))
                dve.wait_ge(cum, PRE + 2)
                v(dve.tensor_tensor(t1[:, :, :], pgl[:, :, :], gc[:, :, :], ALU.subtract))
                dve.tensor_copy(m["cols"][:, :, :, K_GC], gc[:, :, :])
                dve.tensor_copy(m["cols"][:, :, :, K_BETA], beta[:, :, :])
                dve.wait_ge(av, PRE + 5)
                dve.scalar_tensor_tensor(out=m["cols"][:, :, :, K_NGB], in0=t0[:, :, :], scalar=-1.0, in1=beta[:, :, :], op0=ALU.mult, op1=ALU.mult)
                for a in range(2):
                    for b in range(3):
                        dve.wait_ge(turned, PRE + 3 * a + b + 1)
                        s, n = BLK[b]
                        dve.tensor_copy(rows[:, a, s:s + n], prow[:, b, 0:n]).then_inc(emptied, 1)


def project_stage(nc, m, hT, io):
    NC, NQK = CONV_CH // P, 2 * HK
    N = NC + HV
    PW = PADW - HIST
    with Stage(nc, "proj") as st:
        w, w_hi, w_lo = (st.sb(n, [P, 2, KD, P]) for n in ("w", "w_hi", "w_lo"))
        xpad, acc = st.sb("xpad", [P, 2, PADW]), st.sb("acc", [P, 2, PADW])
        out, sq, rinv = st.sb("out", [P, 2, TOK]), st.sb("sq", [P, 2, TOK]), st.sb("rinv", [P, 2, TOK])
        cw = st.sb("cw", [P, 2, CONV_W])
        pm = st.ps("pm", [P, 2, 3, 512])
        pn = st.ps("pn", [P, 2, 512])
        two = lambda n: [st.sem(f"{n}{u}") for u in range(2)]
        w_loaded, done, emptied, conved, silued, kept, hist_set, squared, inverted, united, stored = (two(n) for n in (
            "w_loaded", "tile_summed", "tile_emptied", "convolved", "silued", "tails_kept", "hist_set", "squared", "inverted", "united", "stored"))
        w_rounded, w_split = two("w_rounded"), two("w_split")
        zeroed, nsummed, rooted, own = (st.sem(n) for n in ("pad_zeroed", "norms_summed", "rooted", "vector_step"))
        dram = m["proj_dram"]
        with st.block() as block:
            @block.sync
            def _(sp):
                def store(i, u, ready):
                    sp.wait_ge(ready[u], PRE + i + 1)
                    sp.dma_start(dram[bass.ds(2 * i + u, 1)].rearrange("o p t -> p (o t)"), out[:, u, :]).then_inc(stored[u], 16)

                with sp.Fori(0, NQK // 2) as i:
                    for u in range(2):
                        store(i, u, united)
                with sp.Fori(NQK // 2, N // 2) as i:
                    for u in range(2):
                        store(i, u, silued)
                for u in range(2):
                    sp.wait_ge(stored[u], PRE + 16 * (N // 2))

            @block.tensor
            def _(pe):
                def product(i, u, norms_of=None):
                    pe.wait_ge(w_split[u], PRE + i + 1)
                    pe.wait_ge(emptied[u], PRE + i)
                    for k in range(KD):
                        if k == 1 and norms_of is not None:
                            norms(*norms_of, (2,))
                        for b, (c, n) in enumerate(BLK):
                            last = split_product(pe, pm[:, u, b, 0:n], w_hi[:, u, k, :], w_lo[:, u, k, :], hT[:, 0, k, c:c + n], hT[:, 1, k, c:c + n], k == 0, k == KD - 1)
                    last.then_inc(done[u], 1)

                def norms(i, u, blocks):
                    pe.wait_ge(squared[u], PRE + i + 1)
                    for b in blocks:
                        c, n = BLK[b]
                        pe.wait_ge(rooted, PRE + 6 * i + 3 * u + max(b - 1, 0))
                        pe.matmul(pn[:, (3 * u + b) % 2, 0:n], m["const"][:, C_ONES * P:(C_ONES + 1) * P], sq[:, u, c:c + n],
                                  start=True, stop=True).then_inc(nsummed, 1)

                product(0, 0)
                product(0, 1)
                norms(0, 0, (0, 1))
                with pe.Fori(1, NQK // 2) as i:
                    product(i, 0, (i - 1, 0))
                    norms(i - 1, 1, (0, 1))
                    product(i, 1, (i - 1, 1))
                    norms(i, 0, (0, 1))
                product(NQK // 2, 0, (NQK // 2 - 1, 0))
                norms(NQK // 2 - 1, 1, (0, 1))
                product(NQK // 2, 1, (NQK // 2 - 1, 1))
                with pe.Fori(NQK // 2 + 1, N // 2) as i:
                    for u in range(2):
                        product(i, u)

            @block.gpsimd
            def _(pool):
                def history(i, u):
                    t = 2 * i + u
                    pool.wait_ge(conved[u], PRE + i)
                    pool.tensor_copy(xpad[:, u, HIST + PROMPT:HIST + PROMPT + HIST], m["hist"][:, :, bass.ds(t, 1)].rearrange("p j o -> p (j o)"))
                    pool.tensor_copy(cw[:, u, :], m["convw"][:, :, bass.ds(t, 1)].rearrange("p j o -> p (j o)")).then_inc(hist_set[u], 1)
                    pool.wait_ge(emptied[u], PRE + i + 1)
                    pool.tensor_copy(m["tail"][:, 0, :, bass.ds(t, 1)].rearrange("p j o -> p (j o)"), xpad[:, u, PROMPT:PROMPT + HIST])
                    pool.tensor_copy(m["tail"][:, 1, :, bass.ds(t, 1)].rearrange("p j o -> p (j o)"), xpad[:, u, PADW - HIST:PADW]).then_inc(kept[u], 1)

                def lower(i, u):
                    pool.wait_ge(w_rounded[u], PRE + i + 1)
                    pool.tensor_tensor(as_r(w_lo[:, u, :, :]), w[:, u, :, :], w_hi[:, u, :, :], ALU.subtract).then_inc(w_split[u], 1)

                pool.memset(xpad[:, :, 0:HIST], 0.0).then_inc(zeroed, 1)
                lower(0, 0)
                lower(0, 1)
                with pool.Fori(0, NC // 2) as i:
                    for u in range(2):
                        history(i, u)
                        lower(i + 1, u)
                with pool.Fori(NC // 2 + 1, N // 2) as i:
                    for u in range(2):
                        lower(i, u)

            @block.scalar
            def _(act):
                def load(i, u):
                    act.dma_start(w[:, u, :, :], io["gdn_w_in"][0][:, bass.ds((2 * i + u) * P, P)].rearrange("(k p) c -> p k c", p=P)).then_inc(w_loaded[u], 16)

                def load_next(i, u):
                    act.wait_ge(w_split[u], PRE + i + 1)
                    load(i + 1, u)

                def round_next(i, u):
                    act.wait_ge(w_loaded[u], PRE + 16 * (i + 1))
                    act.wait_ge(done[u], PRE + i)
                    act.activation(as_r(w_hi[:, u, :, :]), w[:, u, :, :], ACT.Copy).then_inc(w_rounded[u], 1)

                def empty(i, u):
                    load_next(i, u)
                    act.wait_ge(done[u], PRE + i + 1)
                    act.wait_ge(conved[u], PRE + i)
                    act.wait_ge(kept[u], PRE + i)
                    act.activation(xpad[:, u, HIST:HIST + 768].rearrange("p (b c) -> p b c", b=2), pm[:, u, 0:2, 0:384], ACT.Copy)
                    act.activation(xpad[:, u, HIST + 768:HIST + PROMPT], pm[:, u, 2, 0:256], ACT.Copy)
                    act.activation(xpad[:, u, PADW - SAMPLE:PADW], pm[:, u, 2, 256:320], ACT.Copy).then_inc(emptied[u], 1)
                    round_next(i + 1, u)

                def silu(i, u):
                    act.wait_ge(conved[u], PRE + i + 1)
                    act.wait_ge(stored[u], PRE + 16 * i)
                    act.activation(out[:, u, 0:PROMPT], acc[:, u, 0:PROMPT], ACT.Silu)
                    act.activation(out[:, u, PROMPT:TOK], acc[:, u, PROMPT + HIST:PW], ACT.Silu).then_inc(silued[u], 1)

                def square(i, u):
                    act.wait_ge(silued[u], PRE + i + 1)
                    act.activation(sq[:, u, :], out[:, u, :], ACT.Square).then_inc(squared[u], 1)

                def roots(i, u):
                    for b, (c, n) in enumerate(BLK):
                        act.wait_ge(nsummed, PRE + 6 * i + 3 * u + b + 1)
                        act.wait_ge(united[u], PRE + i)
                        act.activation(rinv[:, u, c:c + n], pn[:, (3 * u + b) % 2, 0:n], ACT.Ln, bias=m["eps"][:, :]).then_inc(rooted, 1)
                    act.wait_ge(rooted, PRE + 6 * i + 3 * u + 3)
                    act.activation(rinv[:, u, :], rinv[:, u, :], ACT.Exp, scale=-0.5).then_inc(inverted[u], 1)

                def gate(i, u, more=True):
                    if more:
                        load_next(i, u)
                    act.wait_ge(done[u], PRE + i + 1)
                    act.wait_ge(stored[u], PRE + 16 * i)
                    act.activation(out[:, u, 0:768].rearrange("p (b c) -> p b c", b=2), pm[:, u, 0:2, 0:384], ACT.Silu)
                    act.activation(out[:, u, 768:TOK], pm[:, u, 2, 0:320], ACT.Silu).then_inc(emptied[u], 1)
                    if more:
                        round_next(i + 1, u)
                    act.wait_ge(emptied[u], PRE + i + 1)
                    act.sem_inc(silued[u], 1)

                for u in range(2):
                    load(0, u)
                for u in range(2):
                    round_next(0, u)
                empty(0, 0)
                silu(0, 0)
                square(0, 0)
                empty(0, 1)
                roots(0, 0)
                silu(0, 1)
                square(0, 1)
                with act.Fori(1, NQK // 2) as i:
                    empty(i, 0)
                    roots(i - 1, 1)
                    silu(i, 0)
                    square(i, 0)
                    empty(i, 1)
                    roots(i, 0)
                    silu(i, 1)
                    square(i, 1)
                empty(NQK // 2, 0)
                roots(NQK // 2 - 1, 1)
                silu(NQK // 2, 0)
                empty(NQK // 2, 1)
                silu(NQK // 2, 1)
                with act.Fori(NQK // 2 + 1, NC // 2) as i:
                    for u in range(2):
                        empty(i, u)
                        silu(i, u)
                with act.Fori(NC // 2, N // 2 - 1) as i:
                    for u in range(2):
                        gate(i, u)
                for u in range(2):
                    gate(N // 2 - 1, u, more=False)

            @block.vector
            def _(dve):
                def conv(i, u):
                    v = Chain(dve, own, 3 * (2 * i + u))
                    dve.wait_ge(emptied[u], PRE + i + 1)
                    dve.wait_ge(hist_set[u], PRE + i + 1)
                    dve.wait_ge(silued[u], PRE + i)
                    v(dve.tensor_scalar(acc[:, u, 0:PW], xpad[:, u, 0:PW], cw[:, u, 0:1], None, ALU.mult))
                    for j in range(1, CONV_W):
                        op = dve.scalar_tensor_tensor(out=acc[:, u, 0:PW], in0=xpad[:, u, j:j + PW], scalar=cw[:, u, j:j + 1],
                                                      in1=acc[:, u, 0:PW], op0=ALU.mult, op1=ALU.add)
                        if j < CONV_W - 1:
                            v(op)
                    op.then_inc(conved[u], 1)

                def unit(i, u, scale):
                    dve.wait_ge(inverted[u], PRE + i + 1)
                    dve.scalar_tensor_tensor(out=out[:, u, :], in0=out[:, u, :], scalar=scale, in1=rinv[:, u, :], op0=ALU.mult, op1=ALU.mult).then_inc(united[u], 1)

                Q, K = DK ** -0.5, 1.0
                dve.wait_ge(zeroed, PRE + 1)
                conv(0, 0)
                conv(0, 1)
                unit(0, 0, Q)
                with dve.Fori(1, HK // 2) as i:
                    conv(i, 0)
                    unit(i - 1, 1, Q)
                    conv(i, 1)
                    unit(i, 0, Q)
                conv(HK // 2, 0)
                unit(HK // 2 - 1, 1, Q)
                conv(HK // 2, 1)
                unit(HK // 2, 0, K)
                with dve.Fori(HK // 2 + 1, HK) as i:
                    conv(i, 0)
                    unit(i - 1, 1, K)
                    conv(i, 1)
                    unit(i, 0, K)
                conv(HK, 0)
                unit(HK - 1, 1, K)
                conv(HK, 1)
                with dve.Fori(HK + 1, NC // 2) as i:
                    for u in range(2):
                        conv(i, u)


ORDER = ("stage", "R0", "scores", "R1", "level0", "x1", "R2", "d1", "x2", "R3", "d2", "x3", "R4", "d3", "x4", "R5", "d4", "x5", "d5")
CHAINS = 2


def in_order(steps, rec, prep):
    for what in ORDER:
        for ch in range(CHAINS):
            if what[0] == "R":
                c, part = divmod(int(what[1]), 3)
                if rec is not None and c * CHUNK < rec[2]:
                    steps[f"R{part}"](ch, rec[0], rec[1], c)
            elif prep is not None:
                t, par, n = prep
                if what[0] in "xd":
                    steps[what[0]](ch, t, par, n, int(what[1]))
                else:
                    steps[what](ch, t, par, n)


def delta_tiles(eng, steps):
    in_order(steps, None, (0, 0, P))
    with eng.Fori(0, NT // 2 - 1) as i:
        for u in range(2):
            in_order(steps, (2 * i + u, u, P), (2 * i + u + 1, 1 - u, P))
    in_order(steps, (NT - 3, 0, P), (NT - 2, 1, P))
    in_order(steps, (NT - 2, 1, P), (NT - 1, 0, SAMPLE))
    in_order(steps, (NT - 1, 0, SAMPLE), None)


def delta_stage(nc, m, io, pas):
    proj = m["proj_dram"]
    with Stage(nc, "delta") as st:
        C = range(CHAINS)
        each = lambda n, shape: [st.sb(f"{n}{ch}", shape) for ch in C]
        gb = each("gb", [P, 2, 2, GH, P])
        kst, qst, vst = each("kst", [P, 2, GK, P]), each("qst", [P, 2, GK, P]), each("vst", [P, 2, GH, P])
        cst, egl = each("cst", [P, 2, GH, N_COL]), each("egl", [P, 2, GH, 2])
        attn, qg, kd, vb, TT, out = (each(n, [P, 2, GH, P]) for n in ("attn", "qg", "kd", "vb", "TT", "out"))
        dec, at, eg, X, T, rhs, vn = (each(n, [P, GH, P]) for n in ("dec", "at", "eg", "X", "T", "rhs", "vn"))
        BT = each("BT", [P, 2, GH, P])
        S = each("S", [P, 2, GH, DV])
        b_x, b_d, b_w, b_s = ([st.ps(f"{n}{ch}", [P, GH, P]) for ch in C] for n in ("bank_x", "bank_d", "bank_w", "bank_s"))
        names = ("rows_loaded0", "rows_loaded1", "qkv_loaded0", "qkv_loaded1", "state_set", "cols_staged", "v_turned", "k_turned", "scored",
                 "diffs", "dexp", "eg_ready", "attn_masked", "at_half", "attn_ready", "at_ready", "qg_ready", "vb_ready", "kd_ready", "lvl_masked", "x_summed",
                 "x_copied", "deltas", "T_new", "t_new", "ks_summed", "rhs_ready", "vn_summed", "vn_copied", "o_summed", "s_summed", "o_copied", "s_new",
                 "state_stored", "state_loaded", "out_stored0", "out_stored1")
        sems = [{n: st.sem(f"{n}_{ch}") for n in names} for ch in C]
        passed = st.sem("passed")
        cst_sq = lambda n, r: m["const"][0:r, n * P:n * P + r]
        over_heads = lambda a: a.unsqueeze(1).broadcast_to([a.shape[0], GH, a.shape[1]])
        group = lambda ch: 2 * pas + ch
        L = len(LEVELS)
        last_t = NT - 1
        is_first = lambda t: isinstance(t, int) and t == 0
        skip = lambda *a: None
        with st.block() as block:
            @block.sync
            def _(sp):
                def load(t, par, n):
                    for ch in C:
                        e, g = sems[ch], group(ch)
                        for dst, first, count in ((kst, HK + GK * g, GK), (qst, GK * g, GK), (vst, 2 * HK + GH * g, GH)):
                            sp.dma_start(dst[ch][:, par, :, 0:n], proj[bass.ds(first, count), :, bass.ds(t * P, n)].rearrange("h p t -> p h t")).then_inc(e[f"qkv_loaded{par}"], 16)
                        for a in range(2):
                            sp.dma_start(gb[ch][:, par, a, :, 0:n], m["rows_dram"][a, bass.ds(GH * g, GH), bass.ds(t * P, n)].unsqueeze(0)
                                         .broadcast_to([P, GH, n])).then_inc(e[f"rows_loaded{par}"], 16)

                def next_load(t, par, n):
                    for ch in C:
                        e = sems[ch]
                        sp.wait_ge(e["at_ready"], PRE + t - 1)
                        sp.wait_ge(e["eg_ready"], PRE + t - 1)
                        sp.wait_ge(e["o_summed"], PRE + 2 * (t - 1))
                    load(t, par, n)

                load(0, 0, P)
                load(1, 1, P)
                with sp.Fori(1, NT // 2) as i:
                    for u in range(2):
                        next_load(2 * i + u, u, P)
                next_load(last_t, 0, SAMPLE)
                for ch in C:
                    e, heads = sems[ch], bass.ds(GH * group(ch), GH)
                    sp.wait_ge(e["s_new"], PRE + 2 * last_t)
                    sp.dma_start(io["delta_p"][0, 0, heads].rearrange("h k v -> k h v"), S[ch][:, 0, :, :]).then_inc(e["state_stored"], 16)
                for ch in C:
                    e, heads = sems[ch], bass.ds(GH * group(ch), GH)
                    sp.wait_ge(e["state_stored"], PRE + 16)
                    sp.dma_start(S[ch][:, 0, :, :], io["state_delta"][0, 0, heads].rearrange("h k v -> k h v")).then_inc(e["state_loaded"], 16)
                for ch in C:
                    e, heads = sems[ch], bass.ds(GH * group(ch), GH)
                    sp.wait_ge(e["s_new"], PRE + 2 * last_t + 1)
                    sp.dma_start(io["delta_s"][0, 0, heads].rearrange("h k v -> k h v"), S[ch][:, 1, :, :]).then_inc(e["state_stored"], 16)
                for ch in C:
                    sp.wait_ge(sems[ch]["state_stored"], PRE + 32)

            @block.gpsimd
            def _(pool):
                def stage(ch, t, par, n):
                    e = sems[ch]
                    if not is_first(t):
                        pool.wait_ge(e["s_summed"], PRE + 2 * (t - 1))
                    pool.tensor_copy(cst[ch][:, par, :, :], m["cols"][:, bass.ds(t, 1), bass.ds(GH * group(ch), GH), :].rearrange("p o h c -> p (o h) c")).then_inc(e["cols_staged"], 1)

                def masks(ch, t, par, n, l):
                    e = sems[ch]
                    if l == 0:
                        pool.wait_ge(e["at_ready"], PRE + t + 1)
                    elif l <= 2:
                        pool.wait_ge(e["t_new"], PRE + t * L + l - 1)
                    else:
                        pool.wait_ge(e["x_summed"], PRE + t * L + l - 1)
                    pool.tensor_tensor(BT[ch][0:n, l % 2, :, 0:n], at[ch][0:n, :, 0:n], over_heads(cst_sq(C_LVL + l, n)), ALU.mult).then_inc(e["lvl_masked"], 1)

                def level0(ch, t, par, n):
                    e = sems[ch]
                    masks(ch, t, par, n, 0)
                    masks(ch, t, par, n, 1)
                    pool.wait_ge(e["attn_ready"], PRE + t + 1)
                    pool.tensor_tensor(attn[ch][0:n, par, :, 0:n], attn[ch][0:n, par, :, 0:n], over_heads(cst_sq(C_INCL, n)), ALU.mult).then_inc(e["attn_masked"], 1)

                def x(ch, t, par, n, l):
                    if l + 1 < L:
                        masks(ch, t, par, n, l + 1)

                for ch in C:
                    pool.memset(S[ch][:, 0, :, :], 0.0).then_inc(sems[ch]["state_set"], 1)
                delta_tiles(pool, {"stage": stage, "scores": skip, "level0": level0, "x": x, "d": skip, "R0": skip, "R1": skip, "R2": skip})

            @block.tensor
            def _(pe):
                ident = m["const"][:, 0:P]

                def stage(ch, t, par, n):
                    e = sems[ch]
                    pe.wait_ge(e["t_new"], PRE + t * L)
                    pe.wait_ge(e[f"qkv_loaded{par}"], PRE + 24 * t + 48 - 24 * par)
                    for h in range(GH):
                        last = pe.transpose(b_d[ch][0:n, h, :], vst[ch][:, par, h, 0:n], ident)
                    last.then_inc(e["v_turned"], 1)
                    for k in range(GK):
                        pe.matmul(b_x[ch][0:n, k, 0:n], kst[ch][:, par, k, 0:n], kst[ch][:, par, k, 0:n], start=True, stop=True)
                    for k in range(GK):
                        last = pe.matmul(b_x[ch][0:n, GK + k, 0:n], kst[ch][:, par, k, 0:n], qst[ch][:, par, k, 0:n], start=True, stop=True)
                    last.then_inc(e["scored"], 1)

                def scores(ch, t, par, n):
                    e = sems[ch]
                    pe.wait_ge(e["vb_ready"], PRE + t + 1)
                    for k in range(GK):
                        last = pe.transpose(b_d[ch][0:n, k, :], kst[ch][:, par, k, 0:n], ident)
                    last.then_inc(e["k_turned"], 1)

                def level0(ch, t, par, n):
                    e = sems[ch]
                    pe.wait_ge(e["attn_ready"], PRE + t + 1)
                    pe.wait_ge(e["lvl_masked"], PRE + t * L + 1)
                    for h in range(GH):
                        last = pe.matmul(b_x[ch][0:n, h, 0:n], BT[ch][0:n, 0, h, 0:n], cst_sq(C_ID, n), start=True, stop=True)
                    last.then_inc(e["x_summed"], 1)

                def x(ch, t, par, n, l):
                    e = sems[ch]
                    pe.wait_ge(e["lvl_masked"], PRE + t * L + l + 1)
                    pe.wait_ge(e["T_new"], PRE + t * (L - 1) + l)
                    for h in range(GH):
                        last = pe.matmul(b_x[ch][0:n, h, 0:n], BT[ch][0:n, l % 2, h, 0:n], T[ch][0:n, h, 0:n], start=True, stop=True)
                    last.then_inc(e["x_summed"], 1)

                def d(ch, t, par, n, l):
                    e = sems[ch]
                    if l == 1:
                        pe.wait_ge(e["kd_ready"], PRE + t + 1)
                    pe.wait_ge(e["x_copied"], PRE + t * (L - 1) + l)
                    pe.wait_ge(e["t_new"], PRE + t * L + l)
                    for h in range(GH):
                        if l < L - 1:
                            pe.matmul(b_x[ch][0:n, h, 0:n], TT[ch][0:n, par, h, 0:n], X[ch][0:n, h, 0:n], start=True, stop=True)
                        last = pe.matmul(b_d[ch][0:n, h, 0:n], X[ch][0:n, h, 0:n], TT[ch][0:n, par, h, 0:n], start=True, stop=True)
                    last.then_inc(e["deltas"], 1)

                def k_state(ch, t, par, c):
                    e, r = sems[ch], c * CHUNK
                    if isinstance(t, int) and t == last_t:
                        pe.wait_ge(e["state_loaded"], PRE + 16)
                    pe.wait_ge(e["s_new"], PRE + 2 * t + c)
                    pe.wait_ge(e["vn_copied"], PRE + 2 * t + c)
                    for h in range(GH):
                        last = pe.matmul(b_w[ch][r:r + CHUNK, h, :], kst[ch][:, par, h // 2, r:r + CHUNK], S[ch][:, c, h, :], start=True, stop=True)
                    last.then_inc(e["ks_summed"], 1)

                def v_new(ch, t, par, c):
                    e, r = sems[ch], c * CHUNK
                    pe.wait_ge(e["t_new"], PRE + (t + 1) * L)
                    pe.wait_ge(e["rhs_ready"], PRE + 2 * t + c + 1)
                    hold(pe, passed)
                    for h in range(GH):
                        last = pe.matmul(b_w[ch][r:r + CHUNK, h, :], TT[ch][r:r + CHUNK, par, h, r:r + CHUNK], rhs[ch][r:r + CHUNK, h, :], start=True, stop=True)
                    last.then_inc(e["vn_summed"], 1)

                def out_and_state(ch, t, par, c):
                    e, r = sems[ch], c * CHUNK
                    pe.wait_ge(e["qg_ready"], PRE + t + 1)
                    pe.wait_ge(e["o_copied"], PRE + 2 * t + c)
                    pe.wait_ge(e["vn_copied"], PRE + 2 * t + c + 1)
                    for h in range(GH):
                        last = pe.matmul(b_s[ch][:, h, :], kd[ch][r:r + CHUNK, par, h, :], vn[ch][r:r + CHUNK, h, :], start=True, stop=True)
                    last.then_inc(e["s_summed"], 1)
                    if ch == CHAINS - 1:
                        for other in C:
                            outputs(other, t, par, c)

                def outputs(ch, t, par, c):
                    e, r = sems[ch], c * CHUNK
                    pe.wait_ge(e["s_new"], PRE + 2 * t + c + 1)
                    pe.wait_ge(e["attn_masked"], PRE + t + 1)
                    for h in range(GH):
                        pe.matmul(b_s[ch][:, h, 0:CHUNK], S[ch][:, c, h, :], qg[ch][:, par, h, r:r + CHUNK], start=True, stop=False)
                        last = pe.matmul(b_s[ch][:, h, 0:CHUNK], vn[ch][r:r + CHUNK, h, :], attn[ch][r:r + CHUNK, par, h, r:r + CHUNK], start=False, stop=True)
                    last.then_inc(e["o_summed"], 1)

                for ch in C:
                    pe.wait_ge(sems[ch]["state_set"], PRE + 1)
                delta_tiles(pe, {"stage": stage, "scores": scores, "level0": level0, "x": x, "d": d, "R0": k_state, "R1": v_new, "R2": out_and_state})

            @block.scalar
            def _(act):
                def stage(ch, t, par, n):
                    e = sems[ch]
                    if not is_first(t):
                        act.wait_ge(e["s_new"], PRE + 2 * (t - 1))
                    act.wait_ge(e[f"rows_loaded{par}"], PRE + 16 * t + 32 - 16 * par)
                    for c in range(n // CHUNK):
                        act.activation(egl[ch][:, par, :, c:c + 1], gb[ch][:, par, 0, :, (c + 1) * CHUNK - 1:(c + 1) * CHUNK], ACT.Exp)
                    act.wait_ge(e["qg_ready"], PRE + t)
                    act.activation(eg[ch][:, :, 0:n], gb[ch][:, par, 0, :, 0:n], ACT.Exp).then_inc(e["eg_ready"], 1)
                    act.wait_ge(e["diffs"], PRE + t + 1)
                    act.activation(dec[ch][0:n, :, 0:n], dec[ch][0:n, :, 0:n], ACT.Exp).then_inc(e["dexp"], 1)

                def scores(ch, t, par, n):
                    e = sems[ch]
                    if not is_first(t):
                        act.wait_ge(e["s_summed"], PRE + 2 * (t - 1))
                    act.wait_ge(e["v_turned"], PRE + t + 1)
                    act.wait_ge(e["cols_staged"], PRE + t + 1)
                    for h in range(GH):
                        last = act.activation(vb[ch][0:n, par, h, :], b_d[ch][0:n, h, :], ACT.Copy, scale=cst[ch][0:n, par, h, K_BETA:K_BETA + 1])
                    last.then_inc(e["vb_ready"], 1)

                def level0(ch, t, par, n):
                    e = sems[ch]
                    act.wait_ge(e["k_turned"], PRE + t + 1)
                    for h in range(GH):
                        last = act.activation(kd[ch][0:n, par, h, :], b_d[ch][0:n, h // 2, :], ACT.Copy, scale=cst[ch][0:n, par, h, K_KDEC:K_KDEC + 1])
                    last.then_inc(e["kd_ready"], 1)

                def x(ch, t, par, n, l):
                    e = sems[ch]
                    act.wait_ge(e["x_summed"], PRE + t * L + l + 1)
                    act.activation(X[ch][0:n, :, 0:n], b_x[ch][0:n, :, 0:n], ACT.Copy).then_inc(e["x_copied"], 1)

                def v_copy(ch, t, par, c):
                    e, r = sems[ch], c * CHUNK
                    act.wait_ge(e["o_summed"], PRE + 2 * t + c)
                    act.wait_ge(e["vn_summed"], PRE + 2 * t + c + 1)
                    act.activation(vn[ch][r:r + CHUNK, :, :], b_w[ch][r:r + CHUNK, :, :], ACT.Copy).then_inc(e["vn_copied"], 1)

                def o_copy(ch, t, par, c):
                    if ch < CHAINS - 1:
                        return
                    for other in C:
                        e, r = sems[other], c * CHUNK
                        if c == 0:
                            act.wait_ge(e[f"out_stored{par}"], PRE + 8 * t - 8 * par)
                        act.wait_ge(e["o_summed"], PRE + 2 * t + c + 1)
                        act.activation(out[other][:, par, :, r:r + CHUNK], b_s[other][:, :, 0:CHUNK], ACT.Copy).then_inc(e["o_copied"], 1)
                        n = SAMPLE if isinstance(t, int) and t == last_t else P
                        if r + CHUNK == n:
                            act.wait_ge(e["o_copied"], PRE + 2 * t + c + 1)
                            act.dma_start(m["o_dram"][bass.ds(GH * group(other), GH), :, bass.ds(t * P, n)].rearrange("h p t -> p h t"),
                                          out[other][:, par, :, 0:n]).then_inc(e[f"out_stored{par}"], 16)

                delta_tiles(act, {"stage": stage, "scores": scores, "level0": level0, "x": x, "d": skip, "R0": skip, "R1": v_copy, "R2": o_copy})
                for ch in C:
                    act.wait_ge(sems[ch]["out_stored0"], PRE + 16 * ((NT + 1) // 2))
                    act.wait_ge(sems[ch]["out_stored1"], PRE + 16 * (NT // 2))

            @block.vector
            def _(dve):
                def stage(ch, t, par, n):
                    e = sems[ch]
                    dve.wait_ge(e["cols_staged"], PRE + t + 1)
                    dve.wait_ge(e[f"rows_loaded{par}"], PRE + 16 * t + 32 - 16 * par)
                    for h in range(GH):
                        last = dve.tensor_scalar(dec[ch][0:n, h, 0:n], gb[ch][0:n, par, 0, h, 0:n], cst[ch][0:n, par, h, K_GC:K_GC + 1], 0.0, ALU.subtract, ALU.min)
                    last.then_inc(e["diffs"], 1)

                def scores(ch, t, par, n):
                    e = sems[ch]
                    dve.wait_ge(e["dexp"], PRE + t + 1)
                    dve.wait_ge(e["lvl_masked"], PRE + L * t)
                    dve.wait_ge(e["scored"], PRE + t + 1)
                    pairs = lambda a: a[0:n, :, 0:n].rearrange("p (k two) c -> p k two c", two=2)
                    score = lambda k: b_x[ch][0:n, k:k + GK, 0:n].unsqueeze(2).broadcast_to([n, GK, 2, n])
                    dve.tensor_tensor(pairs(at[ch]), score(0), pairs(dec[ch]), ALU.mult).then_inc(e["at_half"], 1)
                    if not is_first(t):
                        dve.wait_ge(e["o_summed"], PRE + 2 * (t - 1))
                    dve.tensor_tensor(pairs(attn[ch][:, par]), score(GK), pairs(dec[ch]), ALU.mult).then_inc(e["attn_ready"], 1)
                    dve.wait_ge(e["at_half"], PRE + t + 1)
                    dve.tensor_tensor(at[ch][0:n, :, 0:n], at[ch][0:n, :, 0:n], gb[ch][0:n, par, 1, :, 0:n], ALU.mult).then_inc(e["at_ready"], 1)

                def level0(ch, t, par, n):
                    e = sems[ch]
                    dve.wait_ge(e["t_new"], PRE + t * L)
                    dve.wait_ge(e["lvl_masked"], PRE + t * L + 1)
                    dve.wait_ge(e["x_summed"], PRE + t * L + 1)
                    dve.tensor_tensor(T[ch][0:n, :, 0:n], over_heads(cst_sq(C_ID, n)), b_x[ch][0:n, :, 0:n], ALU.subtract).then_inc(e["T_new"], 1)
                    dve.tensor_tensor(TT[ch][0:n, par, :, 0:n], over_heads(cst_sq(C_ID, n)), BT[ch][0:n, 0, :, 0:n], ALU.subtract).then_inc(e["t_new"], 1)
                    if not is_first(t):
                        dve.wait_ge(e["o_summed"], PRE + 2 * (t - 1))
                    dve.wait_ge(e["eg_ready"], PRE + t + 1)
                    dve.wait_ge(e[f"qkv_loaded{par}"], PRE + 24 * t + 48 - 24 * par)
                    twice = lambda a: a.rearrange("p (k two) c -> p k two c", two=2)
                    dve.tensor_tensor(twice(qg[ch][:, par, :, 0:n]), qst[ch][:, par, :, 0:n].unsqueeze(2).broadcast_to([P, GK, 2, n]), twice(eg[ch][:, :, 0:n]), ALU.mult).then_inc(e["qg_ready"], 1)

                def d(ch, t, par, n, l):
                    e = sems[ch]
                    dve.wait_ge(e["t_new"], PRE + t * L + l)
                    dve.wait_ge(e["deltas"], PRE + t * (L - 1) + l)
                    if l < L - 1:
                        dve.tensor_tensor(T[ch][0:n, :, 0:n], T[ch][0:n, :, 0:n], b_x[ch][0:n, :, 0:n], ALU.subtract).then_inc(e["T_new"], 1)
                    dve.tensor_tensor(TT[ch][0:n, par, :, 0:n], TT[ch][0:n, par, :, 0:n], b_d[ch][0:n, :, 0:n], ALU.subtract).then_inc(e["t_new"], 1)

                def right_side(ch, t, par, c):
                    e, r = sems[ch], c * CHUNK
                    dve.wait_ge(e["vb_ready"], PRE + t + 1)
                    dve.wait_ge(e["ks_summed"], PRE + 2 * t + c + 1)
                    for h in range(GH):
                        last = dve.scalar_tensor_tensor(out=rhs[ch][r:r + CHUNK, h, :], in0=b_w[ch][r:r + CHUNK, h, :], scalar=cst[ch][r:r + CHUNK, par, h, K_NGB:K_NGB + 1],
                                                        in1=vb[ch][r:r + CHUNK, par, h, :], op0=ALU.mult, op1=ALU.add)
                    last.then_inc(e["rhs_ready"], 1)

                def new_state(ch, t, par, c):
                    e = sems[ch]
                    dve.wait_ge(e["s_summed"], PRE + 2 * t + c + 1)
                    for h in range(GH):
                        last = dve.scalar_tensor_tensor(out=S[ch][:, 1 - c, h, :], in0=S[ch][:, c, h, :], scalar=egl[ch][:, par, h, c:c + 1], in1=b_s[ch][:, h, :],
                                                        op0=ALU.mult, op1=ALU.add)
                    last.then_inc(e["s_new"], 1)

                delta_tiles(dve, {"stage": stage, "scores": scores, "level0": level0, "x": skip, "d": d, "R0": right_side, "R1": skip, "R2": new_state})


def mix_stage(nc, m):
    PAIRS = HV // 2
    with Stage(nc, "mix") as st:
        o, z, g, sq, rinv = (st.sb(n, [P, 2, 2, TOK]) for n in ("o", "z", "g", "sq", "rinv"))
        pm = st.ps("pm", [P, 2, 3, 512])
        two = lambda n: [st.sem(f"{n}{u}") for u in range(2)]
        loaded, squared, inverted, normed, gated, stored, emptied = (two(n) for n in (
            "loaded", "squared", "inverted", "normed", "gated", "stored", "emptied"))
        summed = [two(f"summed{h}_") for h in range(2)]
        heads = lambda t: t.rearrange("h p t -> p h t")
        with st.block() as block:
            @block.sync
            def _(sp):
                with sp.Fori(0, PAIRS // 2) as i:
                    for u in range(2):
                        sp.wait_ge(gated[u], PRE + i)
                        for dst, src, t in ((o, m["o_dram"], 4 * i + 2 * u), (z, m["proj_dram"], CONV_CH // P + 4 * i + 2 * u)):
                            sp.dma_start(dst[:, u, :, :], heads(src[bass.ds(t, 2)])).then_inc(loaded[u], 16)

            @block.gpsimd
            def _(pool):
                with pool.Fori(0, PAIRS // 2) as i:
                    for u in range(2):
                        pool.wait_ge(loaded[u], PRE + 32 * (i + 1))
                        pool.wait_ge(summed[1][u], PRE + i)
                        pool.tensor_tensor(sq[:, u, :, :], o[:, u, :, :], o[:, u, :, :], ALU.mult).then_inc(squared[u], 1)

            @block.tensor
            def _(pe):
                with pe.Fori(0, PAIRS // 2) as i:
                    for u in range(2):
                        pe.wait_ge(squared[u], PRE + i + 1)
                        for h in range(2):
                            pe.wait_ge(emptied[h], PRE + 2 * i + u)
                            for b, (c, n) in enumerate(BLK):
                                last = pe.matmul(pm[:, h, b, 0:n], m["const"][:, C_ONES * P:(C_ONES + 1) * P], sq[:, u, h, c:c + n], start=True, stop=True)
                            last.then_inc(summed[h][u], 1)

            @block.scalar
            def _(act):
                def store(i, u):
                    act.wait_ge(gated[u], PRE + i + 1)
                    act.dma_start(heads(m["og_dram"][bass.ds(4 * i + 2 * u, 2)]), g[:, u, :, :]).then_inc(stored[u], 16)

                def roots(i, u):
                    act.wait_ge(gated[u], PRE + i)
                    for h in range(2):
                        act.wait_ge(summed[h][u], PRE + i + 1)
                        for b, (c, n) in enumerate(BLK):
                            last = act.activation(rinv[:, u, h, c:c + n], pm[:, h, b, 0:n], ACT.Ln, bias=m["eps"][:, :], scale=1.0 / DV)
                        last.then_inc(emptied[h], 1)
                    act.wait_ge(emptied[1], PRE + 2 * i + u + 1)
                    act.activation(rinv[:, u, :, :], rinv[:, u, :, :], ACT.Exp, scale=-0.5).then_inc(inverted[u], 1)

                roots(0, 0)
                roots(0, 1)
                store(0, 0)
                with act.Fori(1, PAIRS // 2) as i:
                    roots(i, 0)
                    store(i - 1, 1)
                    roots(i, 1)
                    store(i, 0)
                store(PAIRS // 2 - 1, 1)
                for u in range(2):
                    act.wait_ge(stored[u], PRE + 16 * (PAIRS // 2))

            @block.vector
            def _(dve):
                with dve.Fori(0, PAIRS // 2) as i:
                    for u in range(2):
                        dve.wait_ge(inverted[u], PRE + i + 1)
                        dve.wait_ge(loaded[u], PRE + 32 * (i + 1))
                        dve.scalar_tensor_tensor(out=rinv[:, u, :, :], in0=o[:, u, :, :], scalar=m["gains"][:, G_ONORM:G_ONORM + 1], in1=rinv[:, u, :, :],
                                                 op0=ALU.mult, op1=ALU.mult).then_inc(normed[u], 1)
                        dve.wait_ge(stored[u], PRE + 16 * i)
                        dve.wait_ge(normed[u], PRE + i + 1)
                        dve.tensor_tensor(g[:, u, :, :], rinv[:, u, :, :], z[:, u, :, :], ALU.mult).then_inc(gated[u], 1)


def tails_stage(nc, m, io):
    with Stage(nc, "tails") as st:
        rows = st.sb("rows", [HIST * 32, 2, P])
        pt = st.ps("pt", [HIST * 32, 2, P])
        turned, copied, stored = st.sem("turned"), st.sem("copied"), st.sem("stored")
        with st.block() as block:
            @block.tensor
            def _(pe):
                for a in range(2):
                    last = pe.transpose(pt[:, a, :], m["tail"][:, a, :, :].rearrange("p j t -> p (j t)"), m["const"][:, 0:P])
                last.then_inc(turned, 1)

            @block.vector
            def _(dve):
                dve.wait_ge(turned, PRE + 1)
                dve.tensor_copy(rows[:, :, :], pt[:, :, :]).then_inc(copied, 1)

            @block.sync
            def _(sp):
                sp.wait_ge(copied, PRE + 1)
                for a, name in enumerate(("conv_p", "conv_s")):
                    sp.dma_start(io[name][0, 0].rearrange("j (t p) -> (j t) p", p=P), rows[:, a, :]).then_inc(stored, 16)
                sp.wait_ge(stored, PRE + 32)


def blocks3(tile):
    return tile[:, 0:768].rearrange("p (b c) -> p b c", b=2), tile[:, 768:TOK]


def ffn_up_stage(nc, m, hT, w1, w3):
    with Stage(nc, "ffnup") as st:
        w, w_hi, w_lo = (st.sb(n, [P, 2, 2, KD, P]) for n in ("w", "w_hi", "w_lo"))
        silu, hid = st.sb("silu", [P, TOK]), st.sb("hid", [P, 2, TOK])
        pm = st.ps("pm", [P, 2, 3, 512])
        two = lambda n: [st.sem(f"{n}{u}") for u in range(2)]
        w_loaded, w_rounded, w_split, used, stored = (two(n) for n in ("w_loaded", "w_rounded", "w_split", "w_used", "stored"))
        a_done, silued, gated, passed = st.sem("a_done"), st.sem("silued"), st.sem("gated"), st.sem("passed")
        with st.block() as block:
            @block.sync
            def _(sp):
                with sp.Fori(0, KF // 2) as i:
                    for u in range(2):
                        sp.wait_ge(w_split[u], PRE + i)
                        for x, src in enumerate((w1, w3)):
                            sp.dma_start(w[:, u, x, :, :], src[:, bass.ds((2 * i + u) * P, P)].rearrange("(k p) c -> p k c", p=P)).then_inc(w_loaded[u], 16)

            @block.gpsimd
            def _(pool):
                with pool.Fori(0, KF // 2) as i:
                    for u in range(2):
                        pool.wait_ge(w_loaded[u], PRE + 32 * (i + 1))
                        pool.wait_ge(used[u], PRE + i)
                        hold(pool, passed)
                        split_weights(pool, w[:, u, :, :, :], w_hi[:, u, :, :, :], w_lo[:, u, :, :, :], w_rounded[u], w_split[u], i)

            @block.tensor
            def _(pe):
                with pe.Fori(0, KF // 2) as i:
                    for u in range(2):
                        pe.wait_ge(w_split[u], PRE + i + 1)
                        for x, (freed, done) in enumerate(((silued, a_done), (gated, used[u]))):
                            pe.wait_ge(freed, PRE + 2 * i + u)
                            for k in range(KD):
                                for b, (c, n) in enumerate(BLK):
                                    last = split_product(pe, pm[:, x, b, 0:n], w_hi[:, u, x, k, :], w_lo[:, u, x, k, :], hT[:, 0, k, c:c + n], hT[:, 1, k, c:c + n],
                                                         k == 0, k == KD - 1)
                            last.then_inc(done, 1)

            @block.scalar
            def _(act):
                with act.Fori(0, KF // 2) as i:
                    for u in range(2):
                        act.wait_ge(a_done, PRE + 2 * i + u + 1)
                        act.wait_ge(gated, PRE + 2 * i + u)
                        two, rest = blocks3(silu)
                        act.activation(two, pm[:, 0, 0:2, 0:384], ACT.Silu)
                        act.activation(rest, pm[:, 0, 2, 0:320], ACT.Silu).then_inc(silued, 1)
                        act.wait_ge(gated, PRE + 2 * i + u + 1)
                        act.dma_start(m["hid_dram"][bass.ds(2 * i + u, 1)].rearrange("o p t -> p (o t)"), hid[:, u, :]).then_inc(stored[u], 16)
                for u in range(2):
                    act.wait_ge(stored[u], PRE + 16 * (KF // 2))

            @block.vector
            def _(dve):
                with dve.Fori(0, KF // 2) as i:
                    for u in range(2):
                        dve.wait_ge(used[u], PRE + i + 1)
                        dve.wait_ge(silued, PRE + 2 * i + u + 1)
                        dve.wait_ge(stored[u], PRE + 16 * i)
                        two, rest = blocks3(hid[:, u, :])
                        stwo, srest = blocks3(silu)
                        dve.tensor_tensor(two, stwo, pm[:, 1, 0:2, 0:384], ALU.mult)
                        dve.tensor_tensor(rest, srest, pm[:, 1, 2, 0:320], ALU.mult).then_inc(gated, 1)


HALF = TOK // 2
HBLK = [(0, HALF // 2), (HALF // 2, HALF // 2)]
RAW = 4


def add_product_stage(nc, m, name, src, kt, load, parts=1, resident=False):
    xT = m["xT"]
    PAIRS, kh = KD // 2, kt // 2
    with Stage(nc, name) as st:
        w, w_hi, w_lo = (st.sb(n, [P, 2, kh, P]) for n in ("w", "w_hi", "w_lo"))
        x = st.sb("x", [P, 2, kt, HALF])
        raw = None if resident else st.sb("raw", [P, RAW, HALF])
        pm = st.ps("pm", [P, 2, 2, 512])
        two = lambda n: [st.sem(f"{n}{u}") for u in range(2)]
        w_loaded, w_rounded, w_split, w_used, added = (two(n) for n in ("w_loaded", "w_rounded", "w_split", "w_used", "tile_added"))
        src_loaded = [st.sem(f"src_loaded{r}") for r in range(RAW)]
        src_rounded, src_split, k_used = st.sem("src_rounded"), st.sem("src_split"), st.sem("k_used")
        piece = lambda h, k: src[:, k, h * HALF:(h + 1) * HALF] if resident else raw[:, (h * kt + k) % RAW, :]
        with st.block() as block:
            @block.sync
            def _(sp):
                def weights(h, t):
                    for p in range(2):
                        sp.wait_ge(w_split[p], PRE + KD * h + t)
                        for to, frm in load(w[:, p, :, :], t, p):
                            sp.dma_start(to, frm).then_inc(w_loaded[p], 16)

                def source(h):
                    for k in range(0 if resident else kt):
                        q = h * kt + k
                        if q >= RAW:
                            sp.wait_ge(src_split, PRE + q - RAW + 1)
                        sp.dma_start(raw[:, q % RAW, :], src[k, :, h * HALF:(h + 1) * HALF]).then_inc(src_loaded[q % RAW], 16)

                for h in range(2):
                    weights(h, 0)
                    source(h)
                    with sp.Fori(1, KD) as i:
                        weights(h, i)

            @block.gpsimd
            def _(pool):
                with pool.Fori(0, 2 * KD) as t:
                    for p in range(2):
                        pool.wait_ge(w_rounded[p], PRE + t + 1)
                        pool.tensor_tensor(as_r(w_lo[:, p, :, :]), w[:, p, :, :], w_hi[:, p, :, :], ALU.subtract).then_inc(w_split[p], 1)

            @block.tensor
            def _(pe):
                for h in range(2):
                    with pe.Fori(0, PAIRS) as i:
                        for u in range(2):
                            pe.wait_ge(added[u], PRE + PAIRS * h + i)
                            for k in range(kt):
                                p = k // kh
                                if k % kh == 0:
                                    pe.wait_ge(w_split[p], PRE + KD * h + 2 * i + u + 1)
                                pe.wait_ge(src_split, PRE + h * kt + k + 1)
                                for b, (c, n) in enumerate(HBLK):
                                    last = split_product(pe, pm[:, u, b, 0:n], w_hi[:, p, k % kh, :], w_lo[:, p, k % kh, :], x[:, 0, k, c:c + n], x[:, 1, k, c:c + n],
                                                         k == 0, k == kt - 1)
                                last.then_inc(w_used[p] if k % kh == kh - 1 else k_used, 1)

            @block.scalar
            def _(act):
                def weights(t, p):
                    act.wait_ge(w_loaded[p], PRE + 16 * parts * (t + 1))
                    act.wait_ge(w_used[p], PRE + t)
                    act.activation(as_r(w_hi[:, p, :, :]), w[:, p, :, :], ACT.Copy).then_inc(w_rounded[p], 1)

                for h in range(2):
                    for k in range(kt):
                        q = h * kt + k
                        if k % kh == 0:
                            weights(KD * h, k // kh)
                        if not resident:
                            act.wait_ge(src_loaded[q % RAW], PRE + 16 * (q // RAW + 1))
                        if h and k % kh < kh - 1:
                            act.wait_ge(k_used, PRE + (kt - 2) * (KD - 1) + k - k // kh + 1)
                        elif h:
                            act.wait_ge(w_used[k // kh], PRE + KD)
                        act.activation(as_r(x[:, 0, k, :]), piece(h, k), ACT.Copy).then_inc(src_rounded, 1)
                    with act.Fori(1, KD) as i:
                        for p in range(2):
                            weights(KD * h + i, p)

            @block.vector
            def _(dve):
                def split(h):
                    for k in range(kt):
                        dve.wait_ge(src_rounded, PRE + h * kt + k + 1)
                        dve.tensor_tensor(as_r(x[:, 1, k, :]), piece(h, k), x[:, 0, k, :], ALU.subtract).then_inc(src_split, 1)

                def add(h, i, u):
                    dve.wait_ge(w_used[1], PRE + KD * h + 2 * i + u + 1)
                    to = xT[:, bass.ds(2 * i + u, 1), h * HALF:(h + 1) * HALF].rearrange("p o (b t) -> p (o b) t", b=2)
                    dve.tensor_tensor(to, to, pm[:, u, :, 0:HALF // 2], ALU.add).then_inc(added[u], 1)

                split(0)
                with dve.Fori(0, PAIRS - 1) as i:
                    add(0, i, 0)
                    add(0, i, 1)
                add(0, PAIRS - 1, 0)
                split(1)
                add(0, PAIRS - 1, 1)
                with dve.Fori(0, PAIRS) as i:
                    add(1, i, 0)
                    add(1, i, 1)


K_CACHE = WINDOW + PROMPT
K_SAMPLE = K_CACHE + WINDOW
KEYS = K_SAMPLE + SAMPLE
KV_T = HKV * HD // P
VS = KEYS // CHUNK



def heads_stage(nc, m, name, hT, n_tiles, rotated, dests, loads, io):
    with Stage(nc, name) as st:
        w = st.sb("w", [P, 2, KD, 4 * P])
        rope = st.sb("rope", [P, 2, TOK])
        raw = st.sb("raw", [P, 2, TOK])
        sn = st.sb("sin_part", [P, TOK])
        pm = st.ps("pm", [P, 2, 3, 512])
        w_loaded = [st.sem(f"w_loaded{u}") for u in range(2)]
        rope_l, done, copied, turned, rot, ready = (st.sem(s) for s in ("rope_loaded", "tile_summed", "tile_copied", "swapped", "rotate_step", "tile_ready"))
        with st.block() as block:
            @block.sync
            def _(sp):
                sp.dma_start(rope[:, :, :], io["rope"].rearrange("a p t -> p a t")).then_inc(rope_l, 16)
                for s, load in enumerate(loads(w)):
                    for to, frm in load:
                        sp.dma_start(to, frm).then_inc(w_loaded[s], 16)

            @block.tensor
            def _(pe):
                def swap(t):
                    pe.wait_ge(copied, PRE + t + 1)
                    for b, (c, n) in enumerate(BLK):
                        last = pe.matmul(pm[:, t % 2, b, 0:n], m["const"][:, C_ROT * P:(C_ROT + 1) * P], raw[:, t % 2, c:c + n], start=True, stop=True)
                    last.then_inc(turned, 1)

                for t in range(n_tiles):
                    s = t // 4
                    if t % 4 == 0:
                        pe.wait_ge(w_loaded[s], PRE + 16 * len(loads(w)[s]))
                    if t >= 2:
                        pe.wait_ge(ready, PRE + t - 1)
                    for k in range(KD):
                        if k == 2 and 1 <= t <= rotated:
                            swap(t - 1)
                        for b, (c, n) in enumerate(BLK):
                            last = pe.matmul(pm[:, t % 2, b, 0:n], w[:, s, k, (t % 4) * P:(t % 4 + 1) * P], hT[:, k, c:c + n], start=(k == 0), stop=(k == KD - 1))
                    last.then_inc(done, 1)
                if rotated == n_tiles:
                    swap(n_tiles - 1)

            @block.scalar
            def _(act):
                for t in range(n_tiles):
                    act.wait_ge(done, PRE + t + 1)
                    if t >= 2:
                        act.wait_ge(ready, PRE + t - 1)
                    two, rest = blocks3(raw[:, t % 2, :])
                    act.activation(two, pm[:, t % 2, 0:2, 0:384], ACT.Copy)
                    act.activation(rest, pm[:, t % 2, 2, 0:320], ACT.Copy).then_inc(copied, 1)

            @block.vector
            def _(dve):
                dve.wait_ge(rope_l, PRE + 16)
                step = Chain(dve, rot)
                for t in range(n_tiles):
                    if t < rotated:
                        dve.wait_ge(turned, PRE + t + 1)
                        two, rest = blocks3(sn)
                        stwo, srest = blocks3(rope[:, 1, :])
                        dve.tensor_tensor(two, stwo, pm[:, t % 2, 0:2, 0:384], ALU.mult)
                        dve.tensor_tensor(rest, srest, pm[:, t % 2, 2, 0:320], ALU.mult)
                        step(dve.tensor_tensor(raw[:, t % 2, :], raw[:, t % 2, :], rope[:, 0, :], ALU.mult))
                        for to, c in dests(t):
                            n = to.shape[-1]
                            last = dve.tensor_tensor(to, raw[:, t % 2, c:c + n], sn[:, c:c + n], ALU.add)
                        last.then_inc(ready, 1)
                        dve.wait_ge(ready, PRE + t + 1)
                    else:
                        dve.wait_ge(copied, PRE + t + 1)
                        for to, c in dests(t):
                            n = to.shape[-1]
                            last = dve.tensor_copy(to, raw[:, t % 2, c:c + n])
                        last.then_inc(ready, 1)


def values_stage(nc, m, kT, vT, v128, io):
    with Stage(nc, "values") as st:
        ck = st.sb("ck", [P, HKV * HD])
        kout = st.sb("kout", [P, 2, HKV * HD])
        pv = st.ps("pv", [P, 2, 4, P])
        pk = st.ps("pk", [P, 4, P])
        loaded, turned, copied, kturned, kcopied, stored = (st.sem(s) for s in ("loaded", "v_turned", "v_copied", "k_turned", "k_copied", "stored"))
        wins = [(s, (s - 2) * CHUNK, P) for s in range(2, 17)] + [(17, PROMPT - CHUNK, CHUNK), (VS - 1, PROMPT, SAMPLE)]
        ident = m["const"][:, 0:P]
        with st.block() as block:
            @block.sync
            def _(sp):
                sp.dma_start(ck[:, :], io["cache_k"][0].rearrange("t h d -> t (h d)")).then_inc(loaded, 16)
                sp.dma_start(v128[:, VS - 3, :], io["cache_v"][0].rearrange("t h d -> t (h d)")).then_inc(loaded, 16)
                sp.wait_ge(kcopied, PRE + 3)
                sp.dma_start(io["k_p"][0].rearrange("t h d -> t (h d)"), kout[:, 0, :]).then_inc(stored, 16)
                sp.dma_start(io["k_s"][0].rearrange("t h d -> t (h d)"), kout[0:SAMPLE, 1, :]).then_inc(stored, 16)
                sp.wait_ge(copied, PRE + len(wins))
                sp.dma_start(io["v_p"][0].rearrange("t h d -> t (h d)"), v128[:, 16, :]).then_inc(stored, 16)
                sp.dma_start(io["v_s"][0].rearrange("t h d -> t (h d)"), v128[0:SAMPLE, VS - 1, :]).then_inc(stored, 16)
                sp.wait_ge(loaded, PRE + 32)
                sp.wait_ge(stored, PRE + 64)

            @block.tensor
            def _(pe):
                for i, (s, tok, n) in enumerate(wins):
                    if i >= 2:
                        pe.wait_ge(copied, PRE + i - 1)
                    for j in range(KV_T):
                        last = pe.transpose(pv[0:n, i % 2, j, :], vT[:, j, tok:tok + n], ident)
                    last.then_inc(turned, 1)
                pe.wait_ge(loaded, PRE + 32)
                for i in range(3):
                    if i:
                        pe.wait_ge(kcopied, PRE + i)
                    for j in range(KV_T):
                        last = (pe.transpose(pk[:, j, :], ck[:, j * P:(j + 1) * P], ident) if i == 0 else
                                pe.transpose(pk[:, j, :], kT[:, j, K_CACHE - WINDOW:K_CACHE], ident) if i == 1 else
                                pe.transpose(pk[0:SAMPLE, j, :], kT[:, j, K_SAMPLE:KEYS], ident))
                    last.then_inc(kturned, 1)

            @block.scalar
            def _(act):
                for i, (s, tok, n) in enumerate(wins):
                    act.wait_ge(turned, PRE + i + 1)
                    act.activation(v128[0:n, s, :].rearrange("p (j c) -> p j c", j=KV_T), pv[0:n, i % 2, 0:KV_T, :], ACT.Copy).then_inc(copied, 1)

            @block.vector
            def _(dve):
                for i, (to, n) in enumerate(((kT[:, :, K_CACHE:K_SAMPLE], P), (kout[:, 0, :].rearrange("p (j c) -> p j c", j=KV_T), P),
                                             (kout[0:SAMPLE, 1, :].rearrange("p (j c) -> p j c", j=KV_T), SAMPLE))):
                    dve.wait_ge(kturned, PRE + i + 1)
                    dve.tensor_copy(to, pk[0:n, 0:KV_T, :]).then_inc(kcopied, 1)


def attend_stage(nc, m, qT, kT, v128, aT):
    SPAN = WINDOW + CHUNK
    LAST = TOK // CHUNK - 1
    def spec(i):
        if isinstance(i, int) and i < 2:
            return (CHUNK, WINDOW, None, 2) if i == 0 else (2 * CHUNK, WINDOW, 2, None)
        if isinstance(i, int) and i == LAST:
            return SPAN, K_CACHE, VS - 3, VS - 1
        return SPAN, i * CHUNK, i, i + 2

    def in_turn(eng, body):
        body(0, 0)
        body(1, 1)
        with eng.Fori(1, LAST // 2 - 1) as c:
            for u in range(2):
                body(2 * c + u, u)
        for i in range(LAST - 2, LAST + 1):
            body(i, i % 2)

    more = lambda i, ahead: not isinstance(i, int) or i + ahead <= LAST
    with Stage(nc, "attend") as st:
        qs, ks, vs = st.sb("qs", [P, 8, CHUNK]), st.sb("ks", [P, KV_T, SPAN]), st.sb("vs", [P, 2, 2, HKV * HD])
        snk = st.sb("snk", [P, HKV, 2])
        prob = st.sb("prob", [P, HKV, 2, SPAN])
        pT = st.sb("pT", [P, 2, 4, P])
        osb = st.sb("osb", [P, HKV, 2, HD])
        mx, nmx, rd = (st.sb(n, [P, HKV, 2]) for n in ("mx", "nmx", "rd"))
        sm, es = (st.sb(n, [P, 2, HKV, 2]) for n in ("sm", "es"))
        ps = st.ps("scores", [P, HKV, 512])
        pt = st.ps("turned", [P, 2, 4, P])
        po, poT = st.ps("out", [P, HKV, 2, HD]), st.ps("outT", [P, HKV, P])
        names = ("sink_set", "q_staged", "k_staged", "v_staged", "scored", "bias_ready", "exped", "max_step", "den_step", "p_turned", "p_copied_a", "p_copied_b",
                 "pv_summed", "o_normed", "o_turned", "o_copied")
        e = {n: st.sem(n) for n in names}
        passed = st.sem("passed")
        ident = m["const"][:, 0:P]
        aview = aT[:, :, :].rearrange("p (j l) t -> p j l t", l=2)
        with st.block() as block:
            @block.tensor
            def _(pe):
                def scores(i, jp):
                    keys = spec(i)[0]
                    pe.wait_ge(e["q_staged"], PRE + i + 1)
                    pe.wait_ge(e["k_staged"], PRE + i + 1)
                    if not isinstance(i, int) or i:
                        pe.wait_ge(e["exped"], PRE + 2 * i + jp - 1)
                    hold(pe, passed)
                    for b in range(2):
                        for g in range(4):
                            last = pe.matmul(ps[CHUNK * (g % 2):CHUNK * (g % 2) + CHUNK, 2 * jp + b, (g // 2) * SPAN:(g // 2) * SPAN + keys],
                                             qs[HD * b:HD * b + HD, 4 * jp + g, :], ks[HD * b:HD * b + HD, jp, 0:keys], start=True, stop=True,
                                             skip_group_check=True)
                    last.then_inc(e["scored"], 1)

                def mix(i, par, jp):
                    keys, _, v0, v1 = spec(i)
                    pe.wait_ge(e["exped"], PRE + 2 * i + jp + 1)
                    pe.wait_ge(e["p_copied_a"], PRE + 2 * i + jp)
                    pe.wait_ge(e["p_copied_b"], PRE + 2 * i + jp)
                    for x in range(4):
                        p = prob[:, 2 * jp + x // 2, x % 2, :]
                        if v0 is not None:
                            last = pe.transpose(pt[:, 0, x, :], p[:, 0:P], ident)
                        if v1 is not None:
                            last = pe.transpose(pt[0:CHUNK, 1, x, :], p[:, keys - CHUNK:keys], ident)
                    last.then_inc(e["p_turned"], 1)
                    pe.wait_ge(e["v_staged"], PRE + i + 1)
                    pe.wait_ge(e["p_copied_a"], PRE + 2 * i + jp + 1)
                    pe.wait_ge(e["p_copied_b"], PRE + 2 * i + jp + 1)
                    pe.wait_ge(e["o_normed"], PRE + 2 * i + jp)
                    for x in range(4):
                        j = 2 * jp + x // 2
                        pieces = [(pT[:, 0, x, :], vs[:, par, 0, j * HD:(j + 1) * HD])] if v0 is not None else []
                        if v1 is not None:
                            pieces.append((pT[0:CHUNK, 1, x, :], vs[0:CHUNK, par, 1, j * HD:(j + 1) * HD]))
                        for n, (l, r) in enumerate(pieces):
                            last = pe.matmul(po[:, j, x % 2, :], l, r, start=(n == 0), stop=(n == len(pieces) - 1))
                    last.then_inc(e["pv_summed"], 1)

                def body(i, par):
                    for jp in range(2):
                        if more(i, 1):
                            scores(i + 1, jp)
                        mix(i, par, jp)
                    pe.wait_ge(e["o_normed"], PRE + 2 * i + 2)
                    pe.wait_ge(e["o_copied"], PRE + i)
                    for j in range(HKV):
                        last = pe.transpose(poT[:, j, :], osb[:, j, :, :].rearrange("p a c -> p (a c)"), ident)
                    last.then_inc(e["o_turned"], 1)

                scores(0, 0)
                scores(0, 1)
                in_turn(pe, body)

            @block.gpsimd
            def _(pool):
                def stage_k(i):
                    keys, k0 = spec(i)[0:2]
                    if not isinstance(i, int) or i:
                        pool.wait_ge(e["scored"], PRE + 2 * i)
                    pool.tensor_copy(ks[:, :, 0:keys], kT[:, :, bass.ds(k0, keys)]).then_inc(e["k_staged"], 1)

                def stage_v(i, par):
                    _, _, v0, v1 = spec(i)
                    if not isinstance(i, int) or i >= 2:
                        pool.wait_ge(e["pv_summed"], PRE + 2 * (i - 1))
                    if v0 is not None:
                        last = pool.tensor_copy(vs[:, par, 0, :], v128[:, bass.ds(v0, 1), :].rearrange("p o c -> p (o c)"))
                    if v1 is not None:
                        last = pool.tensor_copy(vs[0:CHUNK, par, 1, :], v128[0:CHUNK, bass.ds(v1, 1), :].rearrange("p o c -> p (o c)"))
                    last.then_inc(e["v_staged"], 1)

                def body(i, par):
                    if more(i, 2):
                        stage_k(i + 2)
                    if more(i, 1):
                        stage_v(i + 1, 1 - par)

                stage_k(0)
                stage_v(0, 0)
                stage_k(1)
                in_turn(pool, body)

            @block.scalar
            def _(act):
                def stage_q(i):
                    if not isinstance(i, int) or i:
                        act.wait_ge(e["scored"], PRE + 2 * i)
                    act.activation(qs[:, :, :], qT[:, :, bass.ds(i * CHUNK, CHUNK)], ACT.Copy, scale=HD ** -0.5).then_inc(e["q_staged"], 1)

                def exps(i, par, jp):
                    keys = spec(i)[0]
                    act.wait_ge(e["bias_ready"], PRE + 2 * i + jp + 1)
                    if not isinstance(i, int) or i:
                        act.wait_ge(e["p_turned"], PRE + 2 * i + jp - 1)
                    act.activation(es[:, par, 2 * jp:2 * jp + 2, :], es[:, par, 2 * jp:2 * jp + 2, :], ACT.Exp)
                    for x in range(4):
                        j = 2 * jp + x // 2
                        last = act.activation(prob[:, j, x % 2, 0:keys], ps[:, j, (x % 2) * SPAN:(x % 2) * SPAN + keys], ACT.Exp,
                                              bias=nmx[:, j, x % 2:x % 2 + 1], accum_out=sm[:, par, j, x % 2:x % 2 + 1])
                    last.then_inc(e["exped"], 1)

                def body(i, par):
                    for jp in range(2):
                        act.wait_ge(e["p_turned"], PRE + 2 * i + jp + 1)
                        if spec(i)[2] is not None:
                            act.activation(pT[:, 0, :, :], pt[:, 0, :, :], ACT.Copy).then_inc(e["p_copied_a"], 1)
                        else:
                            act.sem_inc(e["p_copied_a"], 1)
                        if more(i, 1):
                            exps(i + 1, 1 - par, jp)
                    if more(i, 2):
                        stage_q(i + 2)
                    act.wait_ge(e["o_turned"], PRE + i + 1)
                    act.activation(aview[:, :, :, bass.ds(i * CHUNK, CHUNK)], poT[:, :, :].rearrange("p j (l q) -> p j l q", l=2), ACT.Copy).then_inc(e["o_copied"], 1)

                stage_q(0)
                exps(0, 0, 0)
                exps(0, 0, 1)
                stage_q(1)
                in_turn(act, body)

            @block.vector
            def _(dve):
                sv = m["swa_sinks"][:, :].rearrange("p (j g l) -> p j g l", g=2, l=2)
                dve.tensor_copy(snk[0:64, :, :], sv[0:64, :, :, 0])
                dve.tensor_copy(snk[64:128, :, :], sv[64:128, :, :, 1]).then_inc(e["sink_set"], 1)
                dve.wait_ge(e["sink_set"], PRE + 1)

                def maxima(i, par, jp):
                    keys, h = spec(i)[0], slice(2 * jp, 2 * jp + 2)
                    step = Chain(dve, e["max_step"], 4 * i + 2 * jp)
                    dve.wait_ge(e["scored"], PRE + 2 * i + jp + 1)
                    sc = ps[:, h, 0:2 * SPAN].rearrange("p j (g c) -> p j g c", g=2)[:, :, :, 0:keys]
                    step(dve.tensor_reduce(mx[:, h, :], sc, AX.X, ALU.max))
                    step(dve.tensor_tensor(mx[:, h, :], mx[:, h, :], snk[:, h, :], ALU.max))
                    dve.tensor_tensor(es[:, par, h, :], snk[:, h, :], mx[:, h, :], ALU.subtract)
                    dve.tensor_scalar(nmx[:, h, :], mx[:, h, :], -1.0, None, ALU.mult).then_inc(e["bias_ready"], 1)

                def body(i, par):
                    for jp in range(2):
                        h = slice(2 * jp, 2 * jp + 2)
                        if more(i, 1):
                            maxima(i + 1, 1 - par, jp)
                        step = Chain(dve, e["den_step"], 4 * i + 2 * jp)
                        if spec(i)[3] is not None:
                            dve.wait_ge(e["p_turned"], PRE + 2 * i + jp + 1)
                            dve.tensor_copy(pT[0:CHUNK, 1, :, :], pt[0:CHUNK, 1, :, :]).then_inc(e["p_copied_b"], 1)
                        else:
                            dve.sem_inc(e["p_copied_b"], 1)
                        dve.wait_ge(e["exped"], PRE + 2 * i + jp + 1)
                        step(dve.tensor_tensor(rd[:, h, :], sm[:, par, h, :], es[:, par, h, :], ALU.add))
                        step(dve.reciprocal(rd[:, h, :], rd[:, h, :]))
                        dve.wait_ge(e["pv_summed"], PRE + 2 * i + jp + 1)
                        dve.tensor_tensor(osb[:, h, :, :], po[:, h, :, :], rd[:, h, :].unsqueeze(3).broadcast_to([P, 2, 2, HD]), ALU.mult).then_inc(e["o_normed"], 1)

                maxima(0, 0, 0)
                maxima(0, 0, 1)
                in_turn(dve, body)


TOP_K = 2
CAP = 320
OVER_MAX = TOP_K * TOK // CAP
JOBS = NE + OVER_MAX
MORE = (TOK - 1) // CAP
SLOTS = JOBS * CAP
TABLE = -(-(JOBS + 1) * CAP // P) * P
CAP_T = [(s, min(P, CAP - s)) for s in range(0, CAP, P)]


def route_stage(nc, m, hT, io, r):
    ramp, pidx = m["const"][:, N_CONST * P:N_CONST * P + NE], m["const"][:, N_CONST * P + NE:N_CONST * P + NE + 1]
    with Stage(nc, "route") as st:
        wr = st.sb("wr", [P, KD, NE])
        hrow = st.sb("hrow", [P, 2, D])
        lg, one, two, tmp, tmp2, offs, rank = (st.sb(n, [P, NT, NE]) for n in ("lg", "one", "two", "tmp", "tmp2", "offs", "rank"))
        m1, m2, rt, e21 = (st.sb(n, [P, NT]) for n in ("m1", "m2", "rt", "e21"))
        total, over, ends, coef, first, t8 = (st.sb(n, [P, NE]) for n in ("total", "over", "ends", "coef", "first", "t8"))
        slotf = st.sb("slotf", [P, TOP_K, NT])
        jobsf = st.sb("jobsf", [P, 16])
        ids = st.sb("ids", [P, NT], I32)
        zero = st.sb("zero", [P, TABLE // P], I32)
        pl, prank, ptot = (st.ps(n, [P, NT, NE]) for n in ("logits", "rank_in_tile", "tile_total"))
        ph = st.ps("ph", [P, 4, 4, P])
        w_loaded, proj, vs, es, counted, ranked = (st.sem(n) for n in ("w_loaded", "projected", "vector_step", "exped", "counted", "ranked"))
        turned, h_copied = st.sem("turned"), st.sem("h_copied")
        h_stored = [st.sem(f"h_stored{u}") for u in range(2)]
        ids_set, slots_ready, x_stored = st.sem("ids_set"), st.sem("slots_ready"), st.sem("x_stored")
        zeroed, scattered = st.sem("zeroed", pre=False), st.sem("scattered", pre=False)
        zero_set = st.sem("zero_set")
        over_tiles = lambda a: a.unsqueeze(1).broadcast_to([P, NT, NE])
        over_experts = lambda a: a.unsqueeze(2).broadcast_to([P, NT, NE])
        with st.block() as block:
            @block.sync
            def _(sp):
                sp.dma_start(wr[:, :, :], io["moe_router"][0].rearrange("(k p) e -> p k e", p=P)).then_inc(w_loaded, 16)
                sp.dma_start(m["x_dram"].rearrange("k p t -> p k t"), m["xT"][:, :, :]).then_inc(x_stored, 16)
                for t, (s, n) in enumerate(TILES):
                    sp.wait_ge(h_copied, PRE + 2 * t + 2)
                    sp.dma_start(m["h_dram"][s:s + n, :], hrow[0:n, t % 2, :]).then_inc(h_stored[t % 2], 16)
                sp.wait_ge(h_stored[0], PRE + 16 * ((NT + 1) // 2))
                sp.wait_ge(h_stored[1], PRE + 16 * (NT // 2))
                sp.wait_ge(x_stored, PRE + 16)

            @block.gpsimd
            def _(pool):
                pool.memset(zero[:, :], 0).then_inc(zero_set, 1)
                pool.wait_ge(zero_set, PRE + 1)
                pool.dma_start(m["slot_tok"].rearrange("(p c) o -> p (c o)", p=P), zero[:, :]).then_inc(zeroed, 16)
                pool.wait_ge(zeroed, 16)
                pool.wait_ge(ids_set, PRE + NT)
                pool.wait_ge(slots_ready, PRE + 1)
                for a in range(TOP_K):
                    for t, (s, n) in enumerate(TILES):
                        pool.indirect_dma_start(out=m["slot_tok"], out_offset=bass.IndirectOffsetOnAxis(ap=r["slot"][0:n, a, t:t + 1], axis=0),
                                                in_=ids[0:n, t:t + 1], in_offset=None).then_inc(scattered, 16)
                pool.wait_ge(scattered, 16 * TOP_K * NT)

            @block.tensor
            def _(pe):
                pe.wait_ge(w_loaded, PRE + 16)
                for t, (s, n) in enumerate(TILES):
                    for k in range(KD):
                        last = pe.matmul(pl[0:n, t, :], hT[:, k, s:s + n], wr[:, k, :], start=(k == 0), stop=(k == KD - 1))
                last.then_inc(proj, 1)
                for t, (s, n) in enumerate(TILES):
                    for h in range(2):
                        i = 2 * t + h
                        if i >= 4:
                            pe.wait_ge(h_copied, PRE + i - 3)
                        for k in range(4):
                            last = pe.transpose(ph[0:n, i % 4, k, :], hT[:, 4 * h + k, s:s + n], m["const"][:, 0:P])
                        last.then_inc(turned, 1)
                pe.wait_ge(counted, PRE + 1)
                pe.matmul(prank[:, :, :], m["const"][:, C_STRICT * P:(C_STRICT + 1) * P], tmp[:, :, :], start=True, stop=True)
                pe.matmul(ptot[:, :, :], m["const"][:, C_ONES * P:(C_ONES + 1) * P], tmp[:, :, :], start=True, stop=True).then_inc(ranked, 1)

            @block.scalar
            def _(act):
                for i in range(2 * NT):
                    t, h = i // 2, i % 2
                    n = TILES[t][1]
                    if t >= 2:
                        act.wait_ge(h_stored[t % 2], PRE + 16 * (t // 2))
                    act.wait_ge(turned, PRE + i + 1)
                    act.activation(hrow[0:n, t % 2, h * 512:h * 512 + 512].rearrange("p (k c) -> p k c", c=P), ph[0:n, i % 4, :, :], ACT.Copy).then_inc(h_copied, 1)
                act.wait_ge(vs, PRE + 14)
                act.activation(e21[:, :], m2[:, :], ACT.Exp).then_inc(es, 1)

            @block.vector
            def _(dve):
                v = Chain(dve, vs)
                for t in range(NT):
                    dve.tensor_scalar(ids[:, t:t + 1], pidx, float(t * P), None, ALU.add).then_inc(ids_set, 1)
                v(dve.memset(lg[:, :, :], 0.0))
                dve.wait_ge(proj, PRE + 1)
                dve.tensor_copy(lg[:, 0:NT - 1, :], pl[:, 0:NT - 1, :])
                v(dve.tensor_copy(lg[0:64, NT - 1, :], pl[0:64, NT - 1, :]))

                def best(top, onehot):
                    v(dve.tensor_reduce(top[:, :], lg[:, :, :], AX.X, ALU.max))
                    v(dve.tensor_tensor(tmp[:, :, :], lg[:, :, :], over_experts(top[:, :]), ALU.is_equal))
                    v(dve.tensor_tensor(tmp[:, :, :], tmp[:, :, :], over_tiles(ramp), ALU.mult))
                    v(dve.tensor_reduce(rt[:, :], tmp[:, :, :], AX.X, ALU.max))
                    return dve.tensor_tensor(onehot[:, :, :], over_tiles(ramp), over_experts(rt[:, :]), ALU.is_equal)

                v(best(m1, one))
                v(dve.scalar_tensor_tensor(out=lg[:, :, :], in0=one[:, :, :], scalar=-3.0e38, in1=lg[:, :, :], op0=ALU.mult, op1=ALU.add))
                last = best(m2, two)
                v(last)
                v(dve.tensor_tensor(m2[:, :], m2[:, :], m1[:, :], ALU.subtract))
                dve.memset(one[64:128, NT - 1, :], 0.0)
                v(dve.memset(two[64:128, NT - 1, :], 0.0))
                v(dve.tensor_tensor(tmp[:, :, :], one[:, :, :], two[:, :, :], ALU.add))
                dve.sem_inc(counted, 1)
                dve.wait_ge(es, PRE + 1)
                v(dve.tensor_scalar(m1[:, :], e21[:, :], 1.0, None, ALU.add))
                v(dve.reciprocal(r["gate"][:, 0, :], m1[:, :]))
                dve.tensor_tensor(r["gate"][:, 1, :], r["gate"][:, 0, :], e21[:, :], ALU.mult)
                dve.wait_ge(ranked, PRE + 1)
                v(dve.memset(offs[:, 0, :], 0.0))
                for t in range(1, NT):
                    v(dve.tensor_tensor(offs[:, t, :], offs[:, t - 1, :], ptot[:, t - 1, :], ALU.add))
                v(dve.tensor_tensor(total[:, :], offs[:, NT - 1, :], ptot[:, NT - 1, :], ALU.add))
                v(dve.tensor_tensor(rank[:, :, :], offs[:, :, :], prank[:, :, :], ALU.add))
                v(dve.tensor_scalar(over[:, :], total[:, :], float(CAP), None, ALU.is_gt))
                for k in range(2, MORE + 1):
                    v(dve.scalar_tensor_tensor(out=over[:, :], in0=total[:, :], scalar=float(k * CAP), in1=over[:, :], op0=ALU.is_gt, op1=ALU.add))
                v(dve.tensor_copy(ends[:, 0:1], over[:, 0:1]))
                for x in range(1, NE):
                    v(dve.tensor_tensor(ends[:, x:x + 1], ends[:, x - 1:x], over[:, x:x + 1], ALU.add))
                v(dve.tensor_tensor(coef[:, :], ends[:, :], over[:, :], ALU.subtract))
                v(dve.scalar_tensor_tensor(out=coef[:, :], in0=coef[:, :], scalar=-1.0, in1=ramp, op0=ALU.add, op1=ALU.add))
                dve.tensor_scalar(first[:, :], ramp, -float(CAP), float(NE * CAP), ALU.mult, ALU.add)
                v(dve.tensor_scalar(coef[:, :], coef[:, :], float(CAP), None, ALU.mult))
                v(dve.tensor_scalar(tmp2[:, :, :], rank[:, :, :], float(CAP), None, ALU.is_ge))
                v(dve.tensor_tensor(tmp2[:, :, :], tmp2[:, :, :], over_tiles(coef[:, :]), ALU.mult))
                v(dve.tensor_tensor(tmp2[:, :, :], tmp2[:, :, :], rank[:, :, :], ALU.add))
                v(dve.tensor_tensor(tmp2[:, :, :], tmp2[:, :, :], over_tiles(first[:, :]), ALU.add))
                v(dve.tensor_tensor(one[:, :, :], one[:, :, :], tmp2[:, :, :], ALU.mult))
                v(dve.tensor_tensor(two[:, :, :], two[:, :, :], tmp2[:, :, :], ALU.mult))
                v(dve.tensor_reduce(slotf[:, 0, :], one[:, :, :], AX.X, ALU.add))
                v(dve.tensor_reduce(slotf[:, 1, :], two[:, :, :], AX.X, ALU.add))
                dve.tensor_copy(r["slot"][:, :, :], slotf[:, :, :]).then_inc(slots_ready, 1)
                v(dve.tensor_scalar(jobsf[:, 0:1], ends[:, NE - 1:NE], float(NE), None, ALU.add))
                for i in range(OVER_MAX):
                    v(dve.tensor_scalar(t8[:, 0:NE], ends[:, :], float(i), None, ALU.is_le))
                    v(dve.tensor_reduce(jobsf[:, NE + i:NE + i + 1], t8[:, 0:NE - 1], AX.X, ALU.add))
                dve.memset(jobsf[:, 1:NE], 0.0)
                v(dve.memset(jobsf[:, JOBS:16], 0.0))
                dve.tensor_copy(r["jobs"][:, :], jobsf[:, :])


def expert_stage(nc, m, io, r):
    w1, w3, w2 = io["moe_w1"][0], io["moe_w3"][0], io["moe_w2"][0]
    NF, ND, KH = KF // 2, KD // 2, KF // 2
    PIECES = KF + KD
    YFILLS = 2 * len(CAP_T)
    with Stage(nc, "experts") as st:
        ids = st.sb("ids", [P, len(CAP_T)], I32)
        rows = st.sb("rows", [P, len(CAP_T), D])
        hx, yT = st.sb("hx", [P, 2, KD, CAP]), st.sb("yT", [P, KD, CAP])
        raw = st.sb("raw", [P, 2, KH, P])
        w13 = st.sb("w13", [P, 2, 2, 2, KD, P])
        hid = st.sb("hid", [P, 2, KF, CAP])
        wd = st.sb("wd", [P, 2, 2, KH, P])
        sg, hf = st.sb("sg", [P, 2, CAP]), st.sb("hf", [P, 2, CAP])
        yrow = st.sb("yrow", [P, len(CAP_T), D])
        pa, pb, pd, pt = (st.ps(n, [P, 2, 512]) for n in ("pa", "pb", "pd", "pt"))
        zero_set, tail_zeroed, passed = st.sem("zero_set"), st.sem("tail_zeroed"), st.sem("passed")
        one = lambda n: st.sem(n)
        two = lambda n: [st.sem(f"{n}{u}") for u in range(2)]
        ids_l, gathered = st.sem("ids_loaded", pre=False), st.sem("gathered", pre=False)
        x_turned, x_rounded, x_split, y_turned, yr_copied, y_left = (one(n) for n in ("x_turned", "x_rounded", "x_split", "y_turned", "yrow_copied", "y_left"))
        y_stored = st.sem("y_stored", pre=False)
        x_bank = lambda k: (pa, pb)[k // 2 % 2][:, k % 2, 0:CAP]
        loaded, rounded, split, wd_used = (two(n) for n in ("loaded", "rounded", "split", "wd_used"))
        a_done, b_done, silued, gated, hid_rounded, hid_ready, y_copied = (two(n) for n in (
            "a_done", "b_done", "silued", "gated", "hid_rounded", "hid_ready", "y_copied"))
        w_used = (a_done, b_done)

        def jobs(eng, job):
            with eng.Fori(0, NE) as j:
                job(j, j)
            n_jobs = eng.value_load(r["jobs"][0:1, 0:1], min_val=NE, max_val=JOBS)
            with eng.Fori(NE, JOBS) as j:
                with eng.If(j < n_jobs):
                    job(j, None)

        def phases(eng, j, split_up, gate, split_down, copy_down, frames):
            split_up(j, 0, 0)
            with eng.Fori(0, NF - 1) as i:
                split_up(j, i, 1)
                gate(j, i, 0)
                split_up(j, i + 1, 0)
                gate(j, i, 1)
            split_up(j, NF - 1, 1)
            gate(j, NF - 1, 0)
            split_down(j, 0, 0)
            gate(j, NF - 1, 1)
            with eng.Fori(0, ND - 1) as i:
                split_down(j, i, 1)
                copy_down(j, i, 0)
                split_down(j, i + 1, 0)
                copy_down(j, i, 1)
            frames(j + 1)
            split_down(j, ND - 1, 1)
            copy_down(j, ND - 1, 0)
            copy_down(j, ND - 1, 1)

        with st.block() as block:
            @block.sync
            def _(sp):
                def job(j, e):
                    if e is None:
                        e = sp.value_load(r["jobs"][0:1, bass.ds(j, 1)], min_val=0, max_val=NE - 1)
                    with sp.Fori(0, KF) as f:
                        for x, w in enumerate((w1, w3)):
                            sp.wait_ge(split[x], PRE + PIECES * j + f)
                            sp.dma_start(raw[:, x, 0:KD, :], w[bass.ds(e, 1), :, bass.ds(f * P, P)].rearrange("o (k p) c -> p (o k) c", p=P)).then_inc(loaded[x], 16)
                    with sp.Fori(0, KD) as k:
                        for x in range(2):
                            sp.wait_ge(split[x], PRE + PIECES * j + KF + k)
                            sp.dma_start(raw[:, x, :, :], w2[bass.ds(e, 1), x * KH * P:(x + 1) * KH * P, bass.ds(k * P, P)].rearrange("o (k p) c -> p (o k) c", p=P)).then_inc(loaded[x], 16)

                jobs(sp, job)

            @block.gpsimd
            def _(pool):
                def gather(j):
                    for i, (s, n) in enumerate(CAP_T):
                        pool.dma_start(ids[0:n, i:i + 1], m["slot_tok"][bass.ds(j * CAP + s, n), :]).then_inc(ids_l, 16)
                    pool.wait_ge(ids_l, 48 * (j + 1))
                    pool.wait_ge(x_turned, PRE + KD * j)
                    hold(pool, passed)
                    for i, (s, n) in enumerate(CAP_T):
                        pool.indirect_dma_start(out=rows[0:n, i, :], out_offset=None, in_=m["h_dram"],
                                                in_offset=bass.IndirectOffsetOnAxis(ap=ids[0:n, i:i + 1].bitcast(U32), axis=0)).then_inc(gathered, 16)
                    pool.wait_ge(gathered, 48 * (j + 1))

                def job(j, e):
                    gather(j + 1)
                    pool.wait_ge(yr_copied, PRE + YFILLS * (j + 1))
                    for i, (s, n) in enumerate(CAP_T):
                        pool.dma_start(m["y_dram"][bass.ds(j * CAP + s, n), :], yrow[0:n, i, :]).then_inc(y_stored, 16)
                    pool.wait_ge(y_stored, 48 * (j + 1))
                    pool.sem_inc(y_left, 1)

                gather(0)
                jobs(pool, job)

            @block.tensor
            def _(pe):
                ident = m["const"][:, 0:P]

                def frames(j):
                    pe.wait_ge(gathered, 48 * (j + 1))
                    for u in range(2):
                        pe.wait_ge(gated[u], PRE + NF * j)
                    hold(pe, passed)
                    for k in range(KD):
                        if k >= 4:
                            pe.wait_ge(x_split, PRE + KD * j + k - 3)
                            hold(pe, passed)
                        for i, (s, n) in enumerate(CAP_T):
                            last = pe.transpose(x_bank(k)[:, s:s + n], rows[0:n, i, k * P:(k + 1) * P], ident[0:n, 0:n])
                        last.then_inc(x_turned, 1)

                def job(j, e):
                    pe.wait_ge(x_split, PRE + KD * (j + 1))
                    hold(pe, passed)
                    with pe.Fori(0, NF) as i:
                        for u in range(2):
                            for x, (bank, freed) in enumerate(((pa, silued), (pb, gated))):
                                pe.wait_ge(split[x], PRE + PIECES * j + 2 * i + u + 1)
                                pe.wait_ge(freed[u], PRE + NF * j + i)
                                for k in range(KD):
                                    last = split_product(pe, bank[:, u, 0:CAP], w13[:, 0, u, x, k, :], w13[:, 1, u, x, k, :], hx[:, 0, k, :], hx[:, 1, k, :],
                                                         k == 0, k == KD - 1)
                                last.then_inc(w_used[x][u], 1)
                    def down(i, u):
                        pe.wait_ge(y_copied[u], PRE + ND * j + i)
                        for k in range(KF):
                            if k % KH == 0:
                                pe.wait_ge(split[k // KH], PRE + PIECES * j + KF + 2 * i + u + 1)
                            if k >= KF - 2:
                                pe.wait_ge(hid_ready[k % 2], PRE + NF * (j + 1))
                            last = split_product(pe, pd[:, u, 0:CAP], wd[:, 0, k // KH, k % KH, :], wd[:, 1, k // KH, k % KH, :], hid[:, 0, k, :], hid[:, 1, k, :],
                                                 k == 0, k == KF - 1)
                            if k % KH == KH - 1:
                                last.then_inc(wd_used[k // KH], 1)

                    with pe.Fori(0, ND - 1) as i:
                        for u in range(2):
                            down(i, u)
                    frames(j + 1)
                    for u in range(2):
                        down(ND - 1, u)
                    for u in range(2):
                        pe.wait_ge(y_copied[u], PRE + ND * (j + 1))
                    fill = 0
                    for i, (s, n) in enumerate(CAP_T):
                        for h in range(2):
                            pe.wait_ge(yr_copied, PRE + YFILLS * j + max(fill - 1, 0))
                            hold(pe, passed)
                            for k in range(4):
                                last = pe.transpose(pt[0:n, fill % 2, k * P:(k + 1) * P], yT[:, 4 * h + k, s:s + n], ident)
                            last.then_inc(y_turned, 1)
                            fill += 1

                frames(0)
                jobs(pe, job)

            @block.scalar
            def _(act):
                def split_up(j, i, u):
                    for x in range(2):
                        act.wait_ge(loaded[x], PRE + 16 * (PIECES * j + 2 * i + u + 1))
                        act.wait_ge(w_used[x][u], PRE + NF * j + i)
                        act.activation(as_r(w13[:, 0, u, x, :, :]), raw[:, x, 0:KD, :], ACT.Copy).then_inc(rounded[x], 1)

                def gate(j, i, u):
                    act.wait_ge(a_done[u], PRE + NF * j + i + 1)
                    act.activation(sg[:, u, :], pa[:, u, 0:CAP], ACT.Silu).then_inc(silued[u], 1)
                    act.wait_ge(gated[u], PRE + NF * j + i + 1)
                    act.activation(as_r(hid[:, 0, bass.ds(2 * i + u, 1), :].rearrange("p o c -> p (o c)")), hf[:, u, :], ACT.Copy).then_inc(hid_rounded[u], 1)

                def split_down(j, i, u):
                    for x in range(2):
                        act.wait_ge(loaded[x], PRE + 16 * (PIECES * j + KF + 2 * i + u + 1))
                        act.wait_ge(wd_used[x], PRE + KD * j + 2 * i + u)
                        act.activation(as_r(wd[:, 0, x, :, :]), raw[:, x, :, :], ACT.Copy).then_inc(rounded[x], 1)

                def copy_down(j, i, u):
                    act.wait_ge(wd_used[1], PRE + KD * j + 2 * i + u + 1)
                    act.activation(yT[:, bass.ds(2 * i + u, 1), :].rearrange("p o c -> p (o c)"), pd[:, u, 0:CAP], ACT.Copy).then_inc(y_copied[u], 1)

                def frames(j):
                    for k in range(KD):
                        act.wait_ge(x_turned, PRE + KD * j + k + 1)
                        act.activation(as_r(hx[:, 0, k, :]), x_bank(k), ACT.Copy).then_inc(x_rounded, 1)

                def job(j, e):
                    phases(act, j, split_up, gate, split_down, copy_down, frames)

                act.wait_ge(zero_set, PRE + 1)
                act.dma_start(m["y_dram"][NE * CAP:, :].rearrange("(a p) c -> p a c", p=P),
                              yrow[:, 0:1, :].broadcast_to([P, OVER_MAX * CAP // P, D])).then_inc(tail_zeroed, 16)
                frames(0)
                jobs(act, job)
                act.wait_ge(tail_zeroed, PRE + 16)

            @block.vector
            def _(dve):
                def split_up(j, i, u):
                    for x in range(2):
                        dve.wait_ge(rounded[x], PRE + PIECES * j + 2 * i + u + 1)
                        dve.tensor_tensor(as_r(w13[:, 1, u, x, :, :]), raw[:, x, 0:KD, :], w13[:, 0, u, x, :, :], ALU.subtract).then_inc(split[x], 1)

                def gate(j, i, u):
                    dve.wait_ge(b_done[u], PRE + NF * j + i + 1)
                    dve.wait_ge(silued[u], PRE + NF * j + i + 1)
                    dve.tensor_tensor(hf[:, u, :], sg[:, u, :], pb[:, u, 0:CAP], ALU.mult).then_inc(gated[u], 1)
                    dve.wait_ge(hid_rounded[u], PRE + NF * j + i + 1)
                    tile = lambda a: hid[:, a, bass.ds(2 * i + u, 1), :].rearrange("p o c -> p (o c)")
                    dve.tensor_tensor(as_r(tile(1)), hf[:, u, :], tile(0), ALU.subtract).then_inc(hid_ready[u], 1)

                def split_down(j, i, u):
                    for x in range(2):
                        dve.wait_ge(rounded[x], PRE + PIECES * j + KF + 2 * i + u + 1)
                        dve.tensor_tensor(as_r(wd[:, 1, x, :, :]), raw[:, x, :, :], wd[:, 0, x, :, :], ALU.subtract).then_inc(split[x], 1)

                def frames(j):
                    for k in range(KD):
                        dve.wait_ge(x_rounded, PRE + KD * j + k + 1)
                        dve.tensor_tensor(as_r(hx[:, 1, k, :]), x_bank(k), hx[:, 0, k, :], ALU.subtract).then_inc(x_split, 1)

                def job(j, e):
                    phases(dve, j, split_up, gate, split_down, lambda j, i, u: None, frames)
                    dve.wait_ge(y_left, PRE + j)
                    dve.wait_ge(tail_zeroed, PRE + 16)
                    fill = 0
                    for i, (s, n) in enumerate(CAP_T):
                        for h in range(2):
                            dve.wait_ge(y_turned, PRE + YFILLS * j + fill + 1)
                            dve.tensor_copy(yrow[0:n, i, h * 512:h * 512 + 512], pt[0:n, fill % 2, :]).then_inc(yr_copied, 1)
                            fill += 1

                dve.memset(yrow[:, 0, :], 0.0).then_inc(zero_set, 1)
                frames(0)
                jobs(dve, job)


def final_stage(nc, m, io, r):
    outs = [io["y_prompt"][0, s:s + n, :] if s < PROMPT else io["y_sample"][0, :, :] for s, n in TILES]
    with Stage(nc, "final") as st:
        y = st.sb("y", [P, 2, TOP_K, D])
        x, sq = st.sb("x", [P, 2, D]), st.sb("sq", [P, D])
        xf = st.sb("xf", [P, 2, KD, P])
        gain = st.sb("gain", [P, D])
        ss, root, rinv = (st.sb(n, [P, NT]) for n in ("ss", "root", "rinv"))
        pt = st.ps("pt", [P, 2, 2, 512])
        g_loaded, turned, mixed, step, squared, rooted, ready = (st.sem(n) for n in ("gain_loaded", "turned", "mixed", "vector_step", "squared", "rooted", "ready"))
        gathered, stored = [st.sem(f"gathered{u}", pre=False) for u in range(2)], [st.sem(f"stored{u}") for u in range(2)]
        x_loaded = [st.sem(f"frames_loaded{u}") for u in range(2)]
        with st.block() as block:
            @block.gpsimd
            def _(pool):
                for t, (s, n) in enumerate(TILES):
                    if t >= 2:
                        pool.wait_ge(mixed, PRE + t - 1)
                    for a in range(TOP_K):
                        pool.indirect_dma_start(out=y[0:n, t % 2, a, :], out_offset=None, in_=m["y_dram"],
                                                in_offset=bass.IndirectOffsetOnAxis(ap=r["slot"][0:n, a, t:t + 1], axis=0)).then_inc(gathered[t % 2], 16)

            @block.sync
            def _(sp):
                def load(t):
                    s, n = TILES[t]
                    sp.dma_start(xf[:, t % 2, :, 0:n], m["x_dram"][:, :, s:s + n].rearrange("k p t -> p k t")).then_inc(x_loaded[t % 2], 16)

                load(0)
                load(1)
                sp.dma_start(gain[:, :], io["final_norm"].unsqueeze(0).broadcast_to([P, D])).then_inc(g_loaded, 16)
                for t, (s, n) in enumerate(TILES):
                    if t + 2 < NT:
                        sp.wait_ge(turned, PRE + t + 1)
                        load(t + 2)
                    sp.wait_ge(ready, PRE + t + 1)
                    sp.dma_start(outs[t], x[0:n, t % 2, :]).then_inc(stored[t % 2], 16)
                sp.wait_ge(stored[0], PRE + 16 * ((NT + 1) // 2))
                sp.wait_ge(stored[1], PRE + 16 * (NT // 2))

            @block.tensor
            def _(pe):
                for t, (s, n) in enumerate(TILES):
                    if t >= 2:
                        pe.wait_ge(mixed, PRE + t - 1)
                    pe.wait_ge(x_loaded[t % 2], PRE + 16 * (t // 2 + 1))
                    for k in range(KD):
                        last = pe.transpose(pt[0:n, t % 2, k // 4, (k % 4) * P:(k % 4 + 1) * P], xf[:, t % 2, k, 0:n], m["const"][:, 0:P])
                    last.then_inc(turned, 1)

            @block.scalar
            def _(act):
                for t, (s, n) in enumerate(TILES):
                    act.wait_ge(mixed, PRE + t + 1)
                    if t:
                        act.wait_ge(rooted, PRE + t)
                    act.activation(sq[0:n, :], x[0:n, t % 2, :], ACT.Square, accum_out=ss[0:n, t:t + 1]).then_inc(squared, 1)
                    act.wait_ge(squared, PRE + t + 1)
                    act.activation(root[0:n, t:t + 1], ss[0:n, t:t + 1], ACT.Sqrt, bias=m["eps"][0:n, :], scale=1.0 / D).then_inc(rooted, 1)

            @block.vector
            def _(dve):
                v = Chain(dve, step)
                dve.wait_ge(g_loaded, PRE + 16)
                for t, (s, n) in enumerate(TILES):
                    dve.wait_ge(turned, PRE + t + 1)
                    dve.wait_ge(gathered[t % 2], 32 * (t // 2 + 1))
                    if t >= 2:
                        dve.wait_ge(stored[t % 2], PRE + 16 * (t // 2))
                    xo = x[0:n, t % 2, :].rearrange("p (h c) -> p h c", h=2)
                    yy = y[0:n, t % 2, :, :].rearrange("p a (h c) -> p a h c", h=2)
                    v(dve.scalar_tensor_tensor(out=xo, in0=yy[:, 0], scalar=r["gate"][0:n, 0, t:t + 1], in1=pt[0:n, t % 2, :, :], op0=ALU.mult, op1=ALU.add))
                    dve.scalar_tensor_tensor(out=xo, in0=yy[:, 1], scalar=r["gate"][0:n, 1, t:t + 1], in1=xo, op0=ALU.mult, op1=ALU.add).then_inc(mixed, 1)
                    dve.wait_ge(rooted, PRE + t + 1)
                    v(dve.reciprocal(rinv[0:n, t:t + 1], root[0:n, t:t + 1]))
                    dve.scalar_tensor_tensor(out=x[0:n, t % 2, :], in0=x[0:n, t % 2, :], scalar=rinv[0:n, t:t + 1], in1=gain[0:n, :], op0=ALU.mult, op1=ALU.mult).then_inc(ready, 1)


def moe_routing(nc, m, io):
    m["h_dram"] = nc.dram_tensor("h_rows", (TOK, D), F32).ap()
    m["x_dram"] = nc.dram_tensor("frames", (KD, P, TOK), F32).ap()
    m["slot_tok"] = nc.dram_tensor("slot_tokens", (TABLE, 1), I32).ap()
    m["y_dram"] = nc.dram_tensor("slot_rows", (SLOTS, D), F32).ap()
    with nc.sbuf_tensor("h_moe", [P, KD, TOK], F32) as hT:
        norm_stage(nc, m, "norm4", hT, G_FFN1)
        route_stage(nc, m, hT, io, m["route"])


def rest_stages(nc, m, io):
    sbt = nc.sbuf_tensor
    m["hid_dram"] = nc.dram_tensor("hidden", (KF, P, TOK), F32).ap()
    with sbt("h_ffn", [P, 2, KD, TOK], F32) as hT:
        norm_stage(nc, m, "norm1", hT, G_FFN0, halves=True)
        ffn_up_stage(nc, m, hT, io["ffn_w1"][0], io["ffn_w3"][0])
    w2 = io["ffn_w2"][0]
    add_product_stage(nc, m, "ffndown", m["hid_dram"], KF, lambda to, t, p: [(to, w2[p * D_FF // 2:(p + 1) * D_FF // 2, bass.ds(t * P, P)].rearrange("(k p) c -> p k c", p=P))])
    with sbt("kT", [P, KV_T, KEYS], F32) as kT, sbt("v128", [P, VS, HKV * HD], F32) as v128, sbt("h_att", [P, KD, TOK], F32) as hT, \
            sbt("rinv_att", [P, TOK], F32) as rinv:
        norm_stage(nc, m, "norm2", hT, G_KV, rinv=rinv)
        with sbt("vTt", [P, KV_T, TOK], F32) as vT:
            heads_stage(nc, m, "kv", hT, 2 * KV_T, KV_T,
                        lambda t: [(kT[:, t, WINDOW:K_CACHE], 0), (kT[:, t, K_SAMPLE:KEYS], PROMPT)] if t < KV_T else [(vT[:, t - KV_T, :], 0)],
                        lambda w: [[(w[:, 0, :, :], io["w_kv"].rearrange("(k p) c -> p k c", p=P))]], io)
            values_stage(nc, m, kT, vT, v128, io)
        norm_stage(nc, m, "norm3", hT, G_ATTN1, rinv=rinv, known=True)
        with sbt("qT", [P, 8, TOK], F32) as qT:
            wq = io["swa_w_q"][0].rearrange("(k p) (jp b c) -> jp b p k c", p=P, jp=2, b=2)

            def q_loads(w):
                return [[(w[:, jp, k, :].rearrange("p (g b c) -> p g b c", b=2, c=HD)[:, :, b, :], wq[jp, b, :, k, :].rearrange("p (g c) -> p g c", c=HD))
                         for b in range(2) for k in range(KD)] for jp in range(2)]

            heads_stage(nc, m, "q", hT, 8, 8, lambda t: [(qT[:, t, :], 0)], q_loads, io)
            attend_stage(nc, m, qT, kT, v128, hT)
        wo = io["swa_w_o"][0].rearrange("(j g l d) c -> g d j l c", j=HKV, g=2, l=2)

        def o_load(to, t, p):
            tv = to.rearrange("p (j l) c -> p j l c", l=2)
            return [(tv[HD * g:HD * g + HD, :, l, :], wo[g, :, HKV // 2 * p:HKV // 2 * (p + 1), l, bass.ds(t * P, P)]) for g in range(2) for l in range(2)]

        add_product_stage(nc, m, "attout", hT, KD, o_load, parts=4, resident=True)
    moe_routing(nc, m, io)


INPUTS = ["x_prompt", "x_sample", "cache_conv", "state_delta", "cache_k", "cache_v", "norm_attn", "norm_ffn", "gdn_w_in", "gdn_w_conv",
          "gdn_a_log", "gdn_dt_bias", "gdn_o_norm", "gdn_w_out", "kv_norm", "w_kv", "swa_w_q", "swa_sinks", "swa_w_o",
          "ffn_w1", "ffn_w3", "ffn_w2", "moe_router", "moe_w1", "moe_w3", "moe_w2", "final_norm"]
OUTPUTS = [("y_prompt", (1, PROMPT, D)), ("y_sample", (1, SAMPLE, D)), ("conv_p", (1, 1, HIST, CONV_CH)), ("delta_p", (1, 1, HV, DK, DV)),
           ("k_p", (1, WINDOW, HKV, HD)), ("v_p", (1, WINDOW, HKV, HD)), ("conv_s", (1, 1, HIST, CONV_CH)), ("delta_s", (1, 1, HV, DK, DV)),
           ("k_s", (1, SAMPLE, HKV, HD)), ("v_s", (1, SAMPLE, HKV, HD))]


def build(nc, io):
    with ExitStack() as keep:
        sb = lambda name, shape, dt=F32: keep.enter_context(nc.sbuf_tensor(name, shape, dt))
        m = {"const": sb("const", [P, CONST_W]), "gains": sb("gains", [P, N_GAINS]), "convw": sb("convw", [P, CONV_W, 32]),
             "hist": sb("hist", [P, HIST, 32]), "tail": sb("tail", [P, 2, HIST, 32]), "eps": sb("eps", [P, 1]),
             "gdn_a_log": sb("a_log", [P, HV]), "gdn_dt_bias": sb("dt_bias", [P, HV]), "swa_sinks": sb("sinks", [P, HQ]),
             "route": {"gate": sb("gate", [P, TOP_K, NT]), "slot": sb("slot", [P, TOP_K, NT], U32), "jobs": sb("jobs", [P, 16], I32)}}
        m["rows_dram"] = nc.dram_tensor("decay_rows", (2, HV, TOK), F32).ap()
        m["proj_dram"] = nc.dram_tensor("projected", (CONV_CH // P + HV, P, TOK), F32).ap()
        m["o_dram"] = nc.dram_tensor("head_outputs", (HV, P, TOK), F32).ap()
        with nc.sbuf_tensor("xT", [P, KD, TOK], F32) as xT:
            m["xT"] = xT
            load_stage(nc, m, io)
            with nc.sbuf_tensor("cols", [P, NT, HV, N_COL], F32) as cols:
                m["cols"] = cols
                with nc.sbuf_tensor("hT", [P, 2, KD, TOK], F32) as hT:
                    norm_stage(nc, m, "norm0", hT, G_ATTN0, halves=True)
                    gates_stage(nc, m, hT, io)
                    project_stage(nc, m, hT, io)
                with nc.Fori(0, GROUPS // CHAINS) as pas:
                    delta_stage(nc, m, io, pas)
            m["og_dram"] = nc.dram_tensor("gated_outputs", (HV, P, TOK), F32).ap()
            mix_stage(nc, m)
            w_out = io["gdn_w_out"][0]
            add_product_stage(nc, m, "mixout", m["og_dram"], HV, lambda to, t, p: [(to, w_out[p * V_DIM // 2:(p + 1) * V_DIM // 2, bass.ds(t * P, P)].rearrange("(k p) c -> p k c", p=P))])
            tails_stage(nc, m, io)
            rest_stages(nc, m, io)
        expert_stage(nc, m, io, m["route"])
        final_stage(nc, m, io, m["route"])


def kernel(**inputs):
    from concourse import bacc
    from concourse.bass_utils import run_bass_kernel_spmd

    nc = bacc.Bacc("TRN2", target_bir_lowering=False, num_devices=1)
    arrays = {f"in_{n}": np.ascontiguousarray(inputs[n]) for n in INPUTS}
    arrays["in_consts"], arrays["in_rope"] = constants(), rope_tables()
    io = {n[3:]: nc.dram_tensor(n, a.shape, mybir.dt.from_np(a.dtype), kind="ExternalInput").ap() for n, a in arrays.items()}
    for n, shape in OUTPUTS:
        io[n] = nc.dram_tensor(f"out_{n}", shape, F32, kind="ExternalOutput").ap()
    build(nc, io)
    r = run_bass_kernel_spmd(nc, [arrays], core_ids=[0])
    return tuple(r.results[0][f"out_{n}"] for n, _ in OUTPUTS)
```
